# Optimizing a Trainium2 kernel written in Bass

```python
import jax, jax.numpy as jnp
from jax import lax
import numpy as np

D_MODEL = 1024
BATCH = 1
SEQ = 1024
DEPTH = 1

BRANCH_WIDTH = D_MODEL // 4
N_BRANCHES = 3
SB_HEADS = 4
SB_HEAD_DIM = BRANCH_WIDTH // SB_HEADS
SB_BLOCK = 128
HGRN_HEADS = 4
HGRN_HEAD_DIM = BRANCH_WIDTH // HGRN_HEADS
HGRN_EXP_CLIP = 60.0
GLA_HEADS = 4
GLA_VALUE_DIM = BRANCH_WIDTH // GLA_HEADS
GLA_KEY_DIM = GLA_VALUE_DIM // 2
GLA_KEY_WIDTH = GLA_HEADS * GLA_KEY_DIM
GLA_GATE_RANK = 16
GLA_TAU = 16.0
CHUNK = 64
NORM_EPS = 1e-5
DEEPNORM_ALPHA = (2 * DEPTH) ** 0.25
DEEPNORM_BETA = (8 * DEPTH) ** -0.25

IN_WIDTHS = (
    BRANCH_WIDTH, BRANCH_WIDTH, BRANCH_WIDTH, BRANCH_WIDTH,
    BRANCH_WIDTH, BRANCH_WIDTH, BRANCH_WIDTH, BRANCH_WIDTH,
    GLA_KEY_WIDTH, GLA_KEY_WIDTH, BRANCH_WIDTH, BRANCH_WIDTH,
    GLA_GATE_RANK,
    D_MODEL, D_MODEL, D_MODEL,
)
IN_SPLITS = tuple(int(s) for s in np.cumsum(IN_WIDTHS)[:-1])
IN_TOTAL = int(sum(IN_WIDTHS))


def split_heads(a, n_heads):
    b, t, w = a.shape
    return a.reshape(b, t, n_heads, w // n_heads).transpose(0, 2, 1, 3)

def merge_heads(a):
    b, h, t, d = a.shape
    return a.transpose(0, 2, 1, 3).reshape(b, t, h * d)

def masked_exp(mask, log_val):
    return jnp.where(mask, jnp.exp(jnp.where(mask, log_val, 0.0)), 0.0)

def head_rmsnorm(o, gain):
    o = o * lax.rsqrt(jnp.mean(o * o, axis=-1, keepdims=True) + NORM_EPS)
    return merge_heads(o) * gain.astype(jnp.float32)

def layer_norm(x, g, b):
    xf = x.astype(jnp.float32)
    mu = jnp.mean(xf, axis=-1, keepdims=True)
    var = jnp.mean(jnp.square(xf - mu), axis=-1, keepdims=True)
    y = (xf - mu) * lax.rsqrt(var + NORM_EPS) * g.astype(jnp.float32) + b.astype(jnp.float32)
    return y.astype(x.dtype)

def stick_breaking_attention(q, k, v):
    t_len, d = q.shape[2], q.shape[3]
    scale = d ** -0.5
    outs = []
    for blk in range(t_len // SB_BLOCK):
        t0 = blk * SB_BLOCK
        t1 = t0 + SB_BLOCK
        qb, kb, vb = q[:, :, t0:t1], k[:, :, :t1], v[:, :, :t1]
        z = jnp.einsum('bhtd,bhsd->bhts', qb, kb).astype(jnp.float32) * scale
        t_idx = t0 + jnp.arange(SB_BLOCK)[:, None]
        s_idx = jnp.arange(t1)[None, :]
        causal = s_idx < t_idx
        log_beta = jax.nn.log_sigmoid(z)
        log_one_minus = jnp.where(causal, jax.nn.log_sigmoid(-z), 0.0)
        tail = lax.cumsum(log_one_minus, axis=3, reverse=True) - log_one_minus
        weights = masked_exp(causal, log_beta + tail)
        outs.append(jnp.einsum('bhts,bhsd->bhtd', weights, vb.astype(jnp.float32)))
    return jnp.concatenate(outs, axis=2)

def chunked_gated_linear_recurrence(q, k, v, log_f):
    b, h, t_len, dk = q.shape
    dv = v.shape[-1]
    n_chunks = t_len // CHUNK

    def to_chunks(a):
        a = a.astype(jnp.float32)
        return a.reshape(b, h, n_chunks, CHUNK, a.shape[-1]).transpose(2, 0, 1, 3, 4)

    qc, kc, vc, gc = to_chunks(q), to_chunks(k), to_chunks(v), to_chunks(log_f)
    causal = jnp.tril(jnp.ones((CHUNK, CHUNK), dtype=bool))[:, :, None]

    def step(state, inp):
        qi, ki, vi, gi = inp
        cum = jnp.cumsum(gi, axis=2)
        o_inter = jnp.einsum('bhck,bhkv->bhcv', qi * jnp.exp(cum), state)
        diff = cum[:, :, :, None, :] - cum[:, :, None, :, :]
        decay = masked_exp(causal, diff)
        scores = jnp.einsum('bhtsk,bhsk->bhts', qi[:, :, :, None, :] * decay, ki)
        o = o_inter + jnp.einsum('bhts,bhsv->bhtv', scores, vi)
        last = cum[:, :, -1:, :]
        state = jnp.exp(last[:, :, 0, :])[..., None] * state + jnp.einsum(
            'bhsk,bhsv->bhkv', ki * jnp.exp(last - cum), vi)
        return state, o

    state0 = jnp.zeros((b, h, dk, dv), jnp.float32)
    _, o = lax.scan(step, state0, (qc, kc, vc, gc))
    return o.transpose(1, 2, 0, 3, 4).reshape(b, h, t_len, dv)

def hybrid_layer(x, w_in, gla_gate_w2, gla_gate_b, hgrn_lb, hgrn_norm_g, gla_norm_g,
                 w_up, w_out, ln_g, ln_b):
    proj = jnp.einsum('btd,dc->btc', x, w_in)
    (a_q, a_k, a_v, a_g,
     h_f, h_i, h_q, h_g,
     c_q, c_k, c_v, c_g, c_r,
     gate_logits_a, gate_logits_b, gate_logits_c) = jnp.split(proj, IN_SPLITS, axis=-1)

    a_out = stick_breaking_attention(split_heads(a_q, SB_HEADS), split_heads(a_k, SB_HEADS),
                                     split_heads(a_v, SB_HEADS))
    y_a = merge_heads(a_out) * jax.nn.silu(a_g.astype(jnp.float32))

    lb = hgrn_lb.astype(jnp.float32).reshape(HGRN_HEADS, 1, HGRN_HEAD_DIM)
    zf = split_heads(h_f, HGRN_HEADS).astype(jnp.float32)
    log_f = jax.nn.log_sigmoid(zf) + jnp.log1p(lb * jnp.exp(jnp.minimum(-zf, HGRN_EXP_CLIP)))
    h_key = (1.0 - lb) * jax.nn.sigmoid(-zf)
    h_out = chunked_gated_linear_recurrence(split_heads(h_q, HGRN_HEADS), h_key,
                                            split_heads(h_i, HGRN_HEADS), log_f)
    y_b = head_rmsnorm(h_out, hgrn_norm_g) * jax.nn.silu(h_g.astype(jnp.float32))

    gate_pre = jnp.einsum('btr,rk->btk', c_r, gla_gate_w2) + gla_gate_b
    c_log_f = jax.nn.log_sigmoid(gate_pre.astype(jnp.float32)) / GLA_TAU
    c_out = chunked_gated_linear_recurrence(
        split_heads(c_q, GLA_HEADS).astype(jnp.float32) * (GLA_KEY_DIM ** -0.5),
        split_heads(c_k, GLA_HEADS), split_heads(c_v, GLA_HEADS),
        split_heads(c_log_f, GLA_HEADS))
    y_c = head_rmsnorm(c_out, gla_norm_g) * jax.nn.silu(c_g.astype(jnp.float32))

    branches = jnp.stack([y_a, y_b, y_c], axis=0).astype(x.dtype)
    up = jnp.einsum('nbtw,nwd->nbtd', branches, w_up)
    gates = jax.nn.sigmoid(jnp.stack([gate_logits_a, gate_logits_b, gate_logits_c], axis=0))
    merged = jnp.sum(gates * up, axis=0)
    out = jnp.einsum('btd,de->bte', merged, w_out)

    return layer_norm(DEEPNORM_ALPHA * x + out, ln_g, ln_b)

def first_inputs(seed: int = 0) -> dict:
    key = jax.random.key(seed)
    ks = jax.random.split(key, 11)
    f32 = jnp.float32
    x = jax.random.normal(ks[0], (BATCH, SEQ, D_MODEL), f32)
    w_in = jax.random.normal(ks[1], (DEPTH, D_MODEL, IN_TOTAL), f32) * D_MODEL ** -0.5
    gla_gate_w2 = jax.random.normal(ks[2], (DEPTH, GLA_GATE_RANK, GLA_KEY_WIDTH), f32) * GLA_GATE_RANK ** -0.5
    gla_gate_b = 0.1 * jax.random.normal(ks[3], (DEPTH, GLA_KEY_WIDTH), f32)
    hgrn_lb_logits = 0.5 * jax.random.normal(ks[4], (DEPTH, BRANCH_WIDTH), f32)
    hgrn_norm_g = 1.0 + 0.02 * jax.random.normal(ks[5], (DEPTH, BRANCH_WIDTH), f32)
    gla_norm_g = 1.0 + 0.02 * jax.random.normal(ks[6], (DEPTH, BRANCH_WIDTH), f32)
    w_up = jax.random.normal(ks[7], (DEPTH, N_BRANCHES, BRANCH_WIDTH, D_MODEL), f32) * (
        BRANCH_WIDTH ** -0.5 * DEEPNORM_BETA)
    w_out = jax.random.normal(ks[8], (DEPTH, D_MODEL, D_MODEL), f32) * (D_MODEL ** -0.5 * DEEPNORM_BETA)
    ln_g = 1.0 + 0.02 * jax.random.normal(ks[9], (DEPTH, D_MODEL), f32)
    ln_b = 0.02 * jax.random.normal(ks[10], (DEPTH, D_MODEL), f32)
    return {"x": x, "w_in": w_in, "gla_gate_w2": gla_gate_w2, "gla_gate_b": gla_gate_b,
            "hgrn_lb_logits": hgrn_lb_logits, "hgrn_norm_g": hgrn_norm_g, "gla_norm_g": gla_norm_g,
            "w_up": w_up, "w_out": w_out, "ln_g": ln_g, "ln_b": ln_b}

def first_block(x, w_in, gla_gate_w2, gla_gate_b, hgrn_lb_logits, hgrn_norm_g, gla_norm_g,
              w_up, w_out, ln_g, ln_b):
    lb_soft = jax.nn.softmax(hgrn_lb_logits.astype(jnp.float32), axis=0)
    lower_bounds = jnp.cumsum(lb_soft, axis=0) - lb_soft[0:1]
    for layer in range(DEPTH):
        x = hybrid_layer(x, w_in[layer], gla_gate_w2[layer], gla_gate_b[layer],
                         lower_bounds[layer], hgrn_norm_g[layer], gla_norm_g[layer],
                         w_up[layer], w_out[layer], ln_g[layer], ln_b[layer])
    return x


_first_inputs = first_inputs


def first_inputs(seed=0):
    import zlib

    import numpy as np

    out = dict(_first_inputs(seed))
    spreads = {}
    factors = {'gla_gate_w2': 5.567,
     'gla_gate_b': 8.0,
     'hgrn_norm_g': 8.0,
     'gla_norm_g': 8.0,
     'ln_g': 2.848,
     'ln_b': 2.921}
    for name, (base, spread) in spreads.items():
        noise = np.random.default_rng([zlib.crc32(name.encode()), seed]).standard_normal(out[name].shape)
        drawn = base * np.exp(spread * noise) if base else spread * noise
        out[name] = __import__('jax').numpy.asarray(drawn.astype(out[name].dtype))
    for name, factor in factors.items():
        out[name] = (out[name] * factor).astype(out[name].dtype)
    return out


_narrow_inputs = first_inputs


def first_inputs(seed=0):

    out = dict(_narrow_inputs(seed))
    wider = {'hgrn_norm_g': 5.95, 'gla_norm_g': 5.98, 'ln_g': 3.21, 'ln_b': 3.2}
    for name, times in wider.items():
        mean = out[name].mean()
        out[name] = (mean + times * (out[name] - mean)).astype(out[name].dtype)
    return out


HEAD_DIM = 64
RWKV_HEADS = 16
RWKV_W = RWKV_HEADS * HEAD_DIM
ATT_HEADS = 16
ATT_W = ATT_HEADS * HEAD_DIM
MIX_W = RWKV_W + ATT_W
DECAY_RANK = 64
ICLR_RANK = 64
SHIFT_COLS = 3 * RWKV_W + DECAY_RANK + ICLR_RANK
RWKV_GATE0 = SHIFT_COLS
ATT0 = RWKV_GATE0 + RWKV_W
ATT_GATE0 = ATT0 + 3 * ATT_W
N_IN = ATT_GATE0 + ATT_W
DILATED_PATTERNS = ((128, 1), (512, 4), (2048, 16))
BLK = 128
RMS_EPS = 1e-5
GN_EPS = 64e-5


def rms_norm(x, w):
    xf = x.astype(jnp.float32)
    y = xf * lax.rsqrt(jnp.mean(xf * xf, axis=-1, keepdims=True) + RMS_EPS)
    return y * w.astype(jnp.float32)

def rwkv7_time_mix(p_shift, gate, w0, w_up, a0, a_up, k_k, k_a, r_k, ln_x_w, ln_x_b):
    B, S, _ = p_shift.shape
    r, k, v, w_lo, a_lo = jnp.split(
        p_shift, [RWKV_W, 2 * RWKV_W, 3 * RWKV_W, 3 * RWKV_W + DECAY_RANK], axis=-1)
    w = -jax.nn.softplus(-(w0 + jnp.tanh(w_lo) @ w_up)) - 0.5
    decay = jnp.exp(-jnp.exp(w))
    a = jax.nn.sigmoid(a0 + a_lo @ a_up)
    heads = lambda t: t.reshape(B, S, RWKV_HEADS, HEAD_DIM)
    kk = heads(k * k_k)
    kk = kk / jnp.maximum(jnp.linalg.norm(kk, axis=-1, keepdims=True), 1e-12)
    k = k * (1.0 + (a - 1.0) * k_a)
    r_h, k_h, v_h, w_h, a_h = heads(r), heads(k), heads(v), heads(decay), heads(a)

    def step(state, inp):
        r_t, w_t, k_t, v_t, av_t, bv_t = inp
        sa = jnp.einsum('bhvk,bhk->bhv', state, av_t)
        state = (state * w_t[:, :, None, :] + sa[..., None] * bv_t[:, :, None, :]
                 + v_t[..., None] * k_t[:, :, None, :])
        return state, jnp.einsum('bhvk,bhk->bhv', state, r_t)

    xs = tuple(t.astype(jnp.float32).transpose(1, 0, 2, 3)
               for t in (r_h, w_h, k_h, v_h, -kk, kk * a_h))
    s0 = jnp.zeros((B, RWKV_HEADS, HEAD_DIM, HEAD_DIM), jnp.float32)
    _, y = lax.scan(step, s0, xs)
    y = y.transpose(1, 0, 2, 3)
    mu = jnp.mean(y, axis=-1, keepdims=True)
    var = jnp.mean(jnp.square(y - mu), axis=-1, keepdims=True)
    y = ((y - mu) * lax.rsqrt(var + GN_EPS)).reshape(B, S, RWKV_W) * ln_x_w + ln_x_b
    bonus = jnp.sum(r_h * k_h * r_k, axis=-1, keepdims=True) * v_h
    return (y + bonus.reshape(B, S, RWKV_W)) * jax.nn.silu(gate)

def dilated_window_attention(q, k, v, window, dilation):
    B, S, H, E = q.shape
    L = S // dilation
    steps = window // dilation
    nb = -(-L // BLK)
    Lp = nb * BLK

    def to_sub(t):
        t = t.reshape(B, L, dilation, H, E).transpose(0, 2, 3, 1, 4)
        t = jnp.pad(t, ((0, 0), (0, 0), (0, 0), (0, Lp - L), (0, 0)))
        return t.reshape(B, dilation, H, nb, BLK, E)

    def band(t):
        prev = jnp.pad(t, ((0, 0), (0, 0), (0, 0), (1, 0), (0, 0), (0, 0)))[:, :, :, :-1]
        return jnp.concatenate([prev, t], axis=4)

    qb = to_sub(q)
    kc, vc = band(to_sub(k)), band(to_sub(v))
    s = jnp.einsum('bdhnqe,bdhnke->bdhnqk', qb, kc) * (E ** -0.5)
    qi = jnp.arange(nb)[:, None, None] * BLK + jnp.arange(BLK)[None, :, None]
    ki = (jnp.arange(nb)[:, None, None] - 1) * BLK + jnp.arange(2 * BLK)[None, None, :]
    dist = qi - ki
    valid = (dist >= 0) & (dist <= steps) & (ki >= 0)
    s = jnp.where(valid, s, -jnp.inf)
    m = jnp.max(s, axis=-1, keepdims=True)
    pexp = jnp.exp(s - m)
    l = jnp.sum(pexp, axis=-1, keepdims=True)
    o = jnp.einsum('bdhnqk,bdhnke->bdhnqe', pexp, vc) / l
    lse = (m + jnp.log(l))[..., 0]
    o = o.reshape(B, dilation, H, Lp, E)[:, :, :, :L].transpose(0, 3, 1, 2, 4).reshape(B, S, H, E)
    lse = lse.reshape(B, dilation, H, Lp)[..., :L].transpose(0, 3, 1, 2).reshape(B, S, H)
    return o, lse

def mixed_dilated_attention(p_att, gate):
    B, S, _ = p_att.shape
    q, k, v = (t.reshape(B, S, ATT_HEADS, HEAD_DIM) for t in jnp.split(p_att, 3, axis=-1))
    outs, lses = [], []
    for window, dilation in DILATED_PATTERNS:
        o, lse = dilated_window_attention(q, k, v, window, dilation)
        outs.append(o)
        lses.append(lse)
    wts = jax.nn.softmax(jnp.stack(lses, axis=0), axis=0)
    o = jnp.sum(wts[..., None] * jnp.stack(outs, axis=0), axis=0)
    return o.reshape(B, S, ATT_W) * jax.nn.silu(gate)

def second_inputs(seed: int = 0) -> dict:
    key = jax.random.key(seed)
    ks = jax.random.split(key, 15)
    nrm = lambda k, shape: jax.random.normal(k, shape, jnp.float32)
    return {
        'x': nrm(ks[0], (BATCH, SEQ, D_MODEL)),
        'norm_w': 1.0 + 0.02 * nrm(ks[1], (D_MODEL,)),
        'w_in': nrm(ks[2], (D_MODEL, N_IN)) * D_MODEL ** -0.5,
        'mu_shift': jax.random.uniform(ks[3], (SHIFT_COLS,), jnp.float32),
        'w0': jax.random.uniform(ks[4], (RWKV_W,), jnp.float32, minval=-6.0, maxval=-1.0),
        'w_up': 0.1 * nrm(ks[5], (DECAY_RANK, RWKV_W)),
        'a0': 0.1 * nrm(ks[6], (RWKV_W,)),
        'a_up': 0.1 * nrm(ks[7], (ICLR_RANK, RWKV_W)),
        'k_k': 0.85 + 0.02 * nrm(ks[8], (RWKV_W,)),
        'k_a': 1.0 + 0.02 * nrm(ks[9], (RWKV_W,)),
        'r_k': 0.1 * nrm(ks[10], (RWKV_HEADS, HEAD_DIM)),
        'ln_x_w': 1.0 + 0.02 * nrm(ks[11], (RWKV_W,)),
        'ln_x_b': 0.02 * nrm(ks[12], (RWKV_W,)),
        'w_out': nrm(ks[13], (MIX_W, D_MODEL)) * MIX_W ** -0.5,
        'final_norm_w': 1.0 + 0.02 * nrm(ks[14], (D_MODEL,)),
    }

def second_block(x, norm_w, w_in, mu_shift, w0, w_up, a0, a_up, k_k, k_a, r_k,
              ln_x_w, ln_x_b, w_out, final_norm_w):
    h = x.astype(jnp.float32)
    for _ in range(DEPTH):
        xn = rms_norm(h, norm_w)
        p = jnp.einsum('bsd,dn->bsn', xn, w_in.astype(jnp.float32))
        p_tm = p[..., :SHIFT_COLS]
        prev = jnp.pad(p_tm, ((0, 0), (1, 0), (0, 0)))[:, :-1]
        p_tm = p_tm + (prev - p_tm) * mu_shift
        y_rwkv = rwkv7_time_mix(p_tm, p[..., RWKV_GATE0:ATT0], w0, w_up, a0, a_up,
                                k_k, k_a, r_k, ln_x_w, ln_x_b)
        y_att = mixed_dilated_attention(p[..., ATT0:ATT_GATE0], p[..., ATT_GATE0:])
        mix = jnp.concatenate([y_rwkv, y_att], axis=-1)
        h = h + jnp.einsum('bsm,md->bsd', mix, w_out.astype(jnp.float32))
    return rms_norm(h, final_norm_w).astype(x.dtype)


_first_inputs_2 = second_inputs


def second_inputs(seed=0):
    import zlib

    import numpy as np

    out = dict(_first_inputs_2(seed))
    spreads = {}
    factors = {'norm_w': 3.084,
     'w_up': 3.897,
     'a0': 3.601,
     'k_k': 7.974,
     'k_a': 6.886,
     'ln_x_w': 7.327,
     'ln_x_b': 7.432,
     'final_norm_w': 2.877}
    for name, (base, spread) in spreads.items():
        noise = np.random.default_rng([zlib.crc32(name.encode()), seed]).standard_normal(out[name].shape)
        drawn = base * np.exp(spread * noise) if base else spread * noise
        out[name] = __import__('jax').numpy.asarray(drawn.astype(out[name].dtype))
    for name, factor in factors.items():
        out[name] = (out[name] * factor).astype(out[name].dtype)
    return out


_narrow_inputs_2 = second_inputs


def second_inputs(seed=0):

    out = dict(_narrow_inputs_2(seed))
    wider = {'k_k': 12.0, 'ln_x_w': 12.0, 'ln_x_b': 12.0, 'final_norm_w': 3.23}
    for name, times in wider.items():
        mean = out[name].mean()
        out[name] = (mean + times * (out[name] - mean)).astype(out[name].dtype)
    return out


D_MIX = D_MODEL
D_A = D_MIX // 2
D_B = D_MIX - D_A
N_HEADS_A = 4
HEAD_DIM_A = D_A // N_HEADS_A
CHUNK_3 = 128
N_GROUPS_B = 4
GROUP_DIM_B = D_B // N_GROUPS_B
D_IN = 3 * D_A + 2 * D_B
EPS = 1e-6


def rms_norm_3(x, g):
    xf = x.astype(jnp.float32)
    ms = jnp.mean(xf * xf, axis=-1, keepdims=True)
    return (xf * lax.rsqrt(ms + EPS)).astype(x.dtype) * g

def layer_norm_3(x, g, b):
    xf = x.astype(jnp.float32)
    mu = jnp.mean(xf, axis=-1, keepdims=True)
    var = jnp.mean(jnp.square(xf - mu), axis=-1, keepdims=True)
    return ((xf - mu) * lax.rsqrt(var + EPS)).astype(x.dtype) * g + b

def spatial_gating(u, v, w_s, b_s, ln_g, ln_b):
    bsz, s, _ = u.shape
    v = layer_norm_3(v, ln_g, ln_b)
    vc = v.reshape(bsz, s // CHUNK_3, CHUNK_3, N_HEADS_A, HEAD_DIM_A)
    mixed = jnp.einsum('hpq,bcqhd->bcphd', w_s, vc) + b_s.T[None, None, :, :, None]
    return u * mixed.reshape(bsz, s, D_A)

def fourier_mix(z, w_f, b_f):
    bsz, s, _ = z.shape
    zg = z.reshape(bsz, s, N_GROUPS_B, GROUP_DIM_B).astype(jnp.float32)
    f = jnp.fft.fftn(zg, axes=(1, 3), norm="ortho").real.astype(z.dtype)
    y = jnp.einsum('bsgc,gce->bsge', f, w_f) + b_f
    return y.reshape(bsz, s, D_B)

def third_inputs(seed: int = 0) -> dict:
    key = jax.random.key(seed)
    ks = jax.random.split(key, 16)
    f32 = jnp.float32
    x = jax.random.normal(ks[0], (BATCH, SEQ, D_MODEL), f32)
    pre_g = 1.0 + 0.02 * jax.random.normal(ks[1], (DEPTH, D_MODEL), f32)
    post_g = 1.0 + 0.02 * jax.random.normal(ks[2], (DEPTH, D_MODEL), f32)
    w_in = jax.random.normal(ks[3], (DEPTH, D_MODEL, D_IN), f32) * D_MODEL ** -0.5
    ln_g = 1.0 + 0.02 * jax.random.normal(ks[4], (DEPTH, D_A), f32)
    ln_b = 0.02 * jax.random.normal(ks[5], (DEPTH, D_A), f32)
    w_s = jax.random.normal(ks[6], (DEPTH, N_HEADS_A, CHUNK_3, CHUNK_3), f32) * CHUNK_3 ** -0.5
    b_s = 0.02 * jax.random.normal(ks[7], (DEPTH, N_HEADS_A, CHUNK_3), f32)
    w_f = jax.random.normal(ks[8], (DEPTH, N_GROUPS_B, GROUP_DIM_B, GROUP_DIM_B), f32) * GROUP_DIM_B ** -0.5
    b_f = 0.02 * jax.random.normal(ks[9], (DEPTH, N_GROUPS_B, GROUP_DIM_B), f32)
    w_out = jax.random.normal(ks[10], (DEPTH, D_MIX, D_MODEL), f32) * D_MIX ** -0.5
    return {"x": x, "pre_g": pre_g, "post_g": post_g, "w_in": w_in,
            "ln_g": ln_g, "ln_b": ln_b, "w_s": w_s, "b_s": b_s,
            "w_f": w_f, "b_f": b_f, "w_out": w_out}

def third_block(x, pre_g, post_g, w_in, ln_g, ln_b, w_s, b_s, w_f, b_f, w_out):
    for l in range(DEPTH):
        h = rms_norm_3(x, pre_g[l])
        p = jnp.einsum('bsd,de->bse', h, w_in[l])
        u_a, v_a, g_a, z_b, g_b = jnp.split(
            p, [D_A, 2 * D_A, 3 * D_A, 3 * D_A + D_B], axis=-1)
        a = spatial_gating(jax.nn.gelu(u_a, approximate=False),
                           jax.nn.gelu(v_a, approximate=False),
                           w_s[l], b_s[l], ln_g[l], ln_b[l]) * jax.nn.silu(g_a)
        b = fourier_mix(z_b, w_f[l], b_f[l]) * jax.nn.silu(g_b)
        y = jnp.einsum('bse,ed->bsd', jnp.concatenate([a, b], axis=-1), w_out[l])
        x = x + rms_norm_3(y, post_g[l])
    return x


_first_inputs_3 = third_inputs


def third_inputs(seed=0):
    import zlib

    import numpy as np

    out = dict(_first_inputs_3(seed))
    spreads = {}
    factors = {}
    for name, (base, spread) in spreads.items():
        noise = np.random.default_rng([zlib.crc32(name.encode()), seed]).standard_normal(out[name].shape)
        drawn = base * np.exp(spread * noise) if base else spread * noise
        out[name] = __import__('jax').numpy.asarray(drawn.astype(out[name].dtype))
    for name, factor in factors.items():
        out[name] = (out[name] * factor).astype(out[name].dtype)
    return out


_narrow_inputs_3 = third_inputs


def third_inputs(seed=0):

    out = dict(_narrow_inputs_3(seed))
    wider = {'post_g': 4.42, 'ln_g': 7.21, 'ln_b': 6.11, 'b_s': 6.78, 'b_f': 4.28}
    for name, times in wider.items():
        mean = out[name].mean()
        out[name] = (mean + times * (out[name] - mean)).astype(out[name].dtype)
    return out


def setup_inputs(seed=0):
    out = dict(first_inputs(seed))
    for name, value in second_inputs(seed + 1).items():
        if name != "x":
            out[name + "_2"] = value
    for name, value in third_inputs(seed + 2).items():
        if name != "x":
            out[name + "_3"] = value
    return out


def reference(
    x, w_in, gla_gate_w2, gla_gate_b, hgrn_lb_logits, hgrn_norm_g, gla_norm_g, w_up, w_out,
    ln_g, ln_b, norm_w_2, w_in_2, mu_shift_2, w0_2, w_up_2, a0_2, a_up_2, k_k_2, k_a_2, r_k_2,
    ln_x_w_2, ln_x_b_2, w_out_2, final_norm_w_2, pre_g_3, post_g_3, w_in_3, ln_g_3, ln_b_3,
    w_s_3, b_s_3, w_f_3, b_f_3, w_out_3,
):
    x = first_block(
        x, w_in, gla_gate_w2, gla_gate_b, hgrn_lb_logits, hgrn_norm_g, gla_norm_g, w_up, w_out,
        ln_g, ln_b,
    )
    x = second_block(
        x, norm_w_2, w_in_2, mu_shift_2, w0_2, w_up_2, a0_2, a_up_2, k_k_2, k_a_2, r_k_2,
        ln_x_w_2, ln_x_b_2, w_out_2, final_norm_w_2,
    )
    return third_block(
        x, pre_g_3, post_g_3, w_in_3, ln_g_3, ln_b_3, w_s_3, b_s_3, w_f_3, b_f_3, w_out_3,
    )


_drawn_inputs = setup_inputs


def setup_inputs(seed=0):
    import zlib

    import numpy as np

    out = dict(_drawn_inputs(seed))
    spreads = {}
    factors = {}
    for name, (base, spread) in spreads.items():
        noise = np.random.default_rng([zlib.crc32(name.encode()), seed]).standard_normal(out[name].shape)
        drawn = base * np.exp(spread * noise) if base else spread * noise
        out[name] = __import__('jax').numpy.asarray(drawn.astype(out[name].dtype))
    for name, factor in factors.items():
        out[name] = (out[name] * factor).astype(out[name].dtype)
    return out
```

```python
import numpy as np
from contextlib import ExitStack
import concourse.bass as bass
from concourse import mybir

F32 = mybir.dt.float32
BF16 = mybir.dt.bfloat16
U32 = mybir.dt.uint32
ALU = mybir.AluOpType
ACT = mybir.ActivationFunctionType
AX = mybir.AxisListType


class Queue:

    def __init__(self, eng, sem, name, linked):
        self.eng, self.sem, self.name, self.linked = eng, sem, name, linked
        self.n = 0
        self.seen = {}

    def wait(self, *tokens):
        for t in tokens:
            if t is None:
                continue
            if isinstance(t, list):
                self.wait(*t)
                continue
            sem, name, value = t
            if self.seen.get(name, 0) < value:
                self.seen[name] = value
                self.eng.wait_ge(sem, value)

    def last(self):
        return (self.sem, self.name, self.n) if self.n else None

    def __call__(self, make, *tokens, sig=True):
        self.wait(*tokens)
        if self.linked:
            self.wait(self.last())
        ins = make()
        if sig:
            self.n += 1
            ins.then_inc(self.sem, 1)
            return (self.sem, self.name, self.n)
        return None


class Slot:

    def __init__(self, ap):
        self.ap = ap
        self.free = []


class Ring:
    def __init__(self, aps):
        self.slots = [Slot(a) for a in aps]
        self.n = 0

    def take(self):
        s = self.slots[self.n % len(self.slots)]
        self.n += 1
        f, s.free = s.free, []
        return s, f


class Kern:
    def __init__(self, nc, ctx):
        self.nc, self.ctx = nc, ctx
        self.nsem = 0
        self.names = 0
        self.dsem = []
        self.stores = {}
        self.phase()

    def sem(self, name):
        self.nsem += 1
        n = f"{name}_{self.nsem}"
        return self.ctx.enter_context(self.nc.semaphore(n)), n

    def phase(self):
        nc = self.nc
        self.P = Queue(nc.tensor, *self.sem("pe"), False)
        self.V = Queue(nc.vector, *self.sem("dve"), True)
        self.S = Queue(nc.scalar, *self.sem("act"), True)
        self.G = Queue(nc.gpsimd, *self.sem("pool"), True)
        self.D = Queue(nc.sync, *self.sem("sp"), False)

    def fence(self):
        qs = [self.P, self.V, self.S, self.G]
        self.P(lambda: self.nc.tensor.matmul(
            self.fence_ps[0:1, 0:1], self.fence_sb[0:1, 0:1], self.fence_sb[0:1, 0:1], start=True, stop=True),
            self.V.last(), self.S.last())
        toks = [q.last() for q in qs]
        for q in qs + [self.D]:
            q.wait(*toks)
        self.phase()

    def stored(self, token):
        self.stores[token[1]] = token

    def sb(self, stack, name, shape, dt=F32):
        self.names += 1
        return stack.enter_context(self.nc.sbuf_tensor(f"{name}_{self.names}", shape, dt))

    def dma(self, dst, src, *tokens, q=None, sem=None):
        q = q or self.D
        q.wait(*tokens)
        if sem is None:
            s, n = self.sem("dma")
            sem = [s, n, 0]
        sem[2] += 16
        q.eng.dma_start(dst, src).then_inc(sem[0], 16)
        return (sem[0], sem[1], sem[2])


class Weights:

    def __init__(self, K, stack, units, depth=3, width=1024):
        self.K, self.units, self.depth = K, units, depth
        self.buf = K.sb(stack, "wring", [128, depth, width])
        self.sems = [[*K.sem("w"), 0] for _ in range(depth)]
        self.rel = [None] * depth
        self.issued = 0
        self.n = 0
        self.tok = {}

    def pump(self):
        while self.issued < min(len(self.units), self.n + self.depth):
            i = self.issued
            s = i % self.depth
            self.tok[i] = self.K.dma(self.buf[:, s, :], self.units[i], self.rel[s], sem=self.sems[s])
            self.issued += 1

    def get(self):
        self.pump()
        i = self.n
        return self.buf[:, i % self.depth, :].rearrange("p (k c) -> p k c", c=128), self.tok[i]

    def done(self, token):
        self.rel[self.n % self.depth] = token
        self.n += 1
        self.pump()




def unit_T(K, W, xT, xtok, pair, free):
    w, tok = W.get()
    for k in range(8):
        for h in range(2):
            t = K.P(lambda: K.nc.tensor.matmul(pair[h], w[:, k, :], xT[:, k, 512 * h:512 * h + 512],
                                               start=(k == 0), stop=(k == 7)),
                    tok, xtok, free, sig=(k == 7 and h == 1))
    W.done(t)
    return t


def rms_T(K, stack, h, htok, xT, xfree, gain, eps, ident, banks, off):
    nc, V, S, P = K.nc, K.V, K.S, K.P
    sq = K.sb(stack, "sq", [128, 1024])
    ss = K.sb(stack, "ss", [128, 8])
    xn = K.sb(stack, "xn", [128, 4, 1024])
    for t in range(8):
        a = S(lambda: nc.scalar.activation(sq[:, :], h[:, t, :], ACT.Square, accum_out=ss[:, t:t + 1]), htok)
    b = V(lambda: nc.vector.tensor_scalar(ss[:, :], ss[:, :], 1.0 / 1024, eps, ALU.mult, ALU.add), a)
    b = S(lambda: nc.scalar.activation(ss[:, :], ss[:, :], ACT.Sqrt), b)
    r = V(lambda: nc.vector.reciprocal(ss[:, :], ss[:, :]), b)
    out = None
    tp = None
    for half in range(2):
        for j in range(4):
            t = 4 * half + j
            nt = V(lambda: nc.vector.tensor_scalar(xn[:, j, :], h[:, t, :], ss[:, t:t + 1], None, ALU.mult),
                   r, tp)
        for k in range(8):
            s, f = banks.take()
            for j in range(4):
                tp = P(lambda: nc.tensor.transpose(s.ap[:, 128 * j:128 * j + 128],
                                                   xn[:, j, 128 * k:128 * k + 128], ident), nt, f, sig=(j == 3))
            out = S(lambda: nc.scalar.activation(xT[:, k, 512 * half:512 * half + 512], s.ap, ACT.Copy,
                                                 scale=gain[:, k:k + 1]), tp, xfree)
            s.free = [out]
    return out


def block3(K, C, h, htok, xT, xfree, A, banksets):
    nc, P, V, S = K.nc, K.P, K.V, K.S
    allbanks = banksets
    with ExitStack() as st:
        ident = C.ident
        cols = K.sb(st, "cols", [128, 8 + 4 + 4])
        ct = K.dma(cols[:, :], A["c3"])
        g8 = cols[:, 0:8]
        bf = cols[:, 8:12]
        ring = Ring(allbanks)
        with ExitStack() as s2:
            xtok = rms_T(K, s2, h, [htok, ct], xT, xfree, g8, 1e-6, ident, ring, 0)
        mixT = K.sb(st, "mixT", [128, 8, 1024])
        u = K.sb(st, "ua", [128, 2, 1024])
        vn = K.sb(st, "vn", [128, 8, 512])
        W = Weights(K, st, [A["w3"][i] for i in range(20)])
        stat = K.sb(st, "stat", [128, 8, 8])
        cmat = K.sb(st, "cmat", [128, 4096])
        t_c = K.dma(cmat[:, 0:2048], A["d3"][:, 0:2048])
        dft = cmat[:, 0:2048].rearrange("p (v m u) -> p v m u", v=8, m=2)
        t_g = K.dma(cmat[:, 2048:2048 + 512], A["lng"][:, :].to_broadcast([128, 512]) if False else A["rows3"][0])
        t_g2 = K.dma(cmat[:, 2560:3072], A["rows3"][1])
        t_bs = K.dma(cmat[:, 3072:3584], A["rows3"][2])
        t_ws = K.dma(cmat[:, 3584:4096], A["ws3"])
        lng, lnb, bs = cmat[:, 2048:2560], cmat[:, 2560:3072], cmat[:, 3072:3584]
        ws = cmat[:, 3584:4096].rearrange("p (h q) -> p h q", h=4)
        cd = K.sb(st, "cd", [128, 256])
        t_cd = K.dma(cd[:, :], A["cd"])
        wf = K.sb(st, "wf", [128, 512])
        t_wf = K.dma(wf[:, :], A["wf3"])
        vt = None
        for c in range(4):
            w, tok = W.get()
            for half in range(2):
                s, f = ring.take()
                for j in range(4):
                    t = 4 * half + j
                    for k in range(8):
                        a = P(lambda: nc.tensor.matmul(s.ap[:, 128 * j:128 * j + 128], xT[:, k, 128 * t:128 * t + 128],
                                                       w[:, k, :], start=(k == 0), stop=(k == 7)),
                              tok, xtok, f, sig=(k == 7 and j == 3))
                vt = S(lambda: nc.scalar.activation(
                    vn[:, 4 * half:4 * half + 4, 128 * c:128 * c + 128],
                    s.ap.rearrange("p (j c) -> p j c", j=4), ACT.Gelu), a)
                s.free = [vt]
            W.done(a)
        for t in range(8):
            V(lambda: nc.vector.bn_stats(stat[:, t, 0:6], vn[:, t, :]), vt)
            x = V(lambda: nc.vector.bn_aggr(stat[:, t, 6:8], stat[:, t, 0:6]))
        x = V(lambda: nc.vector.tensor_scalar(stat[:, :, 7], stat[:, :, 7], 1e-6, None, ALU.add))
        x = S(lambda: nc.scalar.activation(stat[:, :, 7], stat[:, :, 7], ACT.Sqrt), x)
        V(lambda: nc.vector.reciprocal(stat[:, :, 7], stat[:, :, 7]), x)
        for t in range(8):
            V(lambda: nc.vector.tensor_scalar(vn[:, t, :], vn[:, t, :], stat[:, t, 6:7], stat[:, t, 7:8],
                                              ALU.subtract, ALU.mult))
            V(lambda: nc.vector.tensor_tensor(vn[:, t, :], vn[:, t, :], lng, ALU.mult), t_g)
            vtok = V(lambda: nc.vector.tensor_tensor(vn[:, t, :], vn[:, t, :], lnb, ALU.add), t_g2)
        ufree = None
        for c in range(4):
            for kind in range(2):
                pair, fr = [], []
                for _ in range(2):
                    s, f = ring.take()
                    pair.append(s)
                    fr += f
                a = unit_T(K, W, xT, xtok, [p.ap for p in pair], fr)
                for hh in range(2):
                    o = u[:, kind, 512 * hh:512 * hh + 512]
                    b = S(lambda: nc.scalar.activation(o, pair[hh].ap, ACT.Gelu if kind == 0 else ACT.Silu), a, ufree)
                    pair[hh].free = [b]
            ug = V(lambda: nc.vector.tensor_tensor(u[:, 0, :], u[:, 0, :], u[:, 1, :], ALU.mult), b)
            for half in range(2):
                s, f = ring.take()
                for j in range(4):
                    t = 4 * half + j
                    a = P(lambda: nc.tensor.matmul(s.ap[:, 128 * j:128 * j + 128], vn[:, t, 128 * c:128 * c + 128],
                                                   ws[:, c, :], start=True, stop=True), vtok, t_ws, f, sig=(j == 3))
                o = mixT[:, c, 512 * half:512 * half + 512]
                bb = bs[:, 128 * c:128 * c + 128].unsqueeze(1).to_broadcast([128, 4, 128])
                b = V(lambda: nc.vector.tensor_tensor(o.rearrange("p (j q) -> p j q", j=4),
                                                      s.ap.rearrange("p (j q) -> p j q", j=4), bb, ALU.add),
                      a, t_bs)
                s.free = [b]
                ufree = V(lambda: nc.vector.tensor_tensor(o, o, u[:, 0, 512 * half:512 * half + 512], ALU.mult))
        zT = K.sb(st, "zT", [128, 1024])
        Z = K.sb(st, "Z", [128, 2, 8, 2, 128])
        Y = K.sb(st, "Y", [128, 8, 2, 128])
        fT = K.sb(st, "fT", [128, 1024])
        r2 = float(np.sqrt(0.5))
        zfree = yfree = ffree = None
        for c in range(4):
            pair, fr = [], []
            for _ in range(2):
                s, f = ring.take()
                pair.append(s)
                fr += f
            a = unit_T(K, W, xT, xtok, [p.ap for p in pair], fr)
            for hh in range(2):
                b = S(lambda: nc.scalar.activation(zT[:, 512 * hh:512 * hh + 512], pair[hh].ap, ACT.Copy), a, zfree)
                pair[hh].free = [b]
            for q in range(4):
                s, f = ring.take()
                for j in range(2):
                    t = 2 * q + j
                    a = P(lambda: nc.tensor.matmul(s.ap[:, 256 * j:256 * j + 256], zT[:, 128 * t:128 * t + 128],
                                                   cd[:, :], start=True, stop=True), b, t_cd, f, sig=(j == 1))
                zz = S(lambda: nc.scalar.activation(Z[:, 0, 2 * q:2 * q + 2, :, :],
                                                    s.ap.rearrange("p (a m c) -> p a m c", a=2, m=2), ACT.Copy),
                       a, yfree)
                s.free = [zz]
            zfree = a
            z0, z1 = Z[:, 0, :, :, :], Z[:, 1, :, :, :]
            V(lambda: nc.vector.tensor_tensor(z1[:, 0:4], z0[:, 0:4], z0[:, 4:8], ALU.add), zz)
            V(lambda: nc.vector.tensor_tensor(z1[:, 4:8], z0[:, 0:4], z0[:, 4:8], ALU.subtract))
            sc = z0[:, 0, :, :]
            V(lambda: nc.vector.tensor_tensor(sc[:, 0], z1[:, 5, 0], z1[:, 5, 1], ALU.add))
            V(lambda: nc.vector.tensor_tensor(sc[:, 1], z1[:, 5, 1], z1[:, 5, 0], ALU.subtract))
            V(lambda: nc.vector.tensor_scalar(z1[:, 5], sc, r2, None, ALU.mult))
            sc = z0[:, 1, :, :]
            V(lambda: nc.vector.tensor_copy(sc[:, 0], z1[:, 6, 1]))
            V(lambda: nc.vector.tensor_scalar(sc[:, 1], z1[:, 6, 0], -1.0, None, ALU.mult))
            V(lambda: nc.vector.tensor_copy(z1[:, 6], sc))
            V(lambda: nc.vector.tensor_tensor(sc[:, 0], z1[:, 7, 1], z1[:, 7, 0], ALU.subtract))
            V(lambda: nc.vector.tensor_tensor(sc[:, 1], z1[:, 7, 1], z1[:, 7, 0], ALU.add))
            V(lambda: nc.vector.tensor_scalar(z1[:, 7, 0], sc[:, 0], r2, None, ALU.mult))
            V(lambda: nc.vector.tensor_scalar(z1[:, 7, 1], sc[:, 1], -r2, None, ALU.mult))
            for hb in (0, 4):
                V(lambda: nc.vector.tensor_tensor(z0[:, hb:hb + 2], z1[:, hb:hb + 2], z1[:, hb + 2:hb + 4], ALU.add))
                V(lambda: nc.vector.tensor_tensor(z0[:, hb + 2:hb + 4], z1[:, hb:hb + 2], z1[:, hb + 2:hb + 4],
                                                  ALU.subtract))
                V(lambda: nc.vector.tensor_copy(z1[:, hb + 3, 0], z0[:, hb + 3, 1]))
                V(lambda: nc.vector.tensor_scalar(z1[:, hb + 3, 1], z0[:, hb + 3, 0], -1.0, None, ALU.mult))
            for hb in (0, 4):
                o = hb // 4
                V(lambda: nc.vector.tensor_tensor(Y[:, o], z0[:, hb], z0[:, hb + 1], ALU.add), yfree)
                V(lambda: nc.vector.tensor_tensor(Y[:, o + 4], z0[:, hb], z0[:, hb + 1], ALU.subtract))
                V(lambda: nc.vector.tensor_tensor(Y[:, o + 2], z0[:, hb + 2], z1[:, hb + 3], ALU.add))
                yt = V(lambda: nc.vector.tensor_tensor(Y[:, o + 6], z0[:, hb + 2], z1[:, hb + 3], ALU.subtract))
            fv = fT[:, :].rearrange("p (u v) -> p v u", v=8)
            for half in range(2):
                s, f = ring.take()
                for j in range(4):
                    v = 4 * half + j
                    for m in range(2):
                        a = P(lambda: nc.tensor.matmul(s.ap[:, 128 * j:128 * j + 128], Y[:, v, m, :], dft[:, v, m, :],
                                                       start=(m == 0), stop=(m == 1)), yt, t_c, f,
                              sig=(j == 3 and m == 1))
                b = V(lambda: nc.vector.tensor_copy(fv[:, 4 * half:4 * half + 4, :],
                                                    s.ap.rearrange("p (v u) -> p v u", v=4)), a, ffree)
                s.free = [b]
            yfree = [a, yt]
            ft = b
            pair, fr = [], []
            for _ in range(2):
                s, f = ring.take()
                pair.append(s)
                fr += f
            a = unit_T(K, W, xT, xtok, [p.ap for p in pair], fr)
            for hh in range(2):
                sg = S(lambda: nc.scalar.activation(u[:, 0, 512 * hh:512 * hh + 512], pair[hh].ap, ACT.Silu),
                       a, ufree)
                pair[hh].free = [sg]
            for hh in range(2):
                s, f = ring.take()
                ffree = P(lambda: nc.tensor.matmul(s.ap, wf[:, 128 * c:128 * c + 128], fT[:, 512 * hh:512 * hh + 512],
                                                   start=True, stop=True), ft, t_wf, f)
                ufree = V(lambda: nc.vector.scalar_tensor_tensor(
                    mixT[:, 4 + c, 512 * hh:512 * hh + 512], s.ap, bf[:, c:c + 1],
                    u[:, 0, 512 * hh:512 * hh + 512], ALU.add, ALU.mult), ffree, sg)
                s.free = [ufree]
        mtok = ufree
        wo = xT
        pe_done = P.last()
        wt = K.dma(xT[:, :, :], A["wo3"], pe_done, V.last(), S.last())
        pg = K.sb(st, "pg", [128, 1024])
        pt = K.dma(pg[:, :], A["post3"])
        ss = K.sb(st, "ss3", [128, 8, 2])
        sq = K.sb(st, "sq3", [128, 512])
        y = Z[:, 0].rearrange("p a m c -> p (a m c)").rearrange("p (s n) -> p s n", s=2)
        yfr = [None, None]
        for t in range(8):
            two = []
            for hh in range(2):
                s, f = ring.take()
                two.append(s)
                for k in range(8):
                    a = P(lambda: nc.tensor.matmul(s.ap, mixT[:, k, 128 * t:128 * t + 128],
                                                   xT[:, k, 512 * hh:512 * hh + 512], start=(k == 0), stop=(k == 7)),
                          mtok, wt, f, sig=(k == 7))
                b = S(lambda: nc.scalar.activation(sq[:, :], s.ap, ACT.Square, accum_out=ss[:, t, hh:hh + 1]), a)
            r = ss[:, t, 0:1]
            b = V(lambda: nc.vector.tensor_tensor(r, r, ss[:, t, 1:2], ALU.add), b)
            b = V(lambda: nc.vector.tensor_scalar(r, r, 1.0 / 1024, 1e-6, ALU.mult, ALU.add))
            b = S(lambda: nc.scalar.activation(r, r, ACT.Sqrt), b)
            b = V(lambda: nc.vector.reciprocal(r, r), b)
            yy = y[:, t % 2, :]
            for hh in range(2):
                b = V(lambda: nc.vector.scalar_tensor_tensor(
                    yy[:, 512 * hh:512 * hh + 512], two[hh].ap, r, pg[:, 512 * hh:512 * hh + 512],
                    ALU.mult, ALU.mult), yfr[t % 2], pt)
                two[hh].free = [b]
            b = V(lambda: nc.vector.tensor_tensor(yy, yy, h[:, t, :], ALU.add))
            yfr[t % 2] = K.dma(A["out"][t], yy, b)
            K.stored(yfr[t % 2])
    return




def take2(ring):
    pair, fr = [], []
    for _ in range(2):
        s, f = ring.take()
        pair.append(s)
        fr += f
    return pair, fr


def rows_unit(K, W, xT, xtok, ring, dst, c):
    nc = K.nc
    w, tok = W.get()
    for half in range(2):
        s, f = ring.take()
        for j in range(4):
            t = 4 * half + j
            for k in range(8):
                a = K.P(lambda: nc.tensor.matmul(s.ap[:, 128 * j:128 * j + 128], xT[:, k, 128 * t:128 * t + 128],
                                                 w[:, k, :], start=(k == 0), stop=(k == 7)),
                        tok, xtok, f, sig=(k == 7 and j == 3))
        vt = K.S(lambda: nc.scalar.activation(
            dst[:, 4 * half:4 * half + 4, 128 * c:128 * c + 128],
            s.ap.rearrange("p (j c) -> p j c", j=4), ACT.Copy), a)
        s.free = [vt]
    W.done(a)
    return vt


def unit_to(K, W, xT, xtok, ring, dst, func, scale=1.0, *tokens):
    pair, fr = take2(ring)
    a = unit_T(K, W, xT, xtok, [p.ap for p in pair], fr)
    for h in range(2):
        b = K.S(lambda: K.nc.scalar.activation(dst[:, 512 * h:512 * h + 512], pair[h].ap, func, scale=scale),
                a, *tokens)
        pair[h].free = [b]
    return b


def stick_breaking(K, st, C, W, xT, xtok, ring, yT, ct):
    nc, P, V, S = K.nc, K.P, K.V, K.S
    q = K.sb(st, "sbq", [128, 1024])
    k = K.sb(st, "sbk", [128, 1024])
    g = K.sb(st, "sbg", [128, 1024])
    vn = K.sb(st, "sbv", [128, 8, 128])
    be = K.sb(st, "be", [128, 2, 1024])
    nb = K.sb(st, "nb", [128, 2, 1024])
    pr = K.sb(st, "pr", [128, 2, 1025])
    wt = K.sb(st, "wt", [128, 2, 1024])
    one = V(lambda: nc.vector.memset(pr[:, :, :], 1.0))
    avr = [None, None]
    tpr = [None, None]
    usedqk = usedv = usedg = None
    oring = Ring([s.ap for s in ring.slots[6:]])
    for s in oring.slots + ring.slots:
        s.free = []
    ring = Ring([s.ap for s in ring.slots[:6]])
    for p in range(2):
        unit_to(K, W, xT, xtok, ring, q, ACT.Copy, 0.125, usedqk)
        qk = unit_to(K, W, xT, xtok, ring, k, ACT.Copy, 1.0, usedqk)
        S.wait(usedv)
        vt = rows_unit(K, W, xT, xtok, ring, vn, 0)
        gt = unit_to(K, W, xT, xtok, ring, g, ACT.Silu, 1.0, usedg)
        steps = [(h, i) for h in range(2) for i in range(8)]
        ob = None
        for n, (h, i) in enumerate(steps):
            b = n % 2
            r = slice(64 * h, 64 * h + 64)
            L = 128 * (i + 1)
            for c0 in range(0, L, 512):
                w = min(512, L - c0)
                s, f = ring.take()
                a = P(lambda: nc.tensor.matmul(s.ap[:, 0:w], q[r, 128 * i:128 * i + 128], k[r, c0:c0 + w],
                                               start=True, stop=True), qk, f)
                S(lambda: nc.scalar.activation(be[:, b, c0:c0 + w], s.ap[:, 0:w], ACT.Sigmoid), a, tpr[b])
                a = S(lambda: nc.scalar.activation(nb[:, b, c0:c0 + w], s.ap[:, 0:w], ACT.Sigmoid, scale=-1.0),
                      tpr[b])
                s.free = [a]
            V(lambda: nc.vector.tensor_tensor(nb[:, b, L - 128:L], nb[:, b, L - 128:L], C.ge, ALU.max), a, ct)
            V(lambda: nc.vector.tensor_tensor(be[:, b, L - 128:L], be[:, b, L - 128:L], C.lt, ALU.mult))
            V(lambda: nc.vector.memset(pr[:, b, L:L + 1], 1.0))
            V(lambda: nc.vector.tensor_tensor_scan(pr[:, b, 0:L][:, ::-1], nb[:, b, 0:L][:, ::-1],
                                                   nb[:, b, 0:L][:, ::-1], 1.0, ALU.mult, ALU.bypass))
            wtok = V(lambda: nc.vector.tensor_tensor(be[:, b, 0:L], be[:, b, 0:L], pr[:, b, 1:L + 1], ALU.mult))
            for c0 in range(0, i + 1, 4):
                m = min(4, i + 1 - c0)
                s, f = ring.take()
                for j in range(m):
                    t = P(lambda: nc.tensor.transpose(s.ap[:, 128 * j:128 * j + 128],
                                                      be[:, b, 128 * (c0 + j):128 * (c0 + j) + 128], C.ident),
                          wtok, f, sig=(j == m - 1))
                ev = V(lambda: nc.vector.tensor_copy(wt[:, b, 128 * c0:128 * (c0 + m)], s.ap[:, 0:128 * m]),
                       t, avr[b])
                s.free = [ev]
            tpr[b] = [t, wtok]
            if i % 4 == 0:
                ob, f = oring.take()
            for j in range(i + 1):
                a = P(lambda: nc.tensor.matmul(ob.ap[r, 128 * (i % 4):128 * (i % 4) + 128],
                                               vn[:, j, 64 * h:64 * h + 64],
                                               wt[:, b, 128 * j:128 * j + 128], start=(j == 0), stop=(j == i)),
                      ev, vt, f, sig=(j == i))
            avr[b] = a
            if i % 4 == 3:
                c0 = 512 * (i // 4)
                e = V(lambda: nc.vector.tensor_tensor(yT[r, p, c0:c0 + 512], ob.ap[r, :], g[r, c0:c0 + 512],
                                                      ALU.mult), a, gt)
                ob.free = [e]
        usedqk = usedv = P.last()
        usedg = e
    return e


def recurrence(K, B, C, ring, nh, dk, q, k, lf, toks, V_n, vcol, vtok, yT, yi, gates, gtok, gain):
    nc, P, V, S = K.nc, K.P, K.V, K.S
    vw = 64 * nh
    E, Xs, acc, Kn, St, on, dec, rs = B.E, B.X, B.acc, B.Kn, B.St, B.on, B.dec, B.rs
    cum = B.cum
    per = 4 // nh
    ct = V(lambda: nc.vector.tensor_tensor_scan(cum, C.reset, lf, 0.0, ALU.mult, ALU.add), toks)
    a4 = acc[:, 0:nh * 1024].rearrange("p (g j s) -> p g j s", j=4, s=128)
    xr = [None, None]
    for lev in range(-1, 7):
        if lev < 0:
            xt = toks
            left, right = k, q
        else:
            b = lev % 2
            X = Xs[:, b, :]
            Bk = 1 << lev
            c3 = cum.rearrange("p (n b) -> p n b", b=2 * Bk)
            m = c3[:, :, Bk - 1:Bk].to_broadcast([128, 1024 // (2 * Bk), 2 * Bk])
            X3 = X.rearrange("p (n b) -> p n b", b=2 * Bk)
            t = V(lambda: nc.vector.tensor_tensor(X3, c3, m, ALU.subtract), xr[b])
            t = S(lambda: nc.scalar.activation(X, X, ACT.Abs), t)
            t = S(lambda: nc.scalar.activation(X, X, ACT.Exp, scale=-1.0), t)
            q3 = q.rearrange("p (n b) -> p n b", b=2 * Bk)
            k3 = k.rearrange("p (n b) -> p n b", b=2 * Bk)
            V(lambda: nc.vector.tensor_tensor(X3[:, :, 0:Bk], X3[:, :, 0:Bk], k3[:, :, 0:Bk], ALU.mult), t)
            xt = V(lambda: nc.vector.tensor_tensor(X3[:, :, Bk:], X3[:, :, Bk:], q3[:, :, Bk:], ALU.mult))
            left = right = X
        for grp in range(2 * nh):
            s, f = ring.take()
            h = grp // 2
            for j in range(4):
                t = 4 * (grp % 2) + j
                r = slice(dk * h, dk * h + dk)
                a = P(lambda: nc.tensor.matmul(s.ap[:, 128 * j:128 * j + 128], left[r, 128 * t:128 * t + 128],
                                               right[r, 128 * t:128 * t + 128], start=True, stop=True,
                                               tile_position=(dk * h, 0)),
                      xt, f, sig=(j == 3))
            dst = a4[:, grp]
            src = s.ap.rearrange("p (j s) -> p j s", s=128)
            if lev < 0:
                im = C.ident.unsqueeze(1).to_broadcast([128, 4, 128])
                e = V(lambda: nc.vector.tensor_tensor(dst, src, im, ALU.mult), a)
            else:
                lm = C.lmask[:, lev, :].unsqueeze(1).to_broadcast([128, 4, 128])
                e = V(lambda: nc.vector.copy_predicated(dst, lm, src), a)
            s.free = [e]
        if lev >= 0:
            xr[b] = a
        yield
    acct = e
    c3 = cum.rearrange("p (n b) -> p n b", b=128)
    last = c3[:, :, 127:128]
    dt = S(lambda: nc.scalar.activation(dec, c3[:, :, 127], ACT.Exp), ct)
    t = V(lambda: nc.vector.tensor_tensor(E.rearrange("p (n b) -> p n b", b=128), last.to_broadcast([128, 8, 128]), c3,
                                          ALU.subtract))
    t = S(lambda: nc.scalar.activation(E, E, ACT.Exp), t)
    kd = V(lambda: nc.vector.tensor_tensor(E, E, k, ALU.mult), t)
    Qc = Xs[:, 0, :]
    t = S(lambda: nc.scalar.activation(Qc, cum, ACT.Exp), xr[0], xr[1])
    qc = V(lambda: nc.vector.tensor_tensor(Qc, Qc, q, ALU.mult), t)
    for half in range(2):
        s, f = ring.take()
        for j in range(4):
            t = 4 * half + j
            a = P(lambda: nc.tensor.transpose(s.ap[:, 128 * j:128 * j + 128], E[:, 128 * t:128 * t + 128], C.ident),
                  kd, f, sig=(j == 3))
        e = S(lambda: nc.scalar.activation(Kn[:, 512 * half:512 * half + 512], s.ap, ACT.Copy), a)
        s.free = [e]
    kn = e
    yield
    bm = C.bd64 if nh == 2 else C.bd32
    tokS = None
    tmp = B.tmp
    for t in range(7):
        s, f = ring.take()
        a = P(lambda: nc.tensor.matmul(s.ap[:, 0:vw], Kn[:, 128 * t:128 * t + 128], V_n[:, t, vcol:vcol + vw],
                                       start=True, stop=True), kn, vtok, f)
        if t == 0:
            tokS = V(lambda: nc.vector.tensor_tensor(St[:, 1, 0:vw], s.ap[:, 0:vw], bm, ALU.mult), a)
        else:
            V(lambda: nc.vector.tensor_tensor(tmp[:, 0:vw], s.ap[:, 0:vw], bm, ALU.mult), a)
            tokS = V(lambda: nc.vector.scalar_tensor_tensor(St[:, t + 1, 0:vw], St[:, t, 0:vw], dec[:, t:t + 1],
                                                            tmp[:, 0:vw], ALU.mult, ALU.add), dt)
        s.free = [tokS]
        yield
    tpb = 512 // vw
    o3 = on[:, 0:8 * vw]
    for grp in range(8 // tpb):
        s, f = ring.take()
        for j in range(tpb):
            t = grp * tpb + j
            if t > 0:
                P(lambda: nc.tensor.matmul(s.ap[:, vw * j:vw * j + vw], Qc[:, 128 * t:128 * t + 128],
                                           St[:, t, 0:vw], start=True, stop=False, skip_group_check=True),
                  qc, tokS, acct, f, sig=False)
            for h in range(nh):
                idx = 8 * h + t
                a = P(lambda: nc.tensor.matmul(s.ap[:, vw * j + 64 * h:vw * j + 64 * h + 64],
                                               acc[:, 128 * idx:128 * idx + 128],
                                               V_n[:, t, vcol + 64 * h:vcol + 64 * h + 64],
                                               start=(t == 0 and h == 0), stop=(h == nh - 1), skip_group_check=True),
                      acct, vtok, qc, f, sig=(j == tpb - 1 and h == nh - 1))
        e = S(lambda: nc.scalar.activation(on[:, 512 * grp:512 * grp + 512], s.ap, ACT.Copy), a, B.onfree)
        s.free = [e]
        yield
    n = 8 * nh
    e2 = S(lambda: nc.scalar.activation(B.sq[:, 0:8 * vw], on[:, 0:8 * vw], ACT.Square), a)
    V(lambda: nc.vector.tensor_reduce(rs[:, 0:n], B.sq[:, 0:8 * vw].rearrange("p (n v) -> p n v", v=64), AX.X,
                                      ALU.add), e2)
    b = V(lambda: nc.vector.tensor_scalar(rs[:, 0:n], rs[:, 0:n], 1.0 / 64, 1e-5, ALU.mult, ALU.add))
    b = S(lambda: nc.scalar.activation(rs[:, 0:n], rs[:, 0:n], ACT.Sqrt), b)
    V(lambda: nc.vector.reciprocal(rs[:, 0:n], rs[:, 0:n]), b)
    ov = o3.rearrange("p (n v) -> p n v", v=64)
    b = V(lambda: nc.vector.tensor_tensor(ov, ov, rs[:, 0:n].unsqueeze(2).to_broadcast([128, n, 64]), ALU.mult))
    for c in range(nh // 2):
        for half in range(2):
            s, f = ring.take()
            for j in range(4):
                t = 4 * half + j
                a = P(lambda: nc.tensor.transpose(s.ap[:, 128 * j:128 * j + 128],
                                                  on[:, vw * t + 128 * c:vw * t + 128 * c + 128], C.ident),
                      b, f, sig=(j == 3))
            e = V(lambda: nc.vector.scalar_tensor_tensor(yT[:, yi + c, 512 * half:512 * half + 512], s.ap,
                                                         gain[:, c:c + 1], gates[:, c, 512 * half:512 * half + 512],
                                                         ALU.mult, ALU.mult), a, gtok)
            s.free = [e]
        yield
    B.onfree = a
    B.done = e


def log_sigmoid(K, B, src, stok, bias, dst, dtok):
    nc, V, S = K.nc, K.V, K.S
    for h in range(2):
        sl = slice(512 * h, 512 * h + 512)
        e = S(lambda: nc.scalar.activation(B.E[:, sl], src[h].ap, ACT.Identity, bias=bias), stok, dtok)
        src[h].free = src[h].free + [e]
    S(lambda: nc.scalar.activation(dst, B.E, ACT.Abs), dtok)
    S(lambda: nc.scalar.activation(dst, dst, ACT.Exp, scale=-1.0))
    e = S(lambda: nc.scalar.activation(dst, dst, ACT.Ln, bias=1.0))
    return V(lambda: nc.vector.scalar_tensor_tensor(dst, B.E, 0.0, dst, ALU.min, ALU.subtract), e)


class Bufs:
    pass


def run(gen):
    for _ in gen:
        pass


def block1(K, C, h, xT, xtok, A, banks):
    nc, P, V, S = K.nc, K.P, K.V, K.S
    ring = Ring(banks)
    with ExitStack() as st:
        cols = K.sb(st, "cols1", [128, 16])
        rst = K.sb(st, "rst", [128, 1024])
        C.reset = rst[:, :]
        V.wait(K.dma(rst[:, :], A["rst"]))
        ct = K.dma(cols[:, :], A["c1"])
        hg, cg, cb, lbl = cols[:, 0:2], cols[:, 2:4], cols[:, 4:5], cols[:, 5:7]
        lb, oml, z1 = cols[:, 7:9], cols[:, 9:11], cols[:, 11:13]
        yT = K.sb(st, "yT", [128, 6, 1024])
        V(lambda: nc.vector.tensor_tensor(z1, lbl, lbl, ALU.subtract), ct)
        t = V.last()
        t = S(lambda: nc.scalar.activation(z1, z1, ACT.Exp), t)
        V(lambda: nc.vector.reciprocal(lb, z1), t)
        V(lambda: nc.vector.tensor_tensor(z1, z1, lb, ALU.mult))
        V(lambda: nc.vector.tensor_tensor(lb, z1, z1, ALU.subtract))
        lbt = V(lambda: nc.vector.tensor_scalar(oml, lb, -1.0, 1.0, ALU.mult, ALU.add))
        with ExitStack() as s2:
            W = Weights(K, s2, [A["w1"][i] for i in range(8 + 8)] + [A["w1"][i] for i in range(16, 23)])
            with ExitStack() as s3:
                stick_breaking(K, s3, C, W, xT, xtok, ring, yT, C.tok)
                K.fence()
                P, V, S = K.P, K.V, K.S
            B = Bufs()
            big = K.sb(s2, "recb", [128, 4, 1024])
            B.cum, B.E = big[:, 0, :], big[:, 1, :]
            B.X = big[:, 2:4, :]
            q = K.sb(s2, "rq", [128, 1024])
            kk = K.sb(s2, "rk", [128, 1024])
            lf = K.sb(s2, "rlf", [128, 1024])
            gts = K.sb(s2, "rg", [128, 2, 1024])
            vn = K.sb(s2, "rvn", [128, 8, 256])
            acc = K.sb(s2, "racc", [128, 4096])
            B.acc = acc
            B.sq = big[:, 2:4, :].rearrange("p a n -> p (a n)")
            B.on = K.sb(s2, "ron", [128, 2048])
            B.St = K.sb(s2, "rst", [128, 8, 256])
            kn = K.sb(s2, "rkn", [128, 1024])
            B.Kn = kn[:, :]
            B.tmp = K.sb(s2, "rtmp", [128, 256])
            sm = K.sb(s2, "rsm", [128, 64])
            B.dec, B.rs = sm[:, 0:8], sm[:, 8:40]
            B.onfree = None
            for p in range(2):
                pair, fr = take2(ring)
                a = unit_T(K, W, xT, xtok, [x.ap for x in pair], fr)
                for hh in range(2):
                    e = S(lambda: nc.scalar.activation(kk[:, 512 * hh:512 * hh + 512], pair[hh].ap, ACT.Sigmoid,
                                                       scale=-1.0), a)
                    pair[hh].free = [e]
                V(lambda: nc.vector.tensor_scalar(kk[:, :], kk[:, :], oml[:, p:p + 1], None, ALU.mult), e, lbt)
                ls = log_sigmoid(K, B, pair, a, 0.0, lf[:, :], None)
                V(lambda: nc.vector.tensor_scalar(B.E, B.E, -1.0, 60.0, ALU.mult, ALU.min))
                t = S(lambda: nc.scalar.activation(B.E, B.E, ACT.Exp), V.last())
                t = V(lambda: nc.vector.tensor_scalar(B.E, B.E, lb[:, p:p + 1], None, ALU.mult), t)
                t = S(lambda: nc.scalar.activation(B.E, B.E, ACT.Ln, bias=1.0), t)
                lft = V(lambda: nc.vector.tensor_tensor(lf[:, :], lf[:, :], B.E, ALU.add), t)
                qt = unit_to(K, W, xT, xtok, ring, q, ACT.Copy)
                vt = rows_unit(K, W, xT, xtok, ring, vn, 0)
                gt = unit_to(K, W, xT, xtok, ring, gts[:, 0, :], ACT.Silu)
                run(recurrence(K, B, C, ring, 2, 64, q[:, :], kk[:, :], lf[:, :], [qt, lft], vn, 0, vt,
                               yT, 2 + p, gts, gt, hg[:, p:p + 1]))
                S.wait(K.P.last(), K.V.last())
                V.wait(K.P.last(), K.S.last())
            unit_to(K, W, xT, xtok, ring, q, ACT.Copy, 32 ** -0.5)
            qt = unit_to(K, W, xT, xtok, ring, kk, ACT.Copy)
            for c in range(2):
                vt = rows_unit(K, W, xT, xtok, ring, vn, c)
            for c in range(2):
                gt = unit_to(K, W, xT, xtok, ring, gts[:, c, :], ACT.Silu)
            w2 = K.sb(s2, "w2", [16, 128])
            w2t = K.dma(w2[:, :], A["w2"])
            cr = K.sb(s2, "cr", [16, 1024])
            w, tok = W.get()
            pair, fr = take2(ring)
            for k in range(8):
                for hh in range(2):
                    a = P(lambda: nc.tensor.matmul(pair[hh].ap[0:16, :], w[:, k, 0:16],
                                                   xT[:, k, 512 * hh:512 * hh + 512], start=(k == 0), stop=(k == 7)),
                          tok, xtok, fr)
            W.done(a)
            for hh in range(2):
                e = S(lambda: nc.scalar.activation(cr[:, 512 * hh:512 * hh + 512], pair[hh].ap[0:16, :], ACT.Copy), a)
                pair[hh].free = [e]
            pair, fr = take2(ring)
            for hh in range(2):
                a = P(lambda: nc.tensor.matmul(pair[hh].ap, w2[:, :], cr[:, 512 * hh:512 * hh + 512], start=True,
                                               stop=True), e, w2t, fr)
            log_sigmoid(K, B, pair, a, cb, lf[:, :], ct)
            lft = V(lambda: nc.vector.tensor_scalar(lf[:, :], lf[:, :], 1.0 / 16, None, ALU.mult))
            run(recurrence(K, B, C, ring, 4, 32, q[:, :], kk[:, :], lf[:, :], [qt, lft], vn, 0, vt,
                           yT, 4, gts, gt, cg))
            K.fence()
            P, V, S = K.P, K.V, K.S
        with ExitStack() as s2:
            W = Weights(K, s2, [A["wg"][i] for i in range(24)], width=1280)
            merged = K.sb(s2, "merged", [128, 8, 1024])
            sg = K.sb(s2, "sg", [128, 2, 1024])
            ht = K.dma(h[:, :, :], A["x"])
            sgf = [None, None]
            n = 0
            for d in range(8):
                for br in range(3):
                    pair, fr = take2(ring)
                    w, tok = W.get()
                    for k in range(8):
                        for hh in range(2):
                            a = P(lambda: nc.tensor.matmul(pair[hh].ap, w[:, k, :], xT[:, k, 512 * hh:512 * hh + 512],
                                                           start=(k == 0), stop=(k == 7)),
                                  tok, xtok, fr, sig=(k == 7))
                    for hh in range(2):
                        e = S(lambda: nc.scalar.activation(sg[:, n % 2, 512 * hh:512 * hh + 512], pair[hh].ap,
                                                           ACT.Sigmoid), a, sgf[n % 2])
                        pair[hh].free = [e]
                    pair, fr = take2(ring)
                    for k in range(2):
                        for hh in range(2):
                            a = P(lambda: nc.tensor.matmul(pair[hh].ap, w[:, 8 + k, :],
                                                           yT[:, 2 * br + k, 512 * hh:512 * hh + 512],
                                                           start=(k == 0), stop=(k == 1)), fr, sig=(k == 1))
                    W.done(a)
                    for hh in range(2):
                        m = merged[:, d, 512 * hh:512 * hh + 512]
                        g = sg[:, n % 2, 512 * hh:512 * hh + 512]
                        t = V(lambda: nc.vector.tensor_tensor(m if br == 0 else g, pair[hh].ap, g, ALU.mult), a, e)
                        pair[hh].free = [t]
                        if br:
                            t = V(lambda: nc.vector.tensor_tensor(m, m, g, ALU.add))
                    sgf[n % 2] = t
                    n += 1
            mt = t
            wo = K.sb(s2, "wo1", [128, 8, 1024])
            wt = K.dma(wo[:, :, :], A["wo1"])
            rows = K.sb(s2, "rows1", [128, 2, 1024])
            rt = K.dma(rows[:, :, :], A["rows1"])
            stt = K.sb(s2, "st1", [128, 8, 14])
            for t in range(8):
                for hh in range(2):
                    s, f = ring.take()
                    for k in range(8):
                        a = P(lambda: nc.tensor.matmul(s.ap, merged[:, k, 128 * t:128 * t + 128],
                                                       wo[:, k, 512 * hh:512 * hh + 512], start=(k == 0), stop=(k == 7)),
                              mt, wt, f, sig=(k == 7))
                    hs = h[:, t, 512 * hh:512 * hh + 512]
                    e = V(lambda: nc.vector.scalar_tensor_tensor(hs, hs, float(2 ** 0.25), s.ap, ALU.mult, ALU.add),
                          a, ht)
                    s.free = [e]
                    V(lambda: nc.vector.bn_stats(stt[:, t, 6 * hh:6 * hh + 6], hs))
                V(lambda: nc.vector.bn_aggr(stt[:, t, 12:14], stt[:, t, 0:12]))
                e = V(lambda: nc.vector.tensor_scalar(stt[:, t, 13:14], stt[:, t, 13:14], 1e-5, None, ALU.add))
                e = S(lambda: nc.scalar.activation(stt[:, t, 13:14], stt[:, t, 13:14], ACT.Sqrt), e)
                V(lambda: nc.vector.reciprocal(stt[:, t, 13:14], stt[:, t, 13:14]), e)
                V(lambda: nc.vector.tensor_scalar(h[:, t, :], h[:, t, :], stt[:, t, 12:13], stt[:, t, 13:14],
                                                  ALU.subtract, ALU.mult))
                V(lambda: nc.vector.tensor_tensor(h[:, t, :], h[:, t, :], rows[:, 0, :], ALU.mult), rt)
                e = V(lambda: nc.vector.tensor_tensor(h[:, t, :], h[:, t, :], rows[:, 1, :], ALU.add))
            K.fence()
    return e



EC = float(np.exp(-0.5))


def weave(*gens):
    live = list(gens)
    while live:
        for g in list(live):
            try:
                next(g)
            except StopIteration:
                live.remove(g)


def steps(gen, n):
    for _ in range(n):
        try:
            next(gen)
        except StopIteration:
            return
        yield


def unit_steps(K, W, xT, xtok, ring, out):
    pair, fr = take2(ring)
    w, tok = W.get()
    for k in range(8):
        for h in range(2):
            t = K.P(lambda: K.nc.tensor.matmul(pair[h].ap, w[:, k, :], xT[:, k, 512 * h:512 * h + 512],
                                               start=(k == 0), stop=(k == 7)),
                    tok, xtok, fr, sig=(k == 7 and h == 1))
        yield
    W.done(t)
    out.append((pair, t))


def rwkv(K, C, W, xT, xtok, A, banks, st, cols, ctok):
    nc, P, V, S, G = K.nc, K.P, K.V, K.S, K.G
    RU, RG, RC, RY = Ring(banks[0:3]), Ring(banks[3:5]), Ring(banks[5:7]), Ring(banks[7:8])
    sb = lambda n, s, d=F32: K.sb(st, n, s, d)
    AR = sb("AR", [128, 2, 16, 2, 64])
    vT = sb("vT", [128, 2, 1024])
    Bc = sb("Bc", [128, 2, 1024])
    Kc = sb("Kc", [128, 2, 1024])
    bon = sb("bon", [128, 2, 1024])
    pc = sb("pc", [128, 2, 16])
    raw = sb("raw", [128, 1028])
    r = sb("r", [128, 1024])
    k = sb("k", [128, 1024])
    sg = sb("sg2", [128, 1024])
    cum = sb("cum2", [128, 1024])
    ex = sb("ex", [128, 1024])
    av = sb("av", [128, 1024])
    kk = sb("kk", [128, 1024])
    D = sb("D", [128, 1024])
    lo = sb("lo", [128, 1024])
    wup = sb("wup", [128, 1024])
    bdb, bdk, bdv = sb("bdb", [128, 4, 2, 64]), sb("bdk", [128, 4, 2, 64]), sb("bdv", [128, 4, 2, 64])
    LT, X, M1 = sb("LT", [128, 4, 128]), sb("X", [128, 4, 128]), sb("M1", [128, 4, 128])
    bda, bdr = sb("bda", [128, 2, 4, 2, 64]), sb("bdr", [128, 2, 4, 2, 64])
    mka, mkr, mbr = sb("mka", [128, 2, 4, 128]), sb("mkr", [128, 2, 4, 128]), sb("mbr", [128, 2, 4, 128])
    XT = sb("XT", [128, 2, 4, 128])
    Bn, Kn = sb("Bn", [128, 2, 4, 128]), sb("Kn", [128, 2, 4, 128])
    Vn = sb("Vn", [128, 2, 4, 64])
    ST = sb("ST", [128, 2, 64])
    zu = sb("zu", [128, 3, 64])
    Y = sb("Y", [128, 16, 64])
    ybd = sb("ybd", [128, 8, 2, 64])
    ys = sb("ys", [128, 32])
    mu, w0, a0, kkc, kac, rkc, lnw, lnb = [cols[:, 8 * i:8 * i + 8] for i in range(8)]
    mur, muk, muv = cols[:, 64:72], cols[:, 72:80], cols[:, 80:88]
    mulo = cols[:, 88:89]
    omka = cols[:, 96:104]
    for b in (bdb, bdk, bdv, bda, bdr, ybd, raw):
        z = V(lambda: nc.vector.memset(b[:], 0.0))
    for q in (S, G, P):
        q.wait(z)
    V(lambda: nc.vector.tensor_scalar(omka, kac, -1.0, 1.0, ALU.mult, ALU.add), ctok)
    wt = K.dma(wup[:, :], A["wup2"])
    state = {"pairfree": [None, None], "gfree": [None, None], "s1": None, "raw": None, "y": None, "st": None,
             "gn": 0, "tmpf": None}

    def shift(pair, a, mucol, dst, dfree):
        for h in range(2):
            e = S(lambda: nc.scalar.activation(raw[:, 1 + 512 * h:513 + 512 * h], pair[h].ap, ACT.Copy), a,
                  state["raw"])
            pair[h].free = [e]
        V(lambda: nc.vector.tensor_tensor(D[:, :], raw[:, 0:1024], raw[:, 1:1025], ALU.subtract), e, dfree)
        state["raw"] = V(lambda: nc.vector.scalar_tensor_tensor(dst, D[:, :], mucol, raw[:, 1:1025], ALU.mult,
                                                                ALU.add), ctok)
        return state["raw"]

    def prep_lo():
        out = []
        yield from unit_steps(K, W, xT, xtok, RU, out)
        t = shift(*out[0], mulo, lo[:, :], None)
        state["lo"] = S(lambda: nc.scalar.activation(lo[0:64, :], lo[0:64, :], ACT.Tanh), t)

    def both(lhs, rhs, toks):
        pair, fr = take2(RU)
        for h in range(2):
            a = P(lambda: nc.tensor.matmul(pair[h].ap, lhs, rhs[:, 512 * h:512 * h + 512], start=True, stop=True),
                  toks, fr)
        return pair, a

    def evac(pair, a, dst, func, scale=1.0, bias=0.0, *toks):
        for h in range(2):
            if func == ACT.Copy:
                e = S(lambda: nc.scalar.activation(dst[:, 512 * h:512 * h + 512], pair[h].ap, func, scale=scale), a,
                      *toks)
            else:
                e = S(lambda: nc.scalar.activation(dst[:, 512 * h:512 * h + 512], pair[h].ap, func, scale=scale,
                                                   bias=bias), a, *toks)
            pair[h].free = [e]
        return e

    def prep(p):
        b = p % 2
        pf = state["pairfree"][b]
        out = []
        yield from unit_steps(K, W, xT, xtok, RU, out)
        rt = shift(*out[-1], mur[:, p:p + 1], r[:, :], pf)
        yield
        yield from unit_steps(K, W, xT, xtok, RU, out)
        kt = shift(*out[-1], muk[:, p:p + 1], k[:, :], None)
        yield
        yield from unit_steps(K, W, xT, xtok, RU, out)
        vt = shift(*out[-1], muv[:, p:p + 1], vT[:, b, :], pf)
        yield
        cs = slice(128 * p, 128 * p + 128)
        pair, a = both(wup[0:64, cs], lo[0:64, :], [wt, state["lo"]])
        e = evac(pair, a, sg, ACT.Sigmoid, 1.0, w0[:, p:p + 1], state["tmpf"], ctok)
        yield
        ctk = V(lambda: nc.vector.tensor_tensor_scan(cum[:, :], C.reset64, sg[:, :], 0.0, ALU.mult, ALU.add), e)
        pair, a = both(wup[64:128, cs], lo[64:128, :], [wt, state["lo"]])
        at = evac(pair, a, av, ACT.Sigmoid, 1.0, a0[:, p:p + 1], state["tmpf"], ctok)
        yield
        t = V(lambda: nc.vector.tensor_scalar(kk[:, :], k[:, :], kkc[:, p:p + 1], None, ALU.mult))
        t = S(lambda: nc.scalar.activation(ex[:, :], kk[:, :], ACT.Square), t, state["tmpf"])
        pair, a = both(C.bd64, ex, [t])
        t = evac(pair, a, ex, ACT.Sqrt, 1.0, 0.0)
        yield
        V(lambda: nc.vector.tensor_scalar(ex[:, :], ex[:, :], 1e-12, None, ALU.max), t)
        V(lambda: nc.vector.reciprocal(ex[:, :], ex[:, :]))
        V(lambda: nc.vector.tensor_tensor(kk[:, :], kk[:, :], ex[:, :], ALU.mult))
        yield
        V(lambda: nc.vector.tensor_scalar(D[:, :], av[:, :], kac[:, p:p + 1], omka[:, p:p + 1], ALU.mult, ALU.add),
          at)
        V(lambda: nc.vector.tensor_tensor(k[:, :], k[:, :], D[:, :], ALU.mult))
        t = V(lambda: nc.vector.scalar_tensor_tensor(D[:, :], r[:, :], rkc[:, p:p + 1], k[:, :], ALU.mult, ALU.mult))
        pair, a = both(C.bd64, D, [t])
        for h in range(2):
            sl = slice(512 * h, 512 * h + 512)
            e = V(lambda: nc.vector.tensor_tensor(bon[:, b, sl], pair[h].ap, vT[:, b, sl], ALU.mult), a)
            pair[h].free = [e]
        yield
        t = S(lambda: nc.scalar.activation(ex[:, :], cum[:, :], ACT.Exp, scale=-EC), ctk, V.last())
        c16 = lambda x: x.rearrange("p (c t) -> p c t", t=64)
        V(lambda: nc.vector.tensor_tensor(AR[:, b, :, 1, :], c16(r[:, :]), c16(ex[:, :]), ALU.mult), t)
        x = V(lambda: nc.vector.tensor_copy(pc[:, b, :], c16(ex[:, :])[:, :, 63]))
        t = V(lambda: nc.vector.tensor_tensor(D[:, :], cum[:, :], sg[:, :], ALU.subtract), a)
        t = S(lambda: nc.scalar.activation(D[:, :], D[:, :], ACT.Exp, scale=-EC), t)
        t2 = S(lambda: nc.scalar.activation(ex[:, :], cum[:, :], ACT.Exp, scale=EC), x)
        yield
        V(lambda: nc.vector.scalar_tensor_tensor(AR[:, b, :, 0, :], c16(kk[:, :]), -1.0, c16(D[:, :]), ALU.mult,
                                                 ALU.mult), t)
        V(lambda: nc.vector.tensor_tensor(Kc[:, b, :], k[:, :], ex[:, :], ALU.mult), t2)
        yield
        V(lambda: nc.vector.tensor_tensor(kk[:, :], kk[:, :], av[:, :], ALU.mult))
        t = V(lambda: nc.vector.tensor_tensor(Bc[:, b, :], kk[:, :], ex[:, :], ALU.mult))
        state["tmpf"] = t
        state[("prep", p)] = t

    def stage(p, g, n):
        b, gb = p % 2, n % 2
        pt = state[("prep", p)]
        gf = state["gfree"][gb]
        s1 = state["s1"]
        for h in range(2):
            rr = slice(64 * h, 64 * h + 64)
            gs = slice(256 * g, 256 * g + 256)
            c4 = lambda x: x.rearrange("p (c t) -> p c t", t=64)
            G(lambda: nc.gpsimd.tensor_copy(bdb[rr, :, h, :], c4(Bc[rr, b, gs])), pt, s1)
            G(lambda: nc.gpsimd.tensor_copy(bdk[rr, :, h, :], c4(Kc[rr, b, gs])))
            G(lambda: nc.gpsimd.tensor_copy(bdv[rr, :, h, :], c4(vT[rr, b, gs])))
            G(lambda: nc.gpsimd.tensor_copy(bda[rr, gb, :, h, :], AR[rr, b, 4 * g:4 * g + 4, 0, :]), gf)
            bt = G(lambda: nc.gpsimd.tensor_copy(bdr[rr, gb, :, h, :], AR[rr, b, 4 * g:4 * g + 4, 1, :]))
        yield
        for (bd, outs) in ((bdb, ((LT[:, :, :], C.mS), (mbr[:, gb], C.mI))),
                           (bdk, ((mka[:, gb], C.mS), (mkr[:, gb], C.mI)))):
            s, f = RG.take()
            for c in range(4):
                a = P(lambda: nc.tensor.matmul(s.ap[:, 128 * c:128 * c + 128],
                                               bd[:, c, :, :].rearrange("p h s -> p (h s)"),
                                               AR[:, b, 4 * g + c, :, :].rearrange("p x t -> p (x t)"),
                                               start=True, stop=True), bt, pt, f, sig=(c == 3))
            s4 = s.ap.rearrange("p (c x t) -> p c x t", c=4, x=2)
            for x, (dst, m) in enumerate(outs):
                src = s4[:, :, x, :].unsqueeze(2).to_broadcast([128, 4, 2, 64])
                mm = m.rearrange("p (h t) -> p h t", h=2).unsqueeze(1).to_broadcast([128, 4, 2, 64])
                e = V(lambda: nc.vector.tensor_tensor(dst.rearrange("p c (h t) -> p c h t", h=2), src, mm, ALU.mult),
                      a, gf, s1)
            s.free = [e]
            if bd is bdb:
                lt = e
            yield
        mt = e
        xt3 = XT[:, gb]
        lm = lambda l: C.lmask[:, l, :].unsqueeze(1).to_broadcast([128, 4, 128])
        V(lambda: nc.vector.tensor_copy(xt3, C.ident.unsqueeze(1).to_broadcast([128, 4, 128])))
        xtt = V(lambda: nc.vector.copy_predicated(xt3, lm(0), LT[:, :, :]))
        s, f = RG.take()
        for c in range(4):
            a = P(lambda: nc.tensor.transpose(s.ap[:, 128 * c:128 * c + 128],
                                              bdb[:, c, :, :].rearrange("p h s -> p (h s)"), C.ident), bt, f,
                  sig=(c == 3))
        e = S(lambda: nc.scalar.activation(Bn[:, gb].rearrange("p c s -> p (c s)"), s.ap, ACT.Copy), a, gf)
        s.free = [e]
        yield
        s, f = RG.take()
        for c in range(4):
            a = P(lambda: nc.tensor.transpose(s.ap[:, 128 * c:128 * c + 128],
                                              bdk[:, c, :, :].rearrange("p h s -> p (h s)"), C.ident), bt, f,
                  sig=(c == 3))
        e = S(lambda: nc.scalar.activation(Kn[:, gb].rearrange("p c s -> p (c s)"), s.ap, ACT.Copy), a)
        s.free = [e]
        yield
        s, f = RG.take()
        for c in range(4):
            a = P(lambda: nc.tensor.matmul(s.ap[:, 64 * c:64 * c + 64],
                                           bdv[:, c, :, :].rearrange("p h s -> p (h s)"), C.stack,
                                           start=True, stop=True), bt, f, sig=(c == 3))
        nt = S(lambda: nc.scalar.activation(Vn[:, gb].rearrange("p c s -> p (c s)"), s.ap[:, 0:256], ACT.Copy), a)
        s.free = [nt]
        yield
        xpe = s1
        mpe = s1
        for l in range(1, 6):
            s, f = RG.take()
            for c in range(4):
                a = P(lambda: nc.tensor.transpose(s.ap[:, 128 * c:128 * c + 128], xt3[:, c, :], C.ident), xtt, f,
                      sig=(c == 3))
            e = S(lambda: nc.scalar.activation(X[:, :, :].rearrange("p c s -> p (c s)"), s.ap, ACT.Copy), a, xpe)
            s.free = [e]
            yield
            s, f = RG.take()
            for c in range(4):
                a = P(lambda: nc.tensor.matmul(s.ap[:, 128 * c:128 * c + 128], LT[:, c, :], X[:, c, :], start=True,
                                               stop=True), lt, e, f, sig=(c == 3))
            xpe = a
            e = S(lambda: nc.scalar.activation(M1[:, :, :].rearrange("p c s -> p (c s)"), s.ap, ACT.Copy), a, mpe)
            s.free = [e]
            yield
            s, f = RG.take()
            for c in range(4):
                a = P(lambda: nc.tensor.matmul(s.ap[:, 128 * c:128 * c + 128], M1[:, c, :], xt3[:, c, :], start=True,
                                               stop=True), xtt, e, f, sig=(c == 3))
            mpe = a
            xtt = V(lambda: nc.vector.copy_predicated(xt3, lm(l), s.ap.rearrange("p (c s) -> p c s", c=4)), a)
            s.free = [xtt]
            yield
        state["s1"] = a
        state[("st", n)] = [bt, mt, nt, xtt]
        if g == 3:
            state["pf1"] = [a, bt]

    def chain(p, g, n):
        gb, b = n % 2, p % 2
        tk = state[("st", n)]
        ys_, yf = RY.take()
        for c in range(4):
            i = state["gn"] % 2
            j = 1 - i
            cc = 4 * g + c
            if cc == 0:
                state["st"] = V(lambda: nc.vector.memset(ST[:, i, :], 0.0), state["y"])
            stt = state["st"]
            V(lambda: nc.vector.tensor_scalar(zu[:, 2, :], ST[:, i, :], pc[:, b, cc:cc + 1], None, ALU.mult))
            s, f = RC.take()
            P(lambda: nc.tensor.matmul(s.ap[:, 0:64], bda[:, gb, c].rearrange("p h s -> p (h s)"), ST[:, i, :],
                                       start=True, stop=False), stt, tk, f, sig=False)
            a = P(lambda: nc.tensor.matmul(s.ap[:, 0:64], mka[:, gb, c, :], Vn[:, gb, c, :], start=False, stop=True))
            e = V(lambda: nc.vector.tensor_copy(zu[:, 0, :], s.ap[:, 0:64]), a)
            s.free = [e]
            yo = ys_.ap[:, 64 * c:64 * c + 64]
            P(lambda: nc.tensor.matmul(yo, bdr[:, gb, c].rearrange("p h s -> p (h s)"), ST[:, i, :], start=True,
                                       stop=False), yf, sig=False)
            P(lambda: nc.tensor.matmul(yo, mkr[:, gb, c, :], Vn[:, gb, c, :], start=False, stop=False), sig=False)
            yield
            s, f = RC.take()
            a = P(lambda: nc.tensor.matmul(s.ap[:, 0:64], XT[:, gb, c, :], zu[:, 0, :], start=True, stop=True), e, f)
            e = V(lambda: nc.vector.tensor_copy(zu[:, 1, :], s.ap[:, 0:64]), a)
            s.free = [e]
            yield
            s, f = RC.take()
            P(lambda: nc.tensor.matmul(s.ap[:, 0:64], Kn[:, gb, c, :], Vn[:, gb, c, :], start=True, stop=False), f,
              sig=False)
            a = P(lambda: nc.tensor.matmul(s.ap[:, 0:64], Bn[:, gb, c, :], zu[:, 1, :], start=False, stop=True), e)
            state["st"] = V(lambda: nc.vector.scalar_tensor_tensor(ST[:, j, :], s.ap[:, 0:64], pc[:, b, cc:cc + 1],
                                                                   zu[:, 2, :], ALU.mult, ALU.add), a, state["y"])
            s.free = [state["st"]]
            state["y"] = P(lambda: nc.tensor.matmul(yo, mbr[:, gb, c, :], zu[:, 1, :], start=False, stop=True), e)
            state["gn"] += 1
            V.wait(state["y"]) if False else None
            yield
        e = S(lambda: nc.scalar.activation(Y[:, 4 * g:4 * g + 4, :].rearrange("p c v -> p (c v)"),
                                           ys_.ap[:, 0:256], ACT.Copy), state["y"], state.get("yfree"))
        ys_.free = [e]
        state["gfree"][gb] = [state["y"]]
        state["yev"] = e

    def finish(p):
        b = p % 2
        gate, fin = Kc[:, b, :], Bc[:, b, :]
        pf1 = state[("pf1", p)]
        out = []
        yield from unit_steps(K, W, xT, xtok, RU, out)
        pair, a = out[0]
        gt = evac(pair, a, gate, ACT.Silu, 1.0, 0.0, pf1)
        yield
        s16, q16 = ys[:, 0:16], ys[:, 16:32]
        bc = lambda x: x.unsqueeze(2).to_broadcast([128, 16, 64])
        V(lambda: nc.vector.tensor_reduce(s16, Y[:, :, :], AX.X, ALU.add), state["yev"])
        V(lambda: nc.vector.tensor_scalar(s16, s16, 1.0 / 64, None, ALU.mult))
        t = V(lambda: nc.vector.tensor_tensor(Y[:, :, :], Y[:, :, :], bc(s16), ALU.subtract))
        y1 = Y[:, :, :].rearrange("p c v -> p (c v)")
        t = S(lambda: nc.scalar.activation(fin[:, :], y1, ACT.Square), t, pf1)
        V(lambda: nc.vector.tensor_reduce(q16, fin[:, :].rearrange("p (c v) -> p c v", v=64), AX.X, ALU.add), t)
        t = V(lambda: nc.vector.tensor_scalar(q16, q16, 1.0 / 64, 64e-5, ALU.mult, ALU.add))
        t = S(lambda: nc.scalar.activation(q16, q16, ACT.Sqrt), t)
        V(lambda: nc.vector.reciprocal(q16, q16), t)
        yield
        for half in range(2):
            for h in range(2):
                rr = slice(64 * h, 64 * h + 64)
                yt = V(lambda: nc.vector.tensor_tensor(
                    ybd[rr, :, h, :], Y[rr, 8 * half:8 * half + 8, :],
                    q16[rr, 8 * half:8 * half + 8].unsqueeze(2).to_broadcast([64, 8, 64]), ALU.mult),
                    state.get("ybdf"))
            if half == 1:
                state["yfree"] = yt
            s, f = RU.take()
            for c in range(8):
                a = P(lambda: nc.tensor.matmul(s.ap[:, 64 * c:64 * c + 64],
                                               ybd[:, c].rearrange("p h v -> p (h v)"), C.stack, start=True,
                                               stop=True), yt, f, sig=(c == 7))
            state["ybdf"] = a
            sl = slice(512 * half, 512 * half + 512)
            e = S(lambda: nc.scalar.activation(fin[:, sl], s.ap, ACT.Identity, scale=lnw[:, p:p + 1],
                                               bias=lnb[:, p:p + 1]), a, V.last())
            s.free = [e]
            yield
            V(lambda: nc.vector.tensor_tensor(fin[:, sl], fin[:, sl], bon[:, b, sl], ALU.add), e)
            e = V(lambda: nc.vector.tensor_tensor(fin[:, sl], fin[:, sl], gate[:, sl], ALU.mult), gt)
        d = K.dma(A["mix"][p], fin[:, :], e, sem=fsem[b])
        K.stored(d)
        state["pairfree"][b] = pf1 + [e, d]

    fsem = [[*K.sem("fin"), 0] for _ in range(2)]
    run(prep_lo())
    run(prep(0))
    yield_after = None
    NP = 8
    pre = fnsh = None
    for n in range(4 * NP + 1):
        p, g = divmod(n, 4)
        gens = []
        if n > 0:
            gens.append(chain((n - 1) // 4, (n - 1) % 4, n - 1))
        if n < 4 * NP:
            if g == 0:
                pre = None
            if g == 1:
                fl = []
                if p > 0:
                    fl.append(finish(p - 1))
                if p + 1 < NP:
                    fl.append(prep(p + 1))
                pre = (x for y in fl for x in y)
            gens.append(stage(p, g, n))
            if pre is not None:
                gens.append(steps(pre, 1000 if g == 3 else 18))
        weave(*gens)
        if g == 3:
            state[("pf1", p)] = state["pf1"]
    run(finish(NP - 1))


def attention(K, C, W, xT, xtok, A, banks, st):
    nc, P, V, S, G = K.nc, K.P, K.V, K.S, K.G
    RU, RS, RT, RO = Ring(banks[0:2]), Ring(banks[2:4]), Ring(banks[4:6]), Ring(banks[6:8])
    sb = lambda n, s, d=F32: K.sb(st, n, s, d)
    qkvg = sb("qkvg", [128, 2, 4, 1024])
    Vc = sb("Vc", [128, 24, 128])
    Pm = sb("Pm", [128, 2, 512])
    PT = sb("PT", [128, 2, 512])
    O = sb("O", [128, 3, 1024])
    MB = sb("MB", [128, 3, 1024])
    LB = sb("LB", [128, 3, 1024])
    ml = sb("ml", [128, 2, 3, 2, 8])
    state = {"fr": [None, None], "pm": [None, None], "pt": [None, None], "n": 0, "ml": None, "vc": None, "xm": [None, None]}
    fsem = [*K.sem("fa"), 0]

    def prep(p):
        b = p % 2
        for i in range(4):
            out = []
            yield from unit_steps(K, W, xT, xtok, RU, out)
            pair, a = out[0]
            for h in range(2):
                e = S(lambda: nc.scalar.activation(qkvg[:, b, i, 512 * h:512 * h + 512], pair[h].ap,
                                                   ACT.Silu if i == 3 else ACT.Copy,
                                                   scale=0.125 if i == 0 else 1.0), a, state["fr"][b])
                pair[h].free = [e]
            yield
        state[("p", p)] = e

    def view(x, pi):
        if pi == 0:
            return x.rearrange("p (c i) -> p c i", i=128)
        if pi == 1:
            return x.rearrange("p (j r) -> p r j", r=4)
        return x.rearrange("p (j r) -> p r j", r=16)

    def cell(x, pi, c, two=False):
        if pi == 0:
            return x[:, 128 * (c - 1) if two else 128 * c:128 * c + 128]
        if pi == 1:
            v = x.rearrange("p (j r) -> p r j", r=4)
            return v[:, c // 2, 0:256] if two else v[:, c // 2, 128 * (c % 2):128 * (c % 2) + 128]
        v = x.rearrange("p (j r) -> p r j", r=16)
        return v[:, 2 * c:2 * c + 2, :]

    def scell(x, x3, pi, c):
        return x3[:, 128 * c:128 * c + 128] if pi == 2 else cell(x, pi, c)

    def group(x, pi, g):
        if pi == 0:
            return x[:, 512 * g:512 * g + 512], None
        r = 4 if pi == 1 else 16
        n = 2 if pi == 1 else 8
        return x.rearrange("p (j r) -> p r j", r=r)[:, n * g:n * g + n, :], n

    def scat(dst, src, pi, g, eng, *toks):
        d, n = group(dst, pi, g)
        s = src if n is None else src.rearrange("p (r j) -> p r j", r=n)
        if eng is S:
            return S(lambda: nc.scalar.activation(d, s, ACT.Copy), *toks)
        return V(lambda: nc.vector.tensor_copy(d, s), *toks)

    def attn(p):
        b = p % 2
        pt = state[("p", p)]
        q, k, v, g = [qkvg[:, b, i, :] for i in range(4)]
        q3, v3 = QV[:, 0, :], QV[:, 1, :]
        G(lambda: nc.gpsimd.tensor_copy(v3.rearrange("p (r j) -> p r j", r=16),
                                        v.rearrange("p (j r) -> p r j", r=16)), pt, state["vc"])
        g3 = G(lambda: nc.gpsimd.tensor_copy(q3.rearrange("p (r j) -> p r j", r=16),
                                             q.rearrange("p (j r) -> p r j", r=16)))
        for pi in range(3):
            for gg in range(2):
                s, f = RT.take()
                for j in range(4):
                    a = P(lambda: nc.tensor.transpose(s.ap[:, 128 * j:128 * j + 128], scell(v, v3, pi, 4 * gg + j),
                                                      C.ident), pt, g3 if pi == 2 else None, f, sig=(j == 3))
                i0 = 8 * pi + 4 * gg
                vc = S(lambda: nc.scalar.activation(Vc[:, i0:i0 + 4, :].rearrange("p c d -> p (c d)"), s.ap,
                                                    ACT.Copy), a, state["vc"])
                s.free = [vc]
                yield
        for pi in range(3):
            for gg in range(2):
                ob, of = RO.take()
                for h in range(2):
                    rr = slice(64 * h, 64 * h + 64)
                    per = 2 if pi < 2 else 4
                    for c0 in range(4 * gg, 4 * gg + 4, per):
                        n = state["n"]
                        state["n"] += 1
                        bb = n % 2
                        s, f = RS.take()
                        w = 512 // per
                        parts = []
                        for j in range(per):
                            c = c0 + j
                            prev = (pi == 0 and c > 0) or (pi == 1 and c % 2 == 1)
                            parts.append((c, prev))
                            m = C.m3 if pi == 2 else (C.m2 if prev else C.m1)
                            P(lambda: nc.tensor.matmul(s.ap[:, w * j:w * j + w], C.identb, m, start=True, stop=False,
                                                       skip_group_check=True), f, pt, sig=False)
                            o = s.ap[:, w * j:w * j + w] if (prev or pi == 2) else s.ap[:, w * j + 128:w * j + 256]
                            a = P(lambda: nc.tensor.matmul(o, scell(q[rr], q3[rr], pi, c), cell(k[rr], pi, c, prev),
                                                           start=False, stop=True, skip_group_check=True),
                                  sig=(j == per - 1))
                        nm = ml[:, 0, pi, h, c0:c0 + per]
                        t = V(lambda: nc.vector.tensor_reduce(nm, s.ap.rearrange("p (j w) -> p j w", j=per), AX.X,
                                                              ALU.max, negate=True), a, state["ml"])
                        for j, (c, prev) in enumerate(parts):
                            lo = w * j if (prev or pi == 2) else w * j + 128
                            e = S(lambda: nc.scalar.activation(Pm[:, bb, lo:w * j + w], s.ap[:, lo:w * j + w],
                                                               ACT.Exp, bias=ml[:, 0, pi, h, c:c + 1],
                                                               accum_out=ml[:, 1, pi, h, c:c + 1]), t,
                                  state["pm"][bb])
                        s.free = [e]
                        yield
                        s, f = RT.take()
                        blocks = []
                        for j, (c, prev) in enumerate(parts):
                            for lo in ((w * j, w * j + 128) if prev else (w * j + w - 128,)):
                                blocks.append((lo, c, prev and lo == w * j))
                        for x, (lo, c, isp) in enumerate(blocks):
                            a = P(lambda: nc.tensor.transpose(s.ap[:, 128 * x:128 * x + 128], Pm[:, bb, lo:lo + 128],
                                                              C.ident), e, f, sig=(x == len(blocks) - 1))
                        state["pm"][bb] = a
                        nb = len(blocks)
                        e = V(lambda: nc.vector.tensor_copy(PT[:, bb, 0:128 * nb], s.ap[:, 0:128 * nb]), a,
                              state["pt"][bb])
                        s.free = [e]
                        yield
                        for x, (lo, c, isp) in enumerate(blocks):
                            ci = 8 * pi + (c - 1 if isp else c)
                            first = x == 0 or blocks[x - 1][1] != c
                            last = x == nb - 1 or blocks[x + 1][1] != c
                            a = P(lambda: nc.tensor.matmul(ob.ap[rr, 128 * (c % 4):128 * (c % 4) + 128],
                                                           Vc[:, ci, rr], PT[:, bb, 128 * x:128 * x + 128],
                                                           start=first, stop=last), e, vc, of, sig=(x == nb - 1))
                        state["pt"][bb] = a
                        yield
                ob.free = [scat(O[:, pi, :], ob.ap, pi, gg, S, a, state.get("Of"))]
        ot = ob.free[0]
        state["vc"] = a
        mlt = [S.last(), V.last()]
        for x, dst in ((0, MB), (1, LB)):
            for pi in range(3):
                xs = (3 * x + pi) % 2
                for h in range(2):
                    et = G(lambda: nc.gpsimd.tensor_copy(XM[:, xs, :, h, :], ml[:, x, pi, h, :].unsqueeze(2)
                                                         .to_broadcast([128, 8, 64])), mlt, state["xm"][xs])
                for gg in range(2):
                    s, f = RT.take()
                    for j in range(4):
                        c = 4 * gg + j
                        a = P(lambda: nc.tensor.transpose(s.ap[:, 128 * j:128 * j + 128],
                                                          XM[:, xs, c].rearrange("p h v -> p (h v)"), C.ident),
                              et, f, sig=(j == 3))
                    state["xm"][xs] = a
                    e = scat(dst[:, pi, :], s.ap, pi, gg, S, a, state.get("mf"))
                    s.free = [e]
                    yield
        state["ml"] = et
        S.wait(et)
        mt = e
        tt = lambda o, x, y, op, *tk: V(lambda: nc.vector.tensor_tensor(o, x, y, op), *tk)
        mn, den, acc = D[:, 0, :], D[:, 1, :], D[:, 2, :]
        tt(mn, MB[:, 0, :], MB[:, 1, :], ALU.min, mt, ot, state.get("Df"))
        tt(mn, mn, MB[:, 2, :], ALU.min)
        for pi in range(3):
            t = tt(MB[:, pi, :], mn, MB[:, pi, :], ALU.subtract)
            t = S(lambda: nc.scalar.activation(MB[:, pi, :], MB[:, pi, :], ACT.Exp), t)
            tt(LB[:, pi, :], LB[:, pi, :], MB[:, pi, :], ALU.mult, t)
            tt(O[:, pi, :], O[:, pi, :], MB[:, pi, :], ALU.mult)
            if pi == 1:
                tt(den, LB[:, 0, :], LB[:, 1, :], ALU.add)
                tt(acc, O[:, 0, :], O[:, 1, :], ALU.add)
            elif pi == 2:
                tt(den, den, LB[:, 2, :], ALU.add)
                t = tt(acc, acc, O[:, 2, :], ALU.add)
                state["Of"] = state["mf"] = t
            yield
        V(lambda: nc.vector.reciprocal(den, den))
        tt(den, den, g, ALU.mult)
        e = tt(acc, acc, den, ALU.mult)
        state["fr"][b] = [e, a]
        state["Df"] = K.dma(A["mix"][8 + p], acc, e, sem=fsem)
        K.stored(state["Df"])

    D = sb("Dm", [128, 3, 1024])
    QV = sb("QV", [128, 2, 1024])
    XM = sb("XM", [128, 2, 8, 2, 64])
    run(prep(0))
    for p in range(8):
        if p < 7:
            weave(attn(p), prep(p + 1))
        else:
            run(attn(p))


def block2(K, C, h, htok, xT, A, banks):
    nc = K.nc
    with ExitStack() as st:
        cols = K.sb(st, "cols2", [128, 112])
        ct = K.dma(cols[:, 0:96], A["c2"])
        ring = Ring(banks)
        with ExitStack() as s2:
            nw = K.sb(s2, "nw", [128, 8])
            nt = K.dma(nw[:, :], A["nw2"])
            xtok = rms_T(K, s2, h, [htok, nt], xT, None, nw, 1e-5, C.ident, ring, 0)
            hs = K.dma(A["hs"], h[:, :, :], htok)
            K.stored(hs)
            K.fence()
        K.D.wait(hs)
        for q in (K.P, K.V, K.S, K.G):
            q.wait(hs)
        return xtok


def block2_rest(K, C, hbuf, xT, A, banks):
    nc = K.nc
    with ExitStack() as st:
        cols = K.sb(st, "cols2", [128, 112])
        ct = K.dma(cols[:, 0:96], A["c2"])
        with ExitStack() as s2:
            W = Weights(K, s2, [A["w2u"][i] for i in range(33)])
            rwkv(K, C, W, xT, None, A, banks, s2, cols, ct)
            K.fence()
        K.V.wait(*K.stores.values())
        K.D.wait(*K.stores.values())
        with ExitStack() as s2:
            W = Weights(K, s2, [A["w2u"][33 + i] for i in range(32)])
            attention(K, C, W, xT, None, A, banks, s2)
            K.fence()
        for q in (K.P, K.V, K.S, K.D):
            q.wait(*K.stores.values())


def block2_out(K, C, h, xT, A, banks):
    nc, P, V, S = K.nc, K.P, K.V, K.S
    ring = Ring(banks)
    with ExitStack() as st:
        mix = K.sb(st, "mixs", [128, 16, 1024])
        wo = K.sb(st, "wo2", [128, 16, 512])
        t1 = K.dma(h[:, :, :], A["hs"])
        mts = [K.dma(mix[:, i, :], A["mix"][i]) for i in range(16)]
        wf = None
        for hh in range(2):
            wt = K.dma(wo[:, :, :], A["wo2"][hh], wf)
            for t in range(8):
                s, f = ring.take()
                for k in range(16):
                    a = P(lambda: nc.tensor.matmul(s.ap, mix[:, k, 128 * t:128 * t + 128], wo[:, k, :],
                                                   start=(k == 0), stop=(k == 15)), mts[k], wt, f, sig=(k == 15))
                hs = h[:, t, 512 * hh:512 * hh + 512]
                e = V(lambda: nc.vector.tensor_tensor(hs, hs, s.ap, ALU.add), a, t1)
                s.free = [e]
            wf = a
        K.fence()
    P, V, S = K.P, K.V, K.S
    with ExitStack() as st:
        fw = K.sb(st, "fw", [128, 1024])
        ft = K.dma(fw[:, :], A["fw2"])
        ss = K.sb(st, "ssf", [128, 8])
        sq = K.sb(st, "sqf", [128, 1024])
        for t in range(8):
            a = S(lambda: nc.scalar.activation(sq[:, :], h[:, t, :], ACT.Square, accum_out=ss[:, t:t + 1]), e)
        b = V(lambda: nc.vector.tensor_scalar(ss[:, :], ss[:, :], 1.0 / 1024, 1e-5, ALU.mult, ALU.add), a)
        b = S(lambda: nc.scalar.activation(ss[:, :], ss[:, :], ACT.Sqrt), b)
        V(lambda: nc.vector.reciprocal(ss[:, :], ss[:, :]), b)
        for t in range(8):
            e = V(lambda: nc.vector.scalar_tensor_tensor(h[:, t, :], h[:, t, :], ss[:, t:t + 1], fw[:, :], ALU.mult,
                                                         ALU.mult), ft)
        K.fence()
    return e


class Consts:
    pass


def load_consts(K, ctx, A):
    C = Consts()
    cc = K.sb(ctx, "cc", [128, 768])
    lm = K.sb(ctx, "lm", [128, 7, 128], U32)
    c2 = K.sb(ctx, "c2c", [128, 1344])
    mb = K.sb(ctx, "mb", [128, 768], BF16)
    toks = [K.dma(cc[:, :], A["cc"]), K.dma(lm[:, :, :], A["lm"]), K.dma(c2[:, :], A["c2c"]),
            K.dma(mb[:, :], A["mb"])]
    C.tok = toks
    C.ident, C.ge, C.lt = cc[:, 0:128], cc[:, 128:256], cc[:, 256:384]
    C.bd64, C.bd32 = cc[:, 384:512], cc[:, 512:768]
    C.lmask = lm[:, :, :]
    C.mS, C.mI, C.stack, C.reset64 = c2[:, 0:128], c2[:, 128:256], c2[:, 256:320], c2[:, 320:1344]
    C.identb, C.m2, C.m1, C.m3 = mb[:, 0:128], mb[:, 128:384], mb[:, 384:640], mb[:, 640:768]
    K.fence_sb = cc
    for q in (K.P, K.V, K.S, K.G):
        q.wait(*toks)
    return C


def build_program(nc, A):
    with ExitStack() as ctx:
        K = Kern(nc, ctx)
        ps = ctx.enter_context(nc.psum_tensor("ps", [128, 8, 512], F32))
        K.fence_ps = ps[:, 7, :]
        banks = [ps[:, i, :] for i in range(8)]
        C = load_consts(K, ctx, A)
        with ExitStack() as s0:
            xT = K.sb(s0, "xT", [128, 8, 1024])
            t = K.dma(xT[:, :, :], A["xT"])
            with ExitStack() as s1:
                h = K.sb(s1, "h", [128, 8, 1024])
                e = block1(K, C, h, xT, t, A, banks)
                block2(K, C, h, None, xT, A, banks)
            block2_rest(K, C, None, xT, A, banks)
        h = K.sb(ctx, "h", [128, 8, 1024])
        block2_out(K, C, h, None, A, banks)
        xT = K.sb(ctx, "xT", [128, 8, 1024])
        block3(K, C, h, None, xT, None, A, banks)
        K.D.wait(*K.stores.values())



def bc(v):
    return np.ascontiguousarray(np.broadcast_to(v.reshape(1, -1), (128, v.size)))


def units(blocks):
    w = np.concatenate(blocks, axis=1)
    n = w.shape[1] // 128
    return np.ascontiguousarray(w.reshape(8, 128, n, 128).transpose(2, 1, 0, 3).reshape(n, 128, 1024))


def col(v):
    return np.ascontiguousarray(v.reshape(-1, 128).T)


def zeros(*shape):
    return np.zeros(shape, np.float32)


def consts():
    i=np.arange(128)
    A={}
    cc=np.zeros((128,768),np.float32)
    s=i[:,None]; t=i[None]
    cc[:,0:128]=np.eye(128)
    cc[:,128:256]=(t>=s)
    cc[:,256:384]=(t<s)
    cc[:,384:512]=(s//64==t//64)
    cc[:,512:768]=(s//32==np.arange(256)[None]//64)
    A["rst"]=bc((np.arange(1024)%128!=0).astype(np.float32)[None])
    A["cc"]=cc
    c2=np.zeros((128,128+128+64+1024),np.float32)
    bdm=(s//64==t//64)
    c2[:,0:128]=bdm&(s<t); c2[:,128:256]=bdm&(s<=t)
    c2[:,256:320]=(s%64==np.arange(64)[None])
    c2[:,320:]=(np.arange(1024)%64!=0)[None]
    A["c2c"]=c2
    
    NEG=-1e30
    mb=np.zeros((128,128+256*2+128),np.float32)
    mb[:,0:128]=np.eye(128)
    q=i[:,None]; k=i[None]
    prev=np.where(k>=q,0,NEG); cur=np.where(k<=q,0,NEG)
    mb[:,128:256]=prev; mb[:,256:384]=cur
    mb[:,384:512]=NEG; mb[:,512:640]=cur
    mb[:,640:768]=np.where((q//64==k//64)&(k<=q),0,NEG)
    A["mb"]=mb.astype(mybir.dt.np(BF16))
    lm=np.zeros((128,7,128),np.uint32)
    for l in range(7):
        B=1<<l
        lm[:,l]=((s//(2*B)==t//(2*B))&(s//B%2==0)&(t//B%2==1))
    A["lm"]=lm
    return A


def host1(I):
    w=I["w_in"][0]; A={}
    c=lambda o,i=0,n=128:w[:,o+128*i:o+128*i+n]
    L=[]
    for p in range(2): L+=[c(0,p),c(256,p),c(512,p),c(768,p)]
    for p in range(2): L+=[c(1024,p),c(1536,p),c(1280,p),c(1792,p)]
    L+=[c(2048),c(2176),c(2304),c(2304,1),c(2560),c(2560,1),np.concatenate([c(2816,0,16),np.zeros((1024,112),np.float32)],1)]
    A["w1"]=units(L)
    G=units([w[:,2832+1024*b+128*d:2832+1024*b+128*d+128] for d in range(8) for b in range(3)])
    up=I["w_up"][0]
    U=np.stack([up[b].reshape(2,128,8,128)[:,:,d,:].transpose(1,0,2).reshape(128,256) for d in range(8) for b in range(3)])
    A["wg"]=np.ascontiguousarray(np.concatenate([G,U],2))
    A["c1"]=np.ascontiguousarray(np.concatenate([col(I["hgrn_norm_g"][0]),col(I["gla_norm_g"][0]),col(I["gla_gate_b"][0]),col(I["hgrn_lb_logits"][0]),np.zeros((128,9),np.float32)],1))
    A["w2"]=I["gla_gate_w2"][0]
    A["wo1"]=np.ascontiguousarray(I["w_out"][0].reshape(8,128,1024).transpose(1,0,2))
    A["rows1"]=np.ascontiguousarray(np.stack([bc(I["ln_g"][0][None]),bc(I["ln_b"][0][None])],1))
    return A


def host2(I):
    g=lambda n:I[n+"_2"]
    w=g("w_in"); c=lambda o,i=0:w[:,o+128*i:o+128*i+128]
    L=[c(3072)]
    rk=lambda p:[c(0,p),c(1024,p),c(2048,p)]
    G0=3200; A0=4224; AG=7296
    L+=rk(0)
    for p in range(1,8): L+=([c(G0,p-2)] if p>1 else [])+rk(p)
    L+=[c(G0,6),c(G0,7)]
    for p in range(8): L+=[c(A0,p),c(A0+1024,p),c(A0+2048,p),c(AG,p)]
    A={}
    A["w2u"]=units(L)
    mu=g("mu_shift")
    A["c2"]=np.ascontiguousarray(np.concatenate([np.zeros((128,8),np.float32)]+[col(g(n)) for n in ("w0","a0","k_k","k_a")]+[col(g("r_k").reshape(-1)),col(g("ln_x_w")),col(g("ln_x_b")),col(mu[:3072]),col(mu[3072:]),np.zeros((128,7),np.float32)],1))
    A["wup2"]=np.ascontiguousarray(np.concatenate([g("w_up"),g("a_up")],0))
    A["nw2"]=col(g("norm_w"))
    A["wo2"]=np.ascontiguousarray(g("w_out").reshape(16,128,2,512).transpose(2,1,0,3))
    A["fw2"]=bc(g("final_norm_w")[None])
    return A


def host3(I):
    w=I["w_in_3"][0]; o=[]
    v=w[:,512:1024]; u=w[:,:512]; g=w[:,1024:1536]; z=w[:,1536:2048]; gb=w[:,2048:]
    c=lambda a,i:a[:,128*i:128*i+128]
    cols=[c(v,i) for i in range(4)]
    for i in range(4): cols+=[c(u,i),c(g,i)]
    for i in range(4): cols+=[c(z,i),c(gb,i)]
    A={}
    A["w3"]=units(cols)
    A["c3"]=np.ascontiguousarray(np.concatenate([I["pre_g_3"][0].reshape(8,128).T, I["b_f_3"][0].T, np.zeros((128,4),np.float32)],1))
    p=np.arange(128)[:,None]; uu=np.arange(128)[None]
    d=np.zeros((128,8,2,128))
    for vv in range(8):
        th=2*np.pi*(((8*uu+vv)*p)%1024)/1024
        d[:,vv,0]=np.cos(th);d[:,vv,1]=np.sin(th)
    A["d3"]=d.reshape(128,2048).astype(np.float32)
    A["rows3"]=np.stack([bc(I["ln_g_3"][0][None]),bc(I["ln_b_3"][0][None]),bc(I["b_s_3"][0].reshape(1,512))])
    A["ws3"]=np.ascontiguousarray(I["w_s_3"][0].transpose(2,0,1).reshape(128,512))
    th=2*np.pi*((p*uu)%128)/128
    s=1/np.sqrt(1024*128)
    A["cd"]=np.concatenate([np.cos(th)*s,-np.sin(th)*s],1).astype(np.float32)
    A["wf3"]=np.ascontiguousarray(I["w_f_3"][0].transpose(1,0,2).reshape(128,512))
    A["wo3"]=np.ascontiguousarray(I["w_out_3"][0].reshape(8,128,1024).transpose(1,0,2))
    A["post3"]=bc(I["post_g_3"][0][None])
    return A



def kernel(**inputs):
    import concourse.bacc as bacc
    from concourse.bass_utils import run_bass_kernel_spmd

    I = {k: np.asarray(v) for k, v in inputs.items()}
    A = consts()
    A.update(host1(I))
    A.update(host2(I))
    A.update(host3(I))
    x = I["x"][0]
    A["x"] = np.ascontiguousarray(x.reshape(8, 128, 1024).transpose(1, 0, 2))
    A["xT"] = np.ascontiguousarray(x.T.reshape(8, 128, 1024).transpose(1, 0, 2))
    nc = bacc.Bacc("TRN2", target_bir_lowering=False, num_devices=1)
    aps, arrays = {}, {}
    for n, a in A.items():
        arrays["in_" + n] = a
        aps[n] = nc.dram_tensor("in_" + n, a.shape, mybir.dt.from_np(a.dtype), kind="ExternalInput").ap()
    aps["out"] = nc.dram_tensor("out_0", (8, 128, 1024), F32, kind="ExternalOutput").ap()
    aps["hs"] = nc.dram_tensor("hs", (128, 8, 1024), F32, kind="Internal").ap()
    aps["mix"] = nc.dram_tensor("mix", (16, 128, 1024), F32, kind="Internal").ap()
    build_program(nc, aps)
    r = run_bass_kernel_spmd(nc, [arrays], core_ids=[0])
    return r.results[0]["out_0"].reshape(1, 1024, 1024)
```

```python
import numpy as np
from contextlib import ExitStack
import concourse.bass as bass
from concourse import mybir

F32 = mybir.dt.float32
BF16 = mybir.dt.bfloat16
U8 = mybir.dt.uint8
ALU = mybir.AluOpType
ACT = mybir.ActivationFunctionType
AX = mybir.AxisListType


class Queue:

    def __init__(self, eng, sem, name, linked):
        self.eng, self.sem, self.name, self.linked = eng, sem, name, linked
        self.n = 0
        self.seen = {}

    def wait(self, *tokens):
        for t in tokens:
            if t is None:
                continue
            if isinstance(t, list):
                self.wait(*t)
                continue
            sem, name, value = t
            if self.seen.get(name, 0) < value:
                self.seen[name] = value
                self.eng.wait_ge(sem, value)

    def last(self):
        return (self.sem, self.name, self.n) if self.n else None

    def __call__(self, make, *tokens, sig=True):
        self.wait(*tokens)
        if self.linked:
            self.wait(self.last())
        ins = make()
        if sig:
            self.n += 1
            ins.then_inc(self.sem, 1)
            return (self.sem, self.name, self.n)
        return None


class Slot:

    def __init__(self, ap):
        self.ap = ap
        self.free = []


class Ring:
    def __init__(self, aps):
        self.slots = [Slot(a) for a in aps]
        self.n = 0

    def take(self):
        s = self.slots[self.n % len(self.slots)]
        self.n += 1
        f, s.free = s.free, []
        return s, f


class Kern:
    def __init__(self, nc, ctx):
        self.nc, self.ctx = nc, ctx
        self.nsem = 0
        self.names = 0
        self.dsem = []
        self.stores = {}
        self.phase()

    def sem(self, name):
        self.nsem += 1
        n = f"{name}_{self.nsem}"
        return self.ctx.enter_context(self.nc.semaphore(n)), n

    def phase(self):
        nc = self.nc
        self.P = Queue(nc.tensor, *self.sem("pe"), False)
        self.V = Queue(nc.vector, *self.sem("dve"), True)
        self.S = Queue(nc.scalar, *self.sem("act"), True)
        self.G = Queue(nc.gpsimd, *self.sem("pool"), True)
        self.D = Queue(nc.sync, *self.sem("sp"), False)

    def fence(self):
        qs = [self.P, self.V, self.S, self.G]
        self.P(lambda: self.nc.tensor.matmul(
            self.fence_ps[0:1, 0:1], self.fence_sb[0:1, 0:1], self.fence_sb[0:1, 0:1], start=True, stop=True),
            self.V.last(), self.S.last())
        toks = [q.last() for q in qs]
        for q in qs + [self.D]:
            q.wait(*toks)
        self.phase()

    def stored(self, token):
        self.stores[token[1]] = token

    def sb(self, stack, name, shape, dt=F32):
        self.names += 1
        return stack.enter_context(self.nc.sbuf_tensor(f"{name}_{self.names}", shape, dt))

    def dma(self, dst, src, *tokens, q=None, sem=None):
        q = q or self.D
        q.wait(*tokens)
        if sem is None:
            s, n = self.sem("dma")
            sem = [s, n, 0]
        sem[2] += 16
        q.eng.dma_start(dst, src).then_inc(sem[0], 16)
        return (sem[0], sem[1], sem[2])


class Weights:

    def __init__(self, K, stack, units, depth=3, width=1024):
        self.K, self.units, self.depth = K, units, depth
        self.buf = K.sb(stack, "wring", [128, depth, width])
        self.sems = [[*K.sem("w"), 0] for _ in range(depth)]
        self.rel = [None] * depth
        self.issued = 0
        self.n = 0
        self.tok = {}

    def pump(self):
        while self.issued < min(len(self.units), self.n + self.depth):
            i = self.issued
            s = i % self.depth
            self.tok[i] = self.K.dma(self.buf[:, s, :], self.units[i], self.rel[s], sem=self.sems[s])
            self.issued += 1

    def get(self):
        self.pump()
        i = self.n
        return self.buf[:, i % self.depth, :].rearrange("p (k c) -> p k c", c=128), self.tok[i]

    def done(self, token):
        self.rel[self.n % self.depth] = token
        self.n += 1
        self.pump()




def unit_T(K, W, xT, xtok, pair, free):
    w, tok = W.get()
    for k in range(8):
        for h in range(2):
            t = K.P(lambda: K.nc.tensor.matmul(pair[h], w[:, k, :], xT[:, k, 512 * h:512 * h + 512],
                                               start=(k == 0), stop=(k == 7)),
                    tok, xtok, free, sig=(k == 7 and h == 1))
    W.done(t)
    return t


def rms_T(K, stack, h, htok, xT, xfree, gain, eps, ident, banks, off):
    nc, V, S, P = K.nc, K.V, K.S, K.P
    sq = K.sb(stack, "sq", [128, 1024])
    ss = K.sb(stack, "ss", [128, 8])
    xn = K.sb(stack, "xn", [128, 4, 1024])
    for t in range(8):
        a = S(lambda: nc.scalar.activation(sq[:, :], h[:, t, :], ACT.Square, accum_out=ss[:, t:t + 1]), htok)
    b = V(lambda: nc.vector.tensor_scalar(ss[:, :], ss[:, :], 1.0 / 1024, eps, ALU.mult, ALU.add), a)
    b = S(lambda: nc.scalar.activation(ss[:, :], ss[:, :], ACT.Sqrt), b)
    r = V(lambda: nc.vector.reciprocal(ss[:, :], ss[:, :]), b)
    out = None
    tp = None
    for half in range(2):
        for j in range(4):
            t = 4 * half + j
            nt = V(lambda: nc.vector.tensor_scalar(xn[:, j, :], h[:, t, :], ss[:, t:t + 1], None, ALU.mult),
                   r, tp)
        for k in range(8):
            s, f = banks.take()
            for j in range(4):
                tp = P(lambda: nc.tensor.transpose(s.ap[:, 128 * j:128 * j + 128],
                                                   xn[:, j, 128 * k:128 * k + 128], ident), nt, f, sig=(j == 3))
            out = S(lambda: nc.scalar.activation(xT[:, k, 512 * half:512 * half + 512], s.ap, ACT.Copy,
                                                 scale=gain[:, k:k + 1]), tp, xfree)
            s.free = [out]
    return out


def block3(K, C, h, htok, xT, xfree, A, banksets):
    nc, P, V, S = K.nc, K.P, K.V, K.S
    allbanks = banksets
    with ExitStack() as st:
        ident = C.ident
        cols = K.sb(st, "cols", [128, 8 + 4 + 4])
        ct = K.dma(cols[:, :], A["c3"])
        g8 = cols[:, 0:8]
        bf = cols[:, 8:12]
        ring = Ring(allbanks)
        with ExitStack() as s2:
            xtok = rms_T(K, s2, h, [htok, ct], xT, xfree, g8, 1e-6, ident, ring, 0)
        mixT = K.sb(st, "mixT", [128, 8, 1024])
        u = K.sb(st, "ua", [128, 2, 1024])
        vn = K.sb(st, "vn", [128, 8, 512])
        W = Weights(K, st, [A["w3"][i] for i in range(20)])
        stat = K.sb(st, "stat", [128, 8, 8])
        cmat = K.sb(st, "cmat", [128, 4096])
        t_c = K.dma(cmat[:, 0:2048], A["d3"][:, 0:2048])
        dft = cmat[:, 0:2048].rearrange("p (v m u) -> p v m u", v=8, m=2)
        t_g = K.dma(cmat[:, 2048:2048 + 512], A["lng"][:, :].to_broadcast([128, 512]) if False else A["rows3"][0])
        t_g2 = K.dma(cmat[:, 2560:3072], A["rows3"][1])
        t_bs = K.dma(cmat[:, 3072:3584], A["rows3"][2])
        t_ws = K.dma(cmat[:, 3584:4096], A["ws3"])
        lng, lnb, bs = cmat[:, 2048:2560], cmat[:, 2560:3072], cmat[:, 3072:3584]
        ws = cmat[:, 3584:4096].rearrange("p (h q) -> p h q", h=4)
        cd = K.sb(st, "cd", [128, 256])
        t_cd = K.dma(cd[:, :], A["cd"])
        wf = K.sb(st, "wf", [128, 512])
        t_wf = K.dma(wf[:, :], A["wf3"])
        vt = None
        for c in range(4):
            w, tok = W.get()
            for half in range(2):
                s, f = ring.take()
                for j in range(4):
                    t = 4 * half + j
                    for k in range(8):
                        a = P(lambda: nc.tensor.matmul(s.ap[:, 128 * j:128 * j + 128], xT[:, k, 128 * t:128 * t + 128],
                                                       w[:, k, :], start=(k == 0), stop=(k == 7)),
                              tok, xtok, f, sig=(k == 7 and j == 3))
                vt = S(lambda: nc.scalar.activation(
                    vn[:, 4 * half:4 * half + 4, 128 * c:128 * c + 128],
                    s.ap.rearrange("p (j c) -> p j c", j=4), ACT.Gelu), a)
                s.free = [vt]
            W.done(a)
        for t in range(8):
            V(lambda: nc.vector.bn_stats(stat[:, t, 0:6], vn[:, t, :]), vt)
            x = V(lambda: nc.vector.bn_aggr(stat[:, t, 6:8], stat[:, t, 0:6]))
        x = V(lambda: nc.vector.tensor_scalar(stat[:, :, 7], stat[:, :, 7], 1e-6, None, ALU.add))
        x = S(lambda: nc.scalar.activation(stat[:, :, 7], stat[:, :, 7], ACT.Sqrt), x)
        V(lambda: nc.vector.reciprocal(stat[:, :, 7], stat[:, :, 7]), x)
        for t in range(8):
            V(lambda: nc.vector.tensor_scalar(vn[:, t, :], vn[:, t, :], stat[:, t, 6:7], stat[:, t, 7:8],
                                              ALU.subtract, ALU.mult))
            V(lambda: nc.vector.tensor_tensor(vn[:, t, :], vn[:, t, :], lng, ALU.mult), t_g)
            vtok = V(lambda: nc.vector.tensor_tensor(vn[:, t, :], vn[:, t, :], lnb, ALU.add), t_g2)
        ufree = None
        for c in range(4):
            for kind in range(2):
                pair, fr = [], []
                for _ in range(2):
                    s, f = ring.take()
                    pair.append(s)
                    fr += f
                a = unit_T(K, W, xT, xtok, [p.ap for p in pair], fr)
                for hh in range(2):
                    o = u[:, kind, 512 * hh:512 * hh + 512]
                    b = S(lambda: nc.scalar.activation(o, pair[hh].ap, ACT.Gelu if kind == 0 else ACT.Silu), a, ufree)
                    pair[hh].free = [b]
            ug = V(lambda: nc.vector.tensor_tensor(u[:, 0, :], u[:, 0, :], u[:, 1, :], ALU.mult), b)
            for half in range(2):
                s, f = ring.take()
                for j in range(4):
                    t = 4 * half + j
                    a = P(lambda: nc.tensor.matmul(s.ap[:, 128 * j:128 * j + 128], vn[:, t, 128 * c:128 * c + 128],
                                                   ws[:, c, :], start=True, stop=True), vtok, t_ws, f, sig=(j == 3))
                o = mixT[:, c, 512 * half:512 * half + 512]
                bb = bs[:, 128 * c:128 * c + 128].unsqueeze(1).to_broadcast([128, 4, 128])
                b = V(lambda: nc.vector.tensor_tensor(o.rearrange("p (j q) -> p j q", j=4),
                                                      s.ap.rearrange("p (j q) -> p j q", j=4), bb, ALU.add),
                      a, t_bs)
                s.free = [b]
                ufree = V(lambda: nc.vector.tensor_tensor(o, o, u[:, 0, 512 * half:512 * half + 512], ALU.mult))
        zT = K.sb(st, "zT", [128, 1024])
        Z = K.sb(st, "Z", [128, 2, 8, 2, 128])
        Y = K.sb(st, "Y", [128, 8, 2, 128])
        fT = K.sb(st, "fT", [128, 1024])
        r2 = float(np.sqrt(0.5))
        zfree = yfree = ffree = None
        for c in range(4):
            pair, fr = [], []
            for _ in range(2):
                s, f = ring.take()
                pair.append(s)
                fr += f
            a = unit_T(K, W, xT, xtok, [p.ap for p in pair], fr)
            for hh in range(2):
                b = S(lambda: nc.scalar.activation(zT[:, 512 * hh:512 * hh + 512], pair[hh].ap, ACT.Copy), a, zfree)
                pair[hh].free = [b]
            for q in range(4):
                s, f = ring.take()
                for j in range(2):
                    t = 2 * q + j
                    a = P(lambda: nc.tensor.matmul(s.ap[:, 256 * j:256 * j + 256], zT[:, 128 * t:128 * t + 128],
                                                   cd[:, :], start=True, stop=True), b, t_cd, f, sig=(j == 1))
                zz = S(lambda: nc.scalar.activation(Z[:, 0, 2 * q:2 * q + 2, :, :],
                                                    s.ap.rearrange("p (a m c) -> p a m c", a=2, m=2), ACT.Copy),
                       a, yfree)
                s.free = [zz]
            zfree = a
            z0, z1 = Z[:, 0, :, :, :], Z[:, 1, :, :, :]
            V(lambda: nc.vector.tensor_tensor(z1[:, 0:4], z0[:, 0:4], z0[:, 4:8], ALU.add), zz)
            V(lambda: nc.vector.tensor_tensor(z1[:, 4:8], z0[:, 0:4], z0[:, 4:8], ALU.subtract))
            sc = z0[:, 0, :, :]
            V(lambda: nc.vector.tensor_tensor(sc[:, 0], z1[:, 5, 0], z1[:, 5, 1], ALU.add))
            V(lambda: nc.vector.tensor_tensor(sc[:, 1], z1[:, 5, 1], z1[:, 5, 0], ALU.subtract))
            V(lambda: nc.vector.tensor_scalar(z1[:, 5], sc, r2, None, ALU.mult))
            sc = z0[:, 1, :, :]
            V(lambda: nc.vector.tensor_copy(sc[:, 0], z1[:, 6, 1]))
            V(lambda: nc.vector.tensor_scalar(sc[:, 1], z1[:, 6, 0], -1.0, None, ALU.mult))
            V(lambda: nc.vector.tensor_copy(z1[:, 6], sc))
            V(lambda: nc.vector.tensor_tensor(sc[:, 0], z1[:, 7, 1], z1[:, 7, 0], ALU.subtract))
            V(lambda: nc.vector.tensor_tensor(sc[:, 1], z1[:, 7, 1], z1[:, 7, 0], ALU.add))
            V(lambda: nc.vector.tensor_scalar(z1[:, 7, 0], sc[:, 0], r2, None, ALU.mult))
            V(lambda: nc.vector.tensor_scalar(z1[:, 7, 1], sc[:, 1], -r2, None, ALU.mult))
            for hb in (0, 4):
                V(lambda: nc.vector.tensor_tensor(z0[:, hb:hb + 2], z1[:, hb:hb + 2], z1[:, hb + 2:hb + 4], ALU.add))
                V(lambda: nc.vector.tensor_tensor(z0[:, hb + 2:hb + 4], z1[:, hb:hb + 2], z1[:, hb + 2:hb + 4],
                                                  ALU.subtract))
                V(lambda: nc.vector.tensor_copy(z1[:, hb + 3, 0], z0[:, hb + 3, 1]))
                V(lambda: nc.vector.tensor_scalar(z1[:, hb + 3, 1], z0[:, hb + 3, 0], -1.0, None, ALU.mult))
            for hb in (0, 4):
                o = hb // 4
                V(lambda: nc.vector.tensor_tensor(Y[:, o], z0[:, hb], z0[:, hb + 1], ALU.add), yfree)
                V(lambda: nc.vector.tensor_tensor(Y[:, o + 4], z0[:, hb], z0[:, hb + 1], ALU.subtract))
                V(lambda: nc.vector.tensor_tensor(Y[:, o + 2], z0[:, hb + 2], z1[:, hb + 3], ALU.add))
                yt = V(lambda: nc.vector.tensor_tensor(Y[:, o + 6], z0[:, hb + 2], z1[:, hb + 3], ALU.subtract))
            fv = fT[:, :].rearrange("p (u v) -> p v u", v=8)
            for half in range(2):
                s, f = ring.take()
                for j in range(4):
                    v = 4 * half + j
                    for m in range(2):
                        a = P(lambda: nc.tensor.matmul(s.ap[:, 128 * j:128 * j + 128], Y[:, v, m, :], dft[:, v, m, :],
                                                       start=(m == 0), stop=(m == 1)), yt, t_c, f,
                              sig=(j == 3 and m == 1))
                b = V(lambda: nc.vector.tensor_copy(fv[:, 4 * half:4 * half + 4, :],
                                                    s.ap.rearrange("p (v u) -> p v u", v=4)), a, ffree)
                s.free = [b]
            yfree = [a, yt]
            ft = b
            pair, fr = [], []
            for _ in range(2):
                s, f = ring.take()
                pair.append(s)
                fr += f
            a = unit_T(K, W, xT, xtok, [p.ap for p in pair], fr)
            for hh in range(2):
                sg = S(lambda: nc.scalar.activation(u[:, 0, 512 * hh:512 * hh + 512], pair[hh].ap, ACT.Silu),
                       a, ufree)
                pair[hh].free = [sg]
            for hh in range(2):
                s, f = ring.take()
                ffree = P(lambda: nc.tensor.matmul(s.ap, wf[:, 128 * c:128 * c + 128], fT[:, 512 * hh:512 * hh + 512],
                                                   start=True, stop=True), ft, t_wf, f)
                ufree = V(lambda: nc.vector.scalar_tensor_tensor(
                    mixT[:, 4 + c, 512 * hh:512 * hh + 512], s.ap, bf[:, c:c + 1],
                    u[:, 0, 512 * hh:512 * hh + 512], ALU.add, ALU.mult), ffree, sg)
                s.free = [ufree]
        mtok = ufree
        wo = xT
        pe_done = P.last()
        wt = K.dma(xT[:, :, :], A["wo3"], pe_done, V.last(), S.last())
        pg = K.sb(st, "pg", [128, 1024])
        pt = K.dma(pg[:, :], A["post3"])
        ss = K.sb(st, "ss3", [128, 8, 2])
        sq = K.sb(st, "sq3", [128, 512])
        y = Z[:, 0].rearrange("p a m c -> p (a m c)").rearrange("p (s n) -> p s n", s=2)
        yfr = [None, None]
        for t in range(8):
            two = []
            for hh in range(2):
                s, f = ring.take()
                two.append(s)
                for k in range(8):
                    a = P(lambda: nc.tensor.matmul(s.ap, mixT[:, k, 128 * t:128 * t + 128],
                                                   xT[:, k, 512 * hh:512 * hh + 512], start=(k == 0), stop=(k == 7)),
                          mtok, wt, f, sig=(k == 7))
                b = S(lambda: nc.scalar.activation(sq[:, :], s.ap, ACT.Square, accum_out=ss[:, t, hh:hh + 1]), a)
            r = ss[:, t, 0:1]
            b = V(lambda: nc.vector.tensor_tensor(r, r, ss[:, t, 1:2], ALU.add), b)
            b = V(lambda: nc.vector.tensor_scalar(r, r, 1.0 / 1024, 1e-6, ALU.mult, ALU.add))
            b = S(lambda: nc.scalar.activation(r, r, ACT.Sqrt), b)
            b = V(lambda: nc.vector.reciprocal(r, r), b)
            yy = y[:, t % 2, :]
            for hh in range(2):
                b = V(lambda: nc.vector.scalar_tensor_tensor(
                    yy[:, 512 * hh:512 * hh + 512], two[hh].ap, r, pg[:, 512 * hh:512 * hh + 512],
                    ALU.mult, ALU.mult), yfr[t % 2], pt)
                two[hh].free = [b]
            b = V(lambda: nc.vector.tensor_tensor(yy, yy, h[:, t, :], ALU.add))
            yfr[t % 2] = K.dma(A["out"][t], yy, b)
            K.stored(yfr[t % 2])
    return




def take2(ring):
    pair, fr = [], []
    for _ in range(2):
        s, f = ring.take()
        pair.append(s)
        fr += f
    return pair, fr


def rows_unit(K, W, xT, xtok, ring, dst, c):
    nc = K.nc
    w, tok = W.get()
    for half in range(2):
        s, f = ring.take()
        for j in range(4):
            t = 4 * half + j
            for k in range(8):
                a = K.P(lambda: nc.tensor.matmul(s.ap[:, 128 * j:128 * j + 128], xT[:, k, 128 * t:128 * t + 128],
                                                 w[:, k, :], start=(k == 0), stop=(k == 7)),
                        tok, xtok, f, sig=(k == 7 and j == 3))
        vt = K.S(lambda: nc.scalar.activation(
            dst[:, 4 * half:4 * half + 4, 128 * c:128 * c + 128],
            s.ap.rearrange("p (j c) -> p j c", j=4), ACT.Copy), a)
        s.free = [vt]
    W.done(a)
    return vt


def unit_to(K, W, xT, xtok, ring, dst, func, scale=1.0, *tokens):
    pair, fr = take2(ring)
    a = unit_T(K, W, xT, xtok, [p.ap for p in pair], fr)
    for h in range(2):
        b = K.S(lambda: K.nc.scalar.activation(dst[:, 512 * h:512 * h + 512], pair[h].ap, func, scale=scale),
                a, *tokens)
        pair[h].free = [b]
    return b


def stick_breaking(K, st, C, W, xT, xtok, ring, yT, ct):
    nc, P, V, S = K.nc, K.P, K.V, K.S
    q = K.sb(st, "sbq", [128, 1024])
    k = K.sb(st, "sbk", [128, 1024])
    g = K.sb(st, "sbg", [128, 1024])
    vn = K.sb(st, "sbv", [128, 8, 128])
    be = K.sb(st, "be", [128, 2, 1024])
    nb = K.sb(st, "nb", [128, 2, 1024])
    pr = K.sb(st, "pr", [128, 2, 1025])
    wt = K.sb(st, "wt", [128, 2, 1024])
    one = V(lambda: nc.vector.memset(pr[:, :, :], 1.0))
    avr = [None, None]
    tpr = [None, None]
    usedqk = usedv = usedg = None
    oring = Ring([s.ap for s in ring.slots[6:]])
    for s in oring.slots + ring.slots:
        s.free = []
    ring = Ring([s.ap for s in ring.slots[:6]])
    for p in range(2):
        unit_to(K, W, xT, xtok, ring, q, ACT.Copy, 0.125, usedqk)
        qk = unit_to(K, W, xT, xtok, ring, k, ACT.Copy, 1.0, usedqk)
        S.wait(usedv)
        vt = rows_unit(K, W, xT, xtok, ring, vn, 0)
        gt = unit_to(K, W, xT, xtok, ring, g, ACT.Silu, 1.0, usedg)
        steps = [(h, i) for h in range(2) for i in range(8)]
        ob = None
        for n, (h, i) in enumerate(steps):
            b = n % 2
            r = slice(64 * h, 64 * h + 64)
            L = 128 * (i + 1)
            for c0 in range(0, L, 512):
                w = min(512, L - c0)
                s, f = ring.take()
                a = P(lambda: nc.tensor.matmul(s.ap[:, 0:w], q[r, 128 * i:128 * i + 128], k[r, c0:c0 + w],
                                               start=True, stop=True), qk, f)
                S(lambda: nc.scalar.activation(be[:, b, c0:c0 + w], s.ap[:, 0:w], ACT.Sigmoid), a, tpr[b])
                a = S(lambda: nc.scalar.activation(nb[:, b, c0:c0 + w], s.ap[:, 0:w], ACT.Sigmoid, scale=-1.0),
                      tpr[b])
                s.free = [a]
            V(lambda: nc.vector.tensor_tensor(nb[:, b, L - 128:L], nb[:, b, L - 128:L], C.ge, ALU.max), a, ct)
            V(lambda: nc.vector.tensor_tensor(be[:, b, L - 128:L], be[:, b, L - 128:L], C.lt, ALU.mult))
            V(lambda: nc.vector.memset(pr[:, b, L:L + 1], 1.0))
            V(lambda: nc.vector.tensor_tensor_scan(pr[:, b, 0:L][:, ::-1], nb[:, b, 0:L][:, ::-1],
                                                   nb[:, b, 0:L][:, ::-1], 1.0, ALU.mult, ALU.bypass))
            wtok = V(lambda: nc.vector.tensor_tensor(be[:, b, 0:L], be[:, b, 0:L], pr[:, b, 1:L + 1], ALU.mult))
            for c0 in range(0, i + 1, 4):
                m = min(4, i + 1 - c0)
                s, f = ring.take()
                for j in range(m):
                    t = P(lambda: nc.tensor.transpose(s.ap[:, 128 * j:128 * j + 128],
                                                      be[:, b, 128 * (c0 + j):128 * (c0 + j) + 128], C.ident),
                          wtok, f, sig=(j == m - 1))
                ev = V(lambda: nc.vector.tensor_copy(wt[:, b, 128 * c0:128 * (c0 + m)], s.ap[:, 0:128 * m]),
                       t, avr[b])
                s.free = [ev]
            tpr[b] = [t, wtok]
            if i % 4 == 0:
                ob, f = oring.take()
            for j in range(i + 1):
                a = P(lambda: nc.tensor.matmul(ob.ap[r, 128 * (i % 4):128 * (i % 4) + 128],
                                               vn[:, j, 64 * h:64 * h + 64],
                                               wt[:, b, 128 * j:128 * j + 128], start=(j == 0), stop=(j == i)),
                      ev, vt, f, sig=(j == i))
            avr[b] = a
            if i % 4 == 3:
                c0 = 512 * (i // 4)
                e = V(lambda: nc.vector.tensor_tensor(yT[r, p, c0:c0 + 512], ob.ap[r, :], g[r, c0:c0 + 512],
                                                      ALU.mult), a, gt)
                ob.free = [e]
        usedqk = usedv = P.last()
        usedg = e
    return e


def recurrence(K, B, C, ring, nh, dk, q, k, lf, toks, V_n, vcol, vtok, yT, yi, gates, gtok, gain):
    nc, P, V, S = K.nc, K.P, K.V, K.S
    vw = 64 * nh
    E, Xs, acc, Kn, St, on, dec, rs = B.E, B.X, B.acc, B.Kn, B.St, B.on, B.dec, B.rs
    cum = B.cum
    per = 4 // nh
    ct = V(lambda: nc.vector.tensor_tensor_scan(cum, C.reset, lf, 0.0, ALU.mult, ALU.add), toks)
    a4 = acc[:, 0:nh * 1024].rearrange("p (g j s) -> p g j s", j=4, s=128)
    xr = [None, None]
    for lev in range(-1, 7):
        if lev < 0:
            xt = toks
            left, right = k, q
        else:
            b = lev % 2
            X = Xs[:, b, :]
            Bk = 1 << lev
            c3 = cum.rearrange("p (n b) -> p n b", b=2 * Bk)
            m = c3[:, :, Bk - 1:Bk].to_broadcast([128, 1024 // (2 * Bk), 2 * Bk])
            X3 = X.rearrange("p (n b) -> p n b", b=2 * Bk)
            t = V(lambda: nc.vector.tensor_tensor(X3, c3, m, ALU.subtract), xr[b])
            t = S(lambda: nc.scalar.activation(X, X, ACT.Abs), t)
            t = S(lambda: nc.scalar.activation(X, X, ACT.Exp, scale=-1.0), t)
            q3 = q.rearrange("p (n b) -> p n b", b=2 * Bk)
            k3 = k.rearrange("p (n b) -> p n b", b=2 * Bk)
            V(lambda: nc.vector.tensor_tensor(X3[:, :, 0:Bk], X3[:, :, 0:Bk], k3[:, :, 0:Bk], ALU.mult), t)
            xt = V(lambda: nc.vector.tensor_tensor(X3[:, :, Bk:], X3[:, :, Bk:], q3[:, :, Bk:], ALU.mult))
            left = right = X
        for grp in range(2 * nh):
            s, f = ring.take()
            h = grp // 2
            for j in range(4):
                t = 4 * (grp % 2) + j
                r = slice(dk * h, dk * h + dk)
                a = P(lambda: nc.tensor.matmul(s.ap[:, 128 * j:128 * j + 128], left[r, 128 * t:128 * t + 128],
                                               right[r, 128 * t:128 * t + 128], start=True, stop=True,
                                               tile_position=(dk * h, 0)),
                      xt, f, sig=(j == 3))
            dst = a4[:, grp]
            src = s.ap.rearrange("p (j s) -> p j s", s=128)
            if lev < 0:
                im = C.ident.unsqueeze(1).to_broadcast([128, 4, 128])
                e = V(lambda: nc.vector.tensor_tensor(dst, src, im, ALU.mult), a)
            else:
                lm = C.lmask[:, lev, :].unsqueeze(1).to_broadcast([128, 4, 128])
                e = V(lambda: nc.vector.copy_predicated(dst, lm, src), a)
            s.free = [e]
        if lev >= 0:
            xr[b] = a
        yield
    acct = e
    c3 = cum.rearrange("p (n b) -> p n b", b=128)
    last = c3[:, :, 127:128]
    dt = S(lambda: nc.scalar.activation(dec, c3[:, :, 127], ACT.Exp), ct)
    t = V(lambda: nc.vector.tensor_tensor(E.rearrange("p (n b) -> p n b", b=128), last.to_broadcast([128, 8, 128]), c3,
                                          ALU.subtract))
    t = S(lambda: nc.scalar.activation(E, E, ACT.Exp), t)
    kd = V(lambda: nc.vector.tensor_tensor(E, E, k, ALU.mult), t)
    Qc = Xs[:, 0, :]
    t = S(lambda: nc.scalar.activation(Qc, cum, ACT.Exp), xr[0], xr[1])
    qc = V(lambda: nc.vector.tensor_tensor(Qc, Qc, q, ALU.mult), t)
    for half in range(2):
        s, f = ring.take()
        for j in range(4):
            t = 4 * half + j
            a = P(lambda: nc.tensor.transpose(s.ap[:, 128 * j:128 * j + 128], E[:, 128 * t:128 * t + 128], C.ident),
                  kd, f, sig=(j == 3))
        e = S(lambda: nc.scalar.activation(Kn[:, 512 * half:512 * half + 512], s.ap, ACT.Copy), a)
        s.free = [e]
    kn = e
    yield
    bm = C.bd64 if nh == 2 else C.bd32
    tokS = None
    tmp = B.tmp
    for t in range(7):
        s, f = ring.take()
        a = P(lambda: nc.tensor.matmul(s.ap[:, 0:vw], Kn[:, 128 * t:128 * t + 128], V_n[:, t, vcol:vcol + vw],
                                       start=True, stop=True), kn, vtok, f)
        if t == 0:
            tokS = V(lambda: nc.vector.tensor_tensor(St[:, 1, 0:vw], s.ap[:, 0:vw], bm, ALU.mult), a)
        else:
            V(lambda: nc.vector.tensor_tensor(tmp[:, 0:vw], s.ap[:, 0:vw], bm, ALU.mult), a)
            tokS = V(lambda: nc.vector.scalar_tensor_tensor(St[:, t + 1, 0:vw], St[:, t, 0:vw], dec[:, t:t + 1],
                                                            tmp[:, 0:vw], ALU.mult, ALU.add), dt)
        s.free = [tokS]
        yield
    tpb = 512 // vw
    o3 = on[:, 0:8 * vw]
    for grp in range(8 // tpb):
        s, f = ring.take()
        for j in range(tpb):
            t = grp * tpb + j
            if t > 0:
                P(lambda: nc.tensor.matmul(s.ap[:, vw * j:vw * j + vw], Qc[:, 128 * t:128 * t + 128],
                                           St[:, t, 0:vw], start=True, stop=False, skip_group_check=True),
                  qc, tokS, acct, f, sig=False)
            for h in range(nh):
                idx = 8 * h + t
                a = P(lambda: nc.tensor.matmul(s.ap[:, vw * j + 64 * h:vw * j + 64 * h + 64],
                                               acc[:, 128 * idx:128 * idx + 128],
                                               V_n[:, t, vcol + 64 * h:vcol + 64 * h + 64],
                                               start=(t == 0 and h == 0), stop=(h == nh - 1), skip_group_check=True),
                      acct, vtok, qc, f, sig=(j == tpb - 1 and h == nh - 1))
        e = S(lambda: nc.scalar.activation(on[:, 512 * grp:512 * grp + 512], s.ap, ACT.Copy), a, B.onfree)
        s.free = [e]
        yield
    n = 8 * nh
    e2 = S(lambda: nc.scalar.activation(B.sq[:, 0:8 * vw], on[:, 0:8 * vw], ACT.Square), a)
    V(lambda: nc.vector.tensor_reduce(rs[:, 0:n], B.sq[:, 0:8 * vw].rearrange("p (n v) -> p n v", v=64), AX.X,
                                      ALU.add), e2)
    b = V(lambda: nc.vector.tensor_scalar(rs[:, 0:n], rs[:, 0:n], 1.0 / 64, 1e-5, ALU.mult, ALU.add))
    b = S(lambda: nc.scalar.activation(rs[:, 0:n], rs[:, 0:n], ACT.Sqrt), b)
    V(lambda: nc.vector.reciprocal(rs[:, 0:n], rs[:, 0:n]), b)
    ov = o3.rearrange("p (n v) -> p n v", v=64)
    b = V(lambda: nc.vector.tensor_tensor(ov, ov, rs[:, 0:n].unsqueeze(2).to_broadcast([128, n, 64]), ALU.mult))
    for c in range(nh // 2):
        for half in range(2):
            s, f = ring.take()
            for j in range(4):
                t = 4 * half + j
                a = P(lambda: nc.tensor.transpose(s.ap[:, 128 * j:128 * j + 128],
                                                  on[:, vw * t + 128 * c:vw * t + 128 * c + 128], C.ident),
                      b, f, sig=(j == 3))
            e = V(lambda: nc.vector.scalar_tensor_tensor(yT[:, yi + c, 512 * half:512 * half + 512], s.ap,
                                                         gain[:, c:c + 1], gates[:, c, 512 * half:512 * half + 512],
                                                         ALU.mult, ALU.mult), a, gtok)
            s.free = [e]
        yield
    B.onfree = a
    B.done = e


def log_sigmoid(K, B, src, stok, bias, dst, dtok):
    nc, V, S = K.nc, K.V, K.S
    for h in range(2):
        sl = slice(512 * h, 512 * h + 512)
        e = S(lambda: nc.scalar.activation(B.E[:, sl], src[h].ap, ACT.Identity, bias=bias), stok, dtok)
        src[h].free = src[h].free + [e]
    S(lambda: nc.scalar.activation(dst, B.E, ACT.Abs), dtok)
    S(lambda: nc.scalar.activation(dst, dst, ACT.Exp, scale=-1.0))
    e = S(lambda: nc.scalar.activation(dst, dst, ACT.Ln, bias=1.0))
    return V(lambda: nc.vector.scalar_tensor_tensor(dst, B.E, 0.0, dst, ALU.min, ALU.subtract), e)


class Bufs:
    pass


def run(gen):
    for _ in gen:
        pass


def block1(K, C, h, xT, xtok, A, banks):
    nc, P, V, S = K.nc, K.P, K.V, K.S
    ring = Ring(banks)
    with ExitStack() as st:
        cols = K.sb(st, "cols1", [128, 16])
        rst = K.sb(st, "rst", [128, 1024])
        C.reset = rst[:, :]
        V.wait(K.dma(rst[:, :], A["rst"]))
        ct = K.dma(cols[:, :], A["c1"])
        hg, cg, cb, lbl = cols[:, 0:2], cols[:, 2:4], cols[:, 4:5], cols[:, 5:7]
        lb, oml, z1 = cols[:, 7:9], cols[:, 9:11], cols[:, 11:13]
        yT = K.sb(st, "yT", [128, 6, 1024])
        V(lambda: nc.vector.tensor_tensor(z1, lbl, lbl, ALU.subtract), ct)
        t = V.last()
        t = S(lambda: nc.scalar.activation(z1, z1, ACT.Exp), t)
        V(lambda: nc.vector.reciprocal(lb, z1), t)
        V(lambda: nc.vector.tensor_tensor(z1, z1, lb, ALU.mult))
        V(lambda: nc.vector.tensor_tensor(lb, z1, z1, ALU.subtract))
        lbt = V(lambda: nc.vector.tensor_scalar(oml, lb, -1.0, 1.0, ALU.mult, ALU.add))
        with ExitStack() as s2:
            W = Weights(K, s2, [A["w1"][i] for i in range(8 + 8)] + [A["w1"][i] for i in range(16, 23)])
            with ExitStack() as s3:
                stick_breaking(K, s3, C, W, xT, xtok, ring, yT, C.tok)
                K.fence()
                P, V, S = K.P, K.V, K.S
            B = Bufs()
            big = K.sb(s2, "recb", [128, 4, 1024])
            B.cum, B.E = big[:, 0, :], big[:, 1, :]
            B.X = big[:, 2:4, :]
            q = K.sb(s2, "rq", [128, 1024])
            kk = K.sb(s2, "rk", [128, 1024])
            lf = K.sb(s2, "rlf", [128, 1024])
            gts = K.sb(s2, "rg", [128, 2, 1024])
            vn = K.sb(s2, "rvn", [128, 8, 256])
            acc = K.sb(s2, "racc", [128, 4096])
            B.acc = acc
            B.sq = big[:, 2:4, :].rearrange("p a n -> p (a n)")
            B.on = K.sb(s2, "ron", [128, 2048])
            B.St = K.sb(s2, "rst", [128, 8, 256])
            kn = K.sb(s2, "rkn", [128, 1024])
            B.Kn = kn[:, :]
            B.tmp = K.sb(s2, "rtmp", [128, 256])
            sm = K.sb(s2, "rsm", [128, 64])
            B.dec, B.rs = sm[:, 0:8], sm[:, 8:40]
            B.onfree = None
            for p in range(2):
                pair, fr = take2(ring)
                a = unit_T(K, W, xT, xtok, [x.ap for x in pair], fr)
                for hh in range(2):
                    e = S(lambda: nc.scalar.activation(kk[:, 512 * hh:512 * hh + 512], pair[hh].ap, ACT.Sigmoid,
                                                       scale=-1.0), a)
                    pair[hh].free = [e]
                V(lambda: nc.vector.tensor_scalar(kk[:, :], kk[:, :], oml[:, p:p + 1], None, ALU.mult), e, lbt)
                ls = log_sigmoid(K, B, pair, a, 0.0, lf[:, :], None)
                V(lambda: nc.vector.tensor_scalar(B.E, B.E, -1.0, 60.0, ALU.mult, ALU.min))
                t = S(lambda: nc.scalar.activation(B.E, B.E, ACT.Exp), V.last())
                t = V(lambda: nc.vector.tensor_scalar(B.E, B.E, lb[:, p:p + 1], None, ALU.mult), t)
                t = S(lambda: nc.scalar.activation(B.E, B.E, ACT.Ln, bias=1.0), t)
                lft = V(lambda: nc.vector.tensor_tensor(lf[:, :], lf[:, :], B.E, ALU.add), t)
                qt = unit_to(K, W, xT, xtok, ring, q, ACT.Copy)
                vt = rows_unit(K, W, xT, xtok, ring, vn, 0)
                gt = unit_to(K, W, xT, xtok, ring, gts[:, 0, :], ACT.Silu)
                run(recurrence(K, B, C, ring, 2, 64, q[:, :], kk[:, :], lf[:, :], [qt, lft], vn, 0, vt,
                               yT, 2 + p, gts, gt, hg[:, p:p + 1]))
                S.wait(K.P.last(), K.V.last())
                V.wait(K.P.last(), K.S.last())
            unit_to(K, W, xT, xtok, ring, q, ACT.Copy, 32 ** -0.5)
            qt = unit_to(K, W, xT, xtok, ring, kk, ACT.Copy)
            for c in range(2):
                vt = rows_unit(K, W, xT, xtok, ring, vn, c)
            for c in range(2):
                gt = unit_to(K, W, xT, xtok, ring, gts[:, c, :], ACT.Silu)
            w2 = K.sb(s2, "w2", [16, 128])
            w2t = K.dma(w2[:, :], A["w2"])
            cr = K.sb(s2, "cr", [16, 1024])
            w, tok = W.get()
            pair, fr = take2(ring)
            for k in range(8):
                for hh in range(2):
                    a = P(lambda: nc.tensor.matmul(pair[hh].ap[0:16, :], w[:, k, 0:16],
                                                   xT[:, k, 512 * hh:512 * hh + 512], start=(k == 0), stop=(k == 7)),
                          tok, xtok, fr)
            W.done(a)
            for hh in range(2):
                e = S(lambda: nc.scalar.activation(cr[:, 512 * hh:512 * hh + 512], pair[hh].ap[0:16, :], ACT.Copy), a)
                pair[hh].free = [e]
            pair, fr = take2(ring)
            for hh in range(2):
                a = P(lambda: nc.tensor.matmul(pair[hh].ap, w2[:, :], cr[:, 512 * hh:512 * hh + 512], start=True,
                                               stop=True), e, w2t, fr)
            log_sigmoid(K, B, pair, a, cb, lf[:, :], ct)
            lft = V(lambda: nc.vector.tensor_scalar(lf[:, :], lf[:, :], 1.0 / 16, None, ALU.mult))
            run(recurrence(K, B, C, ring, 4, 32, q[:, :], kk[:, :], lf[:, :], [qt, lft], vn, 0, vt,
                           yT, 4, gts, gt, cg))
            K.fence()
            P, V, S = K.P, K.V, K.S
        with ExitStack() as s2:
            W = Weights(K, s2, [A["wg"][i] for i in range(24)], width=1280)
            merged = K.sb(s2, "merged", [128, 8, 1024])
            sg = K.sb(s2, "sg", [128, 2, 1024])
            ht = K.dma(h[:, :, :], A["x"])
            sgf = [None, None]
            n = 0
            for d in range(8):
                for br in range(3):
                    pair, fr = take2(ring)
                    w, tok = W.get()
                    for k in range(8):
                        for hh in range(2):
                            a = P(lambda: nc.tensor.matmul(pair[hh].ap, w[:, k, :], xT[:, k, 512 * hh:512 * hh + 512],
                                                           start=(k == 0), stop=(k == 7)),
                                  tok, xtok, fr, sig=(k == 7))
                    for hh in range(2):
                        e = S(lambda: nc.scalar.activation(sg[:, n % 2, 512 * hh:512 * hh + 512], pair[hh].ap,
                                                           ACT.Sigmoid), a, sgf[n % 2])
                        pair[hh].free = [e]
                    pair, fr = take2(ring)
                    for k in range(2):
                        for hh in range(2):
                            a = P(lambda: nc.tensor.matmul(pair[hh].ap, w[:, 8 + k, :],
                                                           yT[:, 2 * br + k, 512 * hh:512 * hh + 512],
                                                           start=(k == 0), stop=(k == 1)), fr, sig=(k == 1))
                    W.done(a)
                    for hh in range(2):
                        m = merged[:, d, 512 * hh:512 * hh + 512]
                        g = sg[:, n % 2, 512 * hh:512 * hh + 512]
                        t = V(lambda: nc.vector.tensor_tensor(m if br == 0 else g, pair[hh].ap, g, ALU.mult), a, e)
                        pair[hh].free = [t]
                        if br:
                            t = V(lambda: nc.vector.tensor_tensor(m, m, g, ALU.add))
                    sgf[n % 2] = t
                    n += 1
            mt = t
            wo = K.sb(s2, "wo1", [128, 8, 1024])
            wt = K.dma(wo[:, :, :], A["wo1"])
            rows = K.sb(s2, "rows1", [128, 2, 1024])
            rt = K.dma(rows[:, :, :], A["rows1"])
            stt = K.sb(s2, "st1", [128, 8, 14])
            for t in range(8):
                for hh in range(2):
                    s, f = ring.take()
                    for k in range(8):
                        a = P(lambda: nc.tensor.matmul(s.ap, merged[:, k, 128 * t:128 * t + 128],
                                                       wo[:, k, 512 * hh:512 * hh + 512], start=(k == 0), stop=(k == 7)),
                              mt, wt, f, sig=(k == 7))
                    hs = h[:, t, 512 * hh:512 * hh + 512]
                    e = V(lambda: nc.vector.scalar_tensor_tensor(hs, hs, float(2 ** 0.25), s.ap, ALU.mult, ALU.add),
                          a, ht)
                    s.free = [e]
                    V(lambda: nc.vector.bn_stats(stt[:, t, 6 * hh:6 * hh + 6], hs))
                V(lambda: nc.vector.bn_aggr(stt[:, t, 12:14], stt[:, t, 0:12]))
                e = V(lambda: nc.vector.tensor_scalar(stt[:, t, 13:14], stt[:, t, 13:14], 1e-5, None, ALU.add))
                e = S(lambda: nc.scalar.activation(stt[:, t, 13:14], stt[:, t, 13:14], ACT.Sqrt), e)
                V(lambda: nc.vector.reciprocal(stt[:, t, 13:14], stt[:, t, 13:14]), e)
                V(lambda: nc.vector.tensor_scalar(h[:, t, :], h[:, t, :], stt[:, t, 12:13], stt[:, t, 13:14],
                                                  ALU.subtract, ALU.mult))
                V(lambda: nc.vector.tensor_tensor(h[:, t, :], h[:, t, :], rows[:, 0, :], ALU.mult), rt)
                e = V(lambda: nc.vector.tensor_tensor(h[:, t, :], h[:, t, :], rows[:, 1, :], ALU.add))
            K.fence()
    return e



EC = float(np.exp(-0.5))


def weave(*gens):
    live = list(gens)
    while live:
        for g in list(live):
            try:
                next(g)
            except StopIteration:
                live.remove(g)


def steps(gen, n):
    for _ in range(n):
        try:
            next(gen)
        except StopIteration:
            return
        yield


def unit_steps(K, W, xT, xtok, ring, out):
    pair, fr = take2(ring)
    w, tok = W.get()
    for k in range(8):
        for h in range(2):
            t = K.P(lambda: K.nc.tensor.matmul(pair[h].ap, w[:, k, :], xT[:, k, 512 * h:512 * h + 512],
                                               start=(k == 0), stop=(k == 7)),
                    tok, xtok, fr, sig=(k == 7 and h == 1))
        yield
    W.done(t)
    out.append((pair, t))


def rwkv(K, C, W, xT, xtok, A, banks, st, cols, ctok):
    nc, P, V, S, G = K.nc, K.P, K.V, K.S, K.G
    RU, RG, RC, RY = Ring(banks[0:3]), Ring(banks[3:6]), Ring(banks[6:7]), Ring(banks[7:8])
    sb = lambda n, s, d=F32: K.sb(st, n, s, d)
    AR = sb("AR", [128, 2, 16, 2, 64])
    vT = sb("vT", [128, 2, 1024])
    Bc = sb("Bc", [128, 2, 1024])
    Kc = sb("Kc", [128, 2, 1024])
    bon = sb("bon", [128, 3, 1024])
    gf_ = sb("gf", [128, 2, 1024])
    pc = sb("pc", [128, 2, 16])
    raw = sb("raw", [128, 1028])
    r = sb("r", [128, 1024])
    k = sb("k", [128, 1024])
    sg = sb("sg2", [128, 1024])
    cum = sb("cum2", [128, 1024])
    ex = sb("ex", [128, 1024])
    av = sb("av", [128, 1024])
    kk = sb("kk", [128, 1024])
    D = sb("D", [128, 1024])
    lo = sb("lo", [128, 1024])
    wup = sb("wup", [128, 1024])
    MB_ = sb("mb_", [128, 4, 4, 2, 64])
    MK_ = sb("mk_", [128, 4, 4, 2, 64])
    XM_ = sb("X", [128, 2, 2, 4, 64])
    XT = sb("XT", [128, 4, 4, 64])
    Bn, Kn, Vn = sb("Bn", [128, 4, 4, 64]), sb("Kn", [128, 4, 4, 64]), sb("Vn", [128, 4, 4, 64])
    ST = sb("ST", [128, 2, 64])
    zu = sb("zu", [128, 3, 64])
    Y2 = sb("Y", [128, 2, 16, 64])
    ys = sb("ys", [128, 48])
    mu, w0, a0, kkc, kac, rkc, lnw, lnb = [cols[:, 8 * i:8 * i + 8] for i in range(8)]
    mur, muk, muv = cols[:, 64:72], cols[:, 72:80], cols[:, 80:88]
    mulo = cols[:, 88:89]
    omka = cols[:, 96:104]
    for b in (raw,):
        z = V(lambda: nc.vector.memset(b[:], 0.0))
    for q in (S, G, P):
        q.wait(z)
    V(lambda: nc.vector.tensor_scalar(omka, kac, -1.0, 1.0, ALU.mult, ALU.add), ctok)
    wt = K.dma(wup[:, :], A["wup2"])
    state = {"pairfree": [None, None], "gfree": [None] * 4, "s1": [None, None], "raw": None, "y": None, "st": None,
             "gn": 0, "tmpf": None, "fin": None, "yfree": [None, None]}

    def shift(pair, a, mucol, dst, dfree):
        for h in range(2):
            e = S(lambda: nc.scalar.activation(raw[:, 1 + 512 * h:513 + 512 * h], pair[h].ap, ACT.Copy), a,
                  state["raw"])
            pair[h].free = [e]
        V(lambda: nc.vector.tensor_tensor(D[:, :], raw[:, 0:1024], raw[:, 1:1025], ALU.subtract), e, dfree)
        state["raw"] = V(lambda: nc.vector.scalar_tensor_tensor(dst, D[:, :], mucol, raw[:, 1:1025], ALU.mult,
                                                                ALU.add), ctok)
        return state["raw"]

    def prep_lo():
        out = []
        yield from unit_steps(K, W, xT, xtok, RU, out)
        t = shift(*out[0], mulo, lo[:, :], None)
        state["lo"] = S(lambda: nc.scalar.activation(lo[0:64, :], lo[0:64, :], ACT.Tanh), t)

    def both(lhs, rhs, toks):
        pair, fr = take2(RU)
        for h in range(2):
            a = P(lambda: nc.tensor.matmul(pair[h].ap, lhs, rhs[:, 512 * h:512 * h + 512], start=True, stop=True),
                  toks, fr)
        return pair, a

    def evac(pair, a, dst, func, scale=1.0, bias=0.0, *toks):
        for h in range(2):
            if func == ACT.Copy:
                e = S(lambda: nc.scalar.activation(dst[:, 512 * h:512 * h + 512], pair[h].ap, func, scale=scale), a,
                      *toks)
            else:
                e = S(lambda: nc.scalar.activation(dst[:, 512 * h:512 * h + 512], pair[h].ap, func, scale=scale,
                                                   bias=bias), a, *toks)
            pair[h].free = [e]
        return e

    def prep(p):
        b = p % 2
        pf = state[("pf1", p - 2)] if p > 1 else None
        out = []
        yield from unit_steps(K, W, xT, xtok, RU, out)
        rt = shift(*out[-1], mur[:, p:p + 1], r[:, :], None)
        yield
        yield from unit_steps(K, W, xT, xtok, RU, out)
        kt = shift(*out[-1], muk[:, p:p + 1], k[:, :], None)
        yield
        V(lambda: nc.vector.tensor_scalar(kk[:, :], k[:, :], kkc[:, p:p + 1], None, ALU.mult))
        t = S(lambda: nc.scalar.activation(ex[:, :], kk[:, :], ACT.Square), V.last(), state["tmpf"])
        yield from unit_steps(K, W, xT, xtok, RU, out)
        vt = shift(*out[-1], muv[:, p:p + 1], vT[:, b, :], pf)
        yield
        s, f = RU.take()
        for j in range(8):
            a = P(lambda: nc.tensor.matmul(s.ap[:, 2 * j:2 * j + 2], ex[:, 128 * j:128 * j + 128], C.bd64[:, 0:65:64],
                                           start=True, stop=True), t, f, sig=(j == 7))
        n16 = ys[:, 32:48]
        t = S(lambda: nc.scalar.activation(n16, s.ap[:, 0:16], ACT.Sqrt), a)
        s.free = [t]
        V(lambda: nc.vector.tensor_scalar(n16, n16, 1e-12, None, ALU.max), t)
        V(lambda: nc.vector.reciprocal(n16, n16))
        ext = V(lambda: nc.vector.tensor_copy(ex[:, :].rearrange("p (n c) -> p n c", c=64),
                                              n16.unsqueeze(2).to_broadcast([128, 16, 64])), a)
        yield
        cs = slice(128 * p, 128 * p + 128)
        pair, a = both(wup[0:64, cs], lo[0:64, :], [wt, state["lo"]])
        e = evac(pair, a, sg, ACT.Sigmoid, 1.0, w0[:, p:p + 1], state["tmpf"], ctok)
        ctk = V(lambda: nc.vector.tensor_tensor_scan(cum[:, :], C.reset64, sg[:, :], 0.0, ALU.mult, ALU.add), e)
        yield
        pair, a = both(wup[64:128, cs], lo[64:128, :], [wt, state["lo"]])
        at = evac(pair, a, av, ACT.Sigmoid, 1.0, a0[:, p:p + 1], state["tmpf"], ctok)
        yield
        for h in range(2):
            s, f = RU.take()
            for j in range(4):
                a = P(lambda: nc.tensor.transpose(s.ap[:, 128 * j:128 * j + 128],
                                                  ex[:, 512 * h + 128 * j:512 * h + 128 * j + 128], C.ident), ext, f,
                      sig=(j == 3))
            e = V(lambda: nc.vector.tensor_tensor(kk[:, 512 * h:512 * h + 512], kk[:, 512 * h:512 * h + 512], s.ap,
                                                  ALU.mult), a)
            s.free = [e]
            yield
        ea = a
        V(lambda: nc.vector.tensor_scalar(D[:, :], av[:, :], kac[:, p:p + 1], omka[:, p:p + 1], ALU.mult, ALU.add),
          at)
        yield
        V(lambda: nc.vector.tensor_tensor(k[:, :], k[:, :], D[:, :], ALU.mult))
        yield "half"
        pf = state["pairfree"][b]
        td = V(lambda: nc.vector.scalar_tensor_tensor(D[:, :], r[:, :], rkc[:, p:p + 1], k[:, :], ALU.mult, ALU.mult))
        t = S(lambda: nc.scalar.activation(ex[:, :], cum[:, :], ACT.Exp, scale=-EC), ctk, ea)
        yield
        c16 = lambda x: x.rearrange("p (c t) -> p c t", t=64)
        V(lambda: nc.vector.tensor_tensor(AR[:, b, :, 1, :], c16(r[:, :]), c16(ex[:, :]), ALU.mult), t, pf)
        x = V(lambda: nc.vector.tensor_copy(pc[:, b, :], c16(ex[:, :])[:, :, 63]))
        t2 = S(lambda: nc.scalar.activation(ex[:, :], cum[:, :], ACT.Exp, scale=EC), x)
        yield
        pair, a = both(C.bd64, D, [td])
        for h in range(2):
            sl = slice(512 * h, 512 * h + 512)
            e = V(lambda: nc.vector.tensor_tensor(bon[:, p % 3, sl], pair[h].ap, vT[:, b, sl], ALU.mult), a)
            pair[h].free = [e]
        yield
        t = V(lambda: nc.vector.tensor_tensor(D[:, :], cum[:, :], sg[:, :], ALU.subtract), a)
        t = S(lambda: nc.scalar.activation(D[:, :], D[:, :], ACT.Exp, scale=-EC), t)
        V(lambda: nc.vector.tensor_tensor(Kc[:, b, :], k[:, :], ex[:, :], ALU.mult), t2)
        yield
        V(lambda: nc.vector.scalar_tensor_tensor(AR[:, b, :, 0, :], c16(kk[:, :]), -1.0, c16(D[:, :]), ALU.mult,
                                                 ALU.mult), t)
        yield
        V(lambda: nc.vector.tensor_tensor(kk[:, :], kk[:, :], av[:, :], ALU.mult))
        yield
        t = V(lambda: nc.vector.tensor_tensor(Bc[:, b, :], kk[:, :], ex[:, :], ALU.mult))
        state["tmpf"] = t
        state[("prep", p)] = t

    RR = [slice(0, 64), slice(64, 128)]

    def tiles(outs, lhs, rhs, start=True, stop=True, toks=None, sig=True):
        for h, rr in enumerate(RR):
            a = P(lambda: nc.tensor.matmul(outs[rr], lhs[rr], rhs[rr], start=start, stop=stop,
                                           skip_group_check=True), toks, sig=(sig and h == 1))
        return a

    def rows(s, f, src, toks):
        for c in range(4):
            a = P(lambda: nc.tensor.transpose(s.ap[0:64, 128 * c:128 * c + 128], src[:, c, :], C.ident),
                  toks, f, sig=(c == 3))
        return a

    def apart(s, dst, a, toks):
        v = s.ap[0:64, :].rearrange("p (c h x) -> p c h x", c=4, h=2)
        for h, rr in enumerate(RR):
            e = S(lambda: nc.scalar.activation(dst[rr], v[:, :, h, :], ACT.Copy), a, toks)
        s.free = [e]
        return e

    def stage(p, g, n):
        b, gb = p % 2, n % 4
        pt = state[("prep", p)]
        gf = state["gfree"][gb]
        s1 = state["s1"][n % 2]
        X, M1 = XM_[:, 0, n % 2], XM_[:, 1, n % 2]
        gs = slice(256 * g, 256 * g + 256)
        c4 = lambda x: x.rearrange("p (c t) -> p c t", t=64)
        B4, K4, V4 = c4(Bc[:, b, gs]), c4(Kc[:, b, gs]), c4(vT[:, b, gs])
        for src, dst in ((B4, MB_), (K4, MK_)):
            s, f = RG.take()
            for c in range(4):
                a = tiles(s.ap[:, 128 * c:128 * c + 128], src[:, c, :],
                          AR[:, b, 4 * g + c, :, :].rearrange("p x t -> p (x t)"), toks=[pt, f], sig=(c == 3))
            mm = C.mAR.unsqueeze(1).to_broadcast([128, 4, 128])
            e = V(lambda: nc.vector.tensor_tensor(dst[:, gb].rearrange("p c x t -> p c (x t)"),
                                                  s.ap.rearrange("p (c t) -> p c t", c=4), mm, ALU.mult), a, gf)
            s.free = [e]
            if dst is MB_:
                lt = e
                LT = MB_[:, gb, :, 0, :]
                xt3 = XT[:, gb]
                lm = lambda l: C.lm64[:, l, :].unsqueeze(1).to_broadcast([128, 4, 64])
                V(lambda: nc.vector.tensor_copy(xt3, C.stack.unsqueeze(1).to_broadcast([128, 4, 64])))
                xtt = V(lambda: nc.vector.copy_predicated(xt3, lm(0), LT))
            yield
        mt = e
        side = iter([(B4, Bn), (K4, Kn), (V4, Vn)])
        nt = None
        xpe = mpe = s1
        for l in range(1, 6):
            s, f = RG.take()
            a = rows(s, f, xt3, [xtt])
            e = apart(s, X, a, xpe)
            yield
            for src, dst in [next(side, (None, None))]:
                if src is not None:
                    s, f = RG.take()
                    a = rows(s, f, src, [pt])
                    nt = apart(s, dst[:, gb], a, gf)
            s, f = RG.take()
            for c in range(4):
                a = tiles(s.ap[:, 64 * c:64 * c + 64], LT[:, c, :], X[:, c, :], toks=[lt, e, f], sig=(c == 3))
            xpe = a
            e = V(lambda: nc.vector.tensor_copy(M1[:, :, :].rearrange("p c s -> p (c s)"), s.ap[:, 0:256]), a, mpe)
            s.free = [e]
            yield
            s, f = RG.take()
            for c in range(4):
                a = tiles(s.ap[:, 64 * c:64 * c + 64], M1[:, c, :], xt3[:, c, :], toks=[xtt, e, f], sig=(c == 3))
            mpe = a
            xtt = V(lambda: nc.vector.copy_predicated(xt3, lm(l),
                                                      s.ap[:, 0:256].rearrange("p (c s) -> p c s", c=4)), a)
            s.free = [xtt]
            yield
        state["s1"][n % 2] = a
        state[("st", n)] = [mt, nt, xtt]
        if g >= 2:
            state.setdefault(("pf1", p), []).append(a)

    def chain(p, g, n):
        gb, b = n % 4, p % 2
        tk = state[("st", n)]
        ys_, yf = RY.take()
        for c in range(4):
            i = state["gn"] % 2
            j = 1 - i
            cc = 4 * g + c
            if cc == 0:
                state["st"] = V(lambda: nc.vector.memset(ST[:, i, :], 0.0), state["y"])
            stt = state["st"]
            V(lambda: nc.vector.tensor_scalar(zu[:, 2, :], ST[:, i, :], pc[:, b, cc:cc + 1], None, ALU.mult))
            s, f = RC.take()
            z = s.ap[:, 0:64]
            tiles(z, MK_[:, gb, c, 0, :], Vn[:, gb, c, :], True, False, [tk, f], sig=False)
            a = tiles(z, AR[:, b, cc, 0, :], ST[:, i, :], False, True, [stt])
            e = V(lambda: nc.vector.tensor_copy(zu[:, 0, :], z), a)
            s.free = [e]
            yo = ys_.ap[:, 64 * c:64 * c + 64]
            tiles(yo, AR[:, b, cc, 1, :], ST[:, i, :], True, False, [yf], sig=False)
            tiles(yo, MK_[:, gb, c, 1, :], Vn[:, gb, c, :], False, False, sig=False)
            yield
            s, f = RC.take()
            u = s.ap[:, 0:64]
            a = tiles(u, XT[:, gb, c, :], zu[:, 0, :], toks=[e, f])
            e = V(lambda: nc.vector.tensor_copy(zu[:, 1, :], u), a)
            s.free = [e]
            yield
            s, f = RC.take()
            w = s.ap[:, 0:64]
            tiles(w, Kn[:, gb, c, :], Vn[:, gb, c, :], True, False, [f], sig=False)
            a = tiles(w, Bn[:, gb, c, :], zu[:, 1, :], False, True, [e])
            state["st"] = V(lambda: nc.vector.scalar_tensor_tensor(ST[:, j, :], w, pc[:, b, cc:cc + 1],
                                                                   zu[:, 2, :], ALU.mult, ALU.add), a, state["y"])
            s.free = [state["st"]]
            state["y"] = tiles(yo, MB_[:, gb, c, 1, :], zu[:, 1, :], False, True)
            state["gn"] += 1
            yield
        e = S(lambda: nc.scalar.activation(Y2[:, p % 2, 4 * g:4 * g + 4, :].rearrange("p c v -> p (c v)"),
                                           ys_.ap[:, 0:256], ACT.Copy), state["y"], state["yfree"][p % 2])
        ys_.free = [e]
        state["gfree"][gb] = [state["y"]]
        state["yev"] = e
        if g == 3:
            state["pairfree"][b] = state[("pf1", p)] + [state["y"]]

    def finish(p):
        b = p % 2
        gate, fin = gf_[:, 0, :], gf_[:, 1, :]
        Y = Y2[:, b]
        pf1 = state["fin"]
        s16, q16 = ys[:, 0:16], ys[:, 16:32]
        bc = lambda x: x.unsqueeze(2).to_broadcast([128, 16, 64])
        V(lambda: nc.vector.tensor_reduce(s16, Y[:, :, :], AX.X, ALU.add), state["yev"])
        V(lambda: nc.vector.tensor_scalar(s16, s16, 1.0 / 64, None, ALU.mult))
        t = V(lambda: nc.vector.tensor_tensor(Y[:, :, :], Y[:, :, :], bc(s16), ALU.subtract))
        y1 = Y[:, :, :].rearrange("p c v -> p (c v)")
        t = S(lambda: nc.scalar.activation(fin[:, :], y1, ACT.Square), t, pf1)
        V(lambda: nc.vector.tensor_reduce(q16, fin[:, :].rearrange("p (c v) -> p c v", v=64), AX.X, ALU.add), t)
        t = V(lambda: nc.vector.tensor_scalar(q16, q16, 1.0 / 64, 64e-5, ALU.mult, ALU.add))
        t = S(lambda: nc.scalar.activation(q16, q16, ACT.Sqrt), t)
        V(lambda: nc.vector.reciprocal(q16, q16), t)
        yt = V(lambda: nc.vector.tensor_tensor(Y[:, :, :], Y[:, :, :], bc(q16), ALU.mult))
        out = []
        yield from unit_steps(K, W, xT, xtok, RU, out)
        pair, a = out[0]
        gt = evac(pair, a, gate, ACT.Silu, 1.0, 0.0, pf1)
        yield
        for half in range(2):
            s, f = RU.take()
            for c in range(8):
                a = tiles(s.ap[:, 64 * c:64 * c + 64], Y[:, 8 * half + c, :], C.stack, toks=[yt, f], sig=(c == 7))
            state["yfree"][b] = a
            sl = slice(512 * half, 512 * half + 512)
            e = S(lambda: nc.scalar.activation(fin[:, sl], s.ap, ACT.Identity, scale=lnw[:, p:p + 1],
                                               bias=lnb[:, p:p + 1]), a, V.last())
            s.free = [e]
            yield
            V(lambda: nc.vector.tensor_tensor(fin[:, sl], fin[:, sl], bon[:, p % 3, sl], ALU.add), e)
            e = V(lambda: nc.vector.tensor_tensor(fin[:, sl], fin[:, sl], gate[:, sl], ALU.mult), gt)
        d = K.dma(A["mix"][p], fin[:, :], e, sem=fsem[b])
        K.stored(d)
        state["fin"] = [e, d]

    fsem = [[*K.sem("fin"), 0] for _ in range(2)]
    run(prep_lo())
    run(prep(0))
    NP = 8

    def both_chains(n):
        yield from chain(n // 4, n % 4, n)
        yield from chain((n + 1) // 4, (n + 1) % 4, n + 1)

    def until_half(gen):
        for x in gen:
            if x == "half":
                return
            yield

    def then(*gens):
        for g in gens:
            yield from g

    nxt = None
    for n in range(0, 4 * NP + 2, 2):
        p, g = divmod(n, 4)
        gens = []
        if n > 0:
            gens.append(both_chains(n - 2))
        if n < 4 * NP:
            gens += [stage(p, g, n), stage(p, g + 1, n + 1)]
            if g == 0 and p + 1 < NP:
                nxt = prep(p + 1)
                gens.append(until_half(nxt))
            elif g == 2:
                parts = ([nxt] if p + 1 < NP else []) + ([finish(p - 1)] if p > 0 else [])
                gens.append(then(*parts))
        weave(*gens)
    run(finish(NP - 1))


def attention(K, C, W, xT, xtok, A, banks, st):
    nc, P, V, S, G = K.nc, K.P, K.V, K.S, K.G
    RU, RS, RT, RO = Ring(banks[0:2]), Ring(banks[2:4]), Ring(banks[4:6]), Ring(banks[6:8])
    sb = lambda n, s, d=F32: K.sb(st, n, s, d)
    qkvg = sb("qkvg", [128, 2, 4, 1024])
    Vc = sb("Vc", [128, 24, 128])
    Pm = sb("Pm", [128, 4, 512])
    PT = sb("PT", [128, 4, 512])
    O = sb("O", [128, 3, 1024])
    MB = sb("MB", [128, 3, 1024])
    LB = sb("LB", [128, 3, 1024])
    ml = sb("ml", [128, 2, 3, 2, 8])
    state = {"fr": [None, None], "pm": [None] * 4, "pt": [None] * 4, "n": 0, "ml": None, "vc": None, "xm": [None, None]}
    fsem = [*K.sem("fa"), 0]

    def prep(p):
        b = p % 2
        for i in range(4):
            out = []
            yield from unit_steps(K, W, xT, xtok, RU, out)
            pair, a = out[0]
            for h in range(2):
                e = S(lambda: nc.scalar.activation(qkvg[:, b, i, 512 * h:512 * h + 512], pair[h].ap,
                                                   ACT.Silu if i == 3 else ACT.Copy,
                                                   scale=0.125 if i == 0 else 1.0), a, state["fr"][b])
                pair[h].free = [e]
            yield
        state[("p", p)] = e

    def view(x, pi):
        if pi == 0:
            return x.rearrange("p (c i) -> p c i", i=128)
        if pi == 1:
            return x.rearrange("p (j r) -> p r j", r=4)
        return x.rearrange("p (j r) -> p r j", r=16)

    def cell(x, pi, c, two=False):
        if pi == 0:
            return x[:, 128 * (c - 1) if two else 128 * c:128 * c + 128]
        if pi == 1:
            v = x.rearrange("p (j r) -> p r j", r=4)
            return v[:, c // 2, 0:256] if two else v[:, c // 2, 128 * (c % 2):128 * (c % 2) + 128]
        v = x.rearrange("p (j r) -> p r j", r=16)
        return v[:, 2 * c:2 * c + 2, :]

    def scell(x, x3, pi, c):
        return x3[:, 128 * c:128 * c + 128] if pi == 2 else cell(x, pi, c)

    def group(x, pi, g):
        if pi == 0:
            return x[:, 512 * g:512 * g + 512], None
        r = 4 if pi == 1 else 16
        n = 2 if pi == 1 else 8
        return x.rearrange("p (j r) -> p r j", r=r)[:, n * g:n * g + n, :], n

    def scat(dst, src, pi, g, eng, *toks):
        d, n = group(dst, pi, g)
        s = src if n is None else src.rearrange("p (r j) -> p r j", r=n)
        if eng is S:
            return S(lambda: nc.scalar.activation(d, s, ACT.Copy), *toks)
        return V(lambda: nc.vector.tensor_copy(d, s), *toks)

    def attn(p):
        b = p % 2
        pt = state[("p", p)]
        q, k, v, g = [qkvg[:, b, i, :] for i in range(4)]
        q3, v3 = QV[:, 0, :], QV[:, 1, :]
        G(lambda: nc.gpsimd.tensor_copy(v3.rearrange("p (r j) -> p r j", r=16),
                                        v.rearrange("p (j r) -> p r j", r=16)), pt, state["vc"])
        g3 = G(lambda: nc.gpsimd.tensor_copy(q3.rearrange("p (r j) -> p r j", r=16),
                                             q.rearrange("p (j r) -> p r j", r=16)))
        for pi in range(3):
            for gg in range(2):
                s, f = RT.take()
                for j in range(4):
                    a = P(lambda: nc.tensor.transpose(s.ap[:, 128 * j:128 * j + 128], scell(v, v3, pi, 4 * gg + j),
                                                      C.ident), pt, g3 if pi == 2 else None, f, sig=(j == 3))
                i0 = 8 * pi + 4 * gg
                vc = S(lambda: nc.scalar.activation(Vc[:, i0:i0 + 4, :].rearrange("p c d -> p (c d)"), s.ap,
                                                    ACT.Copy), a, state["vc"])
                s.free = [vc]
                yield
        work = []
        for pi in range(3):
            per = 2 if pi < 2 else 4
            for gg in range(2):
                for h in range(2):
                    for c0 in range(4 * gg, 4 * gg + 4, per):
                        work.append((pi, gg, h, c0, per, h == 0 and c0 == 4 * gg, h == 1 and c0 + per == 4 * gg + 4))
        at = {}

        def scores(i):
            pi, gg, h, c0, per, first, last = work[i]
            rr = slice(64 * h, 64 * h + 64)
            bb = i % 4
            s, f = RS.take()
            w = 512 // per
            parts = []
            for j in range(per):
                c = c0 + j
                prev = (pi == 0 and c > 0) or (pi == 1 and c % 2 == 1)
                parts.append((c, prev))
                m = C.m3 if pi == 2 else (C.m2 if prev else C.m1)
                P(lambda: nc.tensor.matmul(s.ap[:, w * j:w * j + w], C.identb, m, start=True, stop=False,
                                           skip_group_check=True), f, pt, g3, sig=False)
                o = s.ap[:, w * j:w * j + w] if (prev or pi == 2) else s.ap[:, w * j + 128:w * j + 256]
                a = P(lambda: nc.tensor.matmul(o, scell(q[rr], q3[rr], pi, c), cell(k[rr], pi, c, prev),
                                               start=False, stop=True, skip_group_check=True),
                      sig=(j == per - 1))
            nm = ml[:, 0, pi, h, c0:c0 + per]
            t = V(lambda: nc.vector.tensor_reduce(nm, s.ap.rearrange("p (j w) -> p j w", j=per), AX.X,
                                                  ALU.max, negate=True), a, state["ml"])
            for j, (c, prev) in enumerate(parts):
                lo = w * j if (prev or pi == 2) else w * j + 128
                e = S(lambda: nc.scalar.activation(Pm[:, bb, lo:w * j + w], s.ap[:, lo:w * j + w],
                                                   ACT.Exp, bias=ml[:, 0, pi, h, c:c + 1],
                                                   accum_out=ml[:, 1, pi, h, c:c + 1]), t, state["pm"][bb])
            s.free = [e]
            at[i] = [parts, e]

        def turn(i):
            pi, gg, h, c0, per, first, last = work[i]
            parts, e = at[i]
            w = 512 // per
            bb = i % 4
            s, f = RT.take()
            blocks = []
            for j, (c, prev) in enumerate(parts):
                for lo in ((w * j, w * j + 128) if prev else (w * j + w - 128,)):
                    blocks.append((lo, c, prev and lo == w * j))
            for x, (lo, c, isp) in enumerate(blocks):
                a = P(lambda: nc.tensor.transpose(s.ap[:, 128 * x:128 * x + 128], Pm[:, bb, lo:lo + 128],
                                                  C.ident), e, f, sig=(x == len(blocks) - 1))
            state["pm"][bb] = a
            nb = len(blocks)
            e = V(lambda: nc.vector.tensor_copy(PT[:, bb, 0:128 * nb], s.ap[:, 0:128 * nb]), a, state["pt"][bb])
            s.free = [e]
            at[i] = [blocks, e]

        def values(i):
            pi, gg, h, c0, per, first, last = work[i]
            rr = slice(64 * h, 64 * h + 64)
            blocks, e = at[i]
            bb = i % 4
            nb = len(blocks)
            if first:
                at["ob"] = RO.take()
            ob, of = at["ob"]
            for x, (lo, c, isp) in enumerate(blocks):
                ci = 8 * pi + (c - 1 if isp else c)
                new = x == 0 or blocks[x - 1][1] != c
                end = x == nb - 1 or blocks[x + 1][1] != c
                a = P(lambda: nc.tensor.matmul(ob.ap[rr, 128 * (c % 4):128 * (c % 4) + 128],
                                               Vc[:, ci, rr], PT[:, bb, 128 * x:128 * x + 128],
                                               start=new, stop=end), e, vc, of, sig=(x == nb - 1))
            state["pt"][bb] = a
            state["vc"] = a
            if last:
                at["o"] = scat(O[:, pi, :], ob.ap, pi, gg, S, a, state.get("Of"))
                ob.free = [at["o"]]

        n = len(work)
        for i in range(n + 4):
            if i < n:
                scores(i)
            if 0 <= i - 2 < n:
                turn(i - 2)
            if 0 <= i - 4 < n:
                values(i - 4)
            yield
        ot = at["o"]
        a = state["vc"]
        mlt = [S.last(), V.last()]
        for x, dst in ((0, MB), (1, LB)):
            for pi in range(3):
                xs = (3 * x + pi) % 2
                for h in range(2):
                    et = G(lambda: nc.gpsimd.tensor_copy(XM[:, xs, :, h, :], ml[:, x, pi, h, :].unsqueeze(2)
                                                         .to_broadcast([128, 8, 64])), mlt, state["xm"][xs])
                for gg in range(2):
                    s, f = RT.take()
                    for j in range(4):
                        c = 4 * gg + j
                        a = P(lambda: nc.tensor.transpose(s.ap[:, 128 * j:128 * j + 128],
                                                          XM[:, xs, c].rearrange("p h v -> p (h v)"), C.ident),
                              et, f, sig=(j == 3))
                    state["xm"][xs] = a
                    e = scat(dst[:, pi, :], s.ap, pi, gg, S, a, state.get("mf"))
                    s.free = [e]
                    yield
        state["ml"] = et
        S.wait(et)
        mt = e
        tt = lambda o, x, y, op, *tk: V(lambda: nc.vector.tensor_tensor(o, x, y, op), *tk)
        mn, den, acc = D[:, 0, :], D[:, 1, :], D[:, 2, :]
        tt(mn, MB[:, 0, :], MB[:, 1, :], ALU.min, mt, ot, state.get("Df"))
        tt(mn, mn, MB[:, 2, :], ALU.min)
        for pi in range(3):
            t = tt(MB[:, pi, :], mn, MB[:, pi, :], ALU.subtract)
            t = S(lambda: nc.scalar.activation(MB[:, pi, :], MB[:, pi, :], ACT.Exp), t)
            tt(LB[:, pi, :], LB[:, pi, :], MB[:, pi, :], ALU.mult, t)
            tt(O[:, pi, :], O[:, pi, :], MB[:, pi, :], ALU.mult)
            if pi == 1:
                tt(den, LB[:, 0, :], LB[:, 1, :], ALU.add)
                tt(acc, O[:, 0, :], O[:, 1, :], ALU.add)
            elif pi == 2:
                tt(den, den, LB[:, 2, :], ALU.add)
                t = tt(acc, acc, O[:, 2, :], ALU.add)
                state["Of"] = state["mf"] = t
            yield
        V(lambda: nc.vector.reciprocal(den, den))
        tt(den, den, g, ALU.mult)
        e = tt(acc, acc, den, ALU.mult)
        state["fr"][b] = [e, a]
        state["Df"] = K.dma(A["mix"][8 + p], acc, e, sem=fsem)
        K.stored(state["Df"])

    D = sb("Dm", [128, 3, 1024])
    QV = sb("QV", [128, 2, 1024])
    XM = sb("XM", [128, 2, 8, 2, 64])
    run(prep(0))
    for p in range(8):
        if p < 7:
            weave(attn(p), prep(p + 1))
        else:
            run(attn(p))


def block2(K, C, h, htok, xT, A, banks):
    nc = K.nc
    with ExitStack() as st:
        cols = K.sb(st, "cols2", [128, 112])
        ct = K.dma(cols[:, 0:96], A["c2"])
        ring = Ring(banks)
        with ExitStack() as s2:
            nw = K.sb(s2, "nw", [128, 8])
            nt = K.dma(nw[:, :], A["nw2"])
            xtok = rms_T(K, s2, h, [htok, nt], xT, None, nw, 1e-5, C.ident, ring, 0)
            hs = K.dma(A["hs"], h[:, :, :], htok)
            K.stored(hs)
            K.fence()
        K.D.wait(hs)
        for q in (K.P, K.V, K.S, K.G):
            q.wait(hs)
        return xtok


def block2_rest(K, C, hbuf, xT, A, banks):
    nc = K.nc
    with ExitStack() as st:
        cols = K.sb(st, "cols2", [128, 112])
        ct = K.dma(cols[:, 0:96], A["c2"])
        with ExitStack() as s2:
            W = Weights(K, s2, [A["w2u"][i] for i in range(33)])
            rwkv(K, C, W, xT, None, A, banks, s2, cols, ct)
            K.fence()
        K.V.wait(*K.stores.values())
        K.D.wait(*K.stores.values())
        with ExitStack() as s2:
            W = Weights(K, s2, [A["w2u"][33 + i] for i in range(32)])
            attention(K, C, W, xT, None, A, banks, s2)
            K.fence()
        for q in (K.P, K.V, K.S, K.D):
            q.wait(*K.stores.values())


def block2_out(K, C, h, xT, A, banks):
    nc, P, V, S = K.nc, K.P, K.V, K.S
    ring = Ring(banks)
    with ExitStack() as st:
        mix = K.sb(st, "mixs", [128, 16, 1024])
        wo = K.sb(st, "wo2", [128, 16, 512])
        t1 = K.dma(h[:, :, :], A["hs"])
        mts = [K.dma(mix[:, i, :], A["mix"][i]) for i in range(16)]
        wf = None
        for hh in range(2):
            wt = K.dma(wo[:, :, :], A["wo2"][hh], wf)
            for t in range(8):
                s, f = ring.take()
                for k in range(16):
                    a = P(lambda: nc.tensor.matmul(s.ap, mix[:, k, 128 * t:128 * t + 128], wo[:, k, :],
                                                   start=(k == 0), stop=(k == 15)), mts[k], wt, f, sig=(k == 15))
                hs = h[:, t, 512 * hh:512 * hh + 512]
                e = V(lambda: nc.vector.tensor_tensor(hs, hs, s.ap, ALU.add), a, t1)
                s.free = [e]
            wf = a
        K.fence()
    P, V, S = K.P, K.V, K.S
    with ExitStack() as st:
        fw = K.sb(st, "fw", [128, 1024])
        ft = K.dma(fw[:, :], A["fw2"])
        ss = K.sb(st, "ssf", [128, 8])
        sq = K.sb(st, "sqf", [128, 1024])
        for t in range(8):
            a = S(lambda: nc.scalar.activation(sq[:, :], h[:, t, :], ACT.Square, accum_out=ss[:, t:t + 1]), e)
        b = V(lambda: nc.vector.tensor_scalar(ss[:, :], ss[:, :], 1.0 / 1024, 1e-5, ALU.mult, ALU.add), a)
        b = S(lambda: nc.scalar.activation(ss[:, :], ss[:, :], ACT.Sqrt), b)
        V(lambda: nc.vector.reciprocal(ss[:, :], ss[:, :]), b)
        for t in range(8):
            e = V(lambda: nc.vector.scalar_tensor_tensor(h[:, t, :], h[:, t, :], ss[:, t:t + 1], fw[:, :], ALU.mult,
                                                         ALU.mult), ft)
        K.fence()
    return e


class Consts:
    pass


def load_consts(K, ctx, A):
    C = Consts()
    cc = K.sb(ctx, "cc", [128, 768])
    lm = K.sb(ctx, "lm", [128, 1280], U8)
    c2 = K.sb(ctx, "c2c", [128, 1344])
    mb = K.sb(ctx, "mb", [128, 768], BF16)
    with ExitStack() as st:
        wide = K.sb(st, "lmf", [128, 1280])
        t = K.V(lambda: K.nc.vector.tensor_copy(lm[:, :], wide[:, :]), K.dma(wide[:, :], A["lm"]))
        K.D.wait(t)
    toks = [K.dma(cc[:, :], A["cc"]), K.dma(c2[:, :], A["c2c"]), K.dma(mb[:, :], A["mb"]), t]
    C.tok = toks
    C.ident, C.ge, C.lt = cc[:, 0:128], cc[:, 128:256], cc[:, 256:384]
    C.bd64, C.bd32 = cc[:, 384:512], cc[:, 512:768]
    C.lmask = lm[:, 0:896].rearrange("p (l t) -> p l t", l=7)
    C.lm64 = lm[:, 896:1280].rearrange("p (l t) -> p l t", l=6)
    C.mAR, C.stack, C.reset64 = c2[:, 0:128], c2[:, 256:320], c2[:, 320:1344]
    C.identb, C.m2, C.m1, C.m3 = mb[:, 0:128], mb[:, 128:384], mb[:, 384:640], mb[:, 640:768]
    K.fence_sb = cc
    for q in (K.P, K.V, K.S, K.G):
        q.wait(*toks)
    return C


def build_program(nc, A):
    with ExitStack() as ctx:
        K = Kern(nc, ctx)
        ps = ctx.enter_context(nc.psum_tensor("ps", [128, 8, 512], F32))
        K.fence_ps = ps[:, 7, :]
        banks = [ps[:, i, :] for i in range(8)]
        C = load_consts(K, ctx, A)
        with ExitStack() as s0:
            xT = K.sb(s0, "xT", [128, 8, 1024])
            t = K.dma(xT[:, :, :], A["xT"])
            with ExitStack() as s1:
                h = K.sb(s1, "h", [128, 8, 1024])
                e = block1(K, C, h, xT, t, A, banks)
                block2(K, C, h, None, xT, A, banks)
            block2_rest(K, C, None, xT, A, banks)
        h = K.sb(ctx, "h", [128, 8, 1024])
        block2_out(K, C, h, None, A, banks)
        xT = K.sb(ctx, "xT", [128, 8, 1024])
        block3(K, C, h, None, xT, None, A, banks)
        K.D.wait(*K.stores.values())



def bc(v):
    return np.ascontiguousarray(np.broadcast_to(v.reshape(1, -1), (128, v.size)))


def units(blocks):
    w = np.concatenate(blocks, axis=1)
    n = w.shape[1] // 128
    return np.ascontiguousarray(w.reshape(8, 128, n, 128).transpose(2, 1, 0, 3).reshape(n, 128, 1024))


def col(v):
    return np.ascontiguousarray(v.reshape(-1, 128).T)


def zeros(*shape):
    return np.zeros(shape, np.float32)


def consts():
    i=np.arange(128)
    A={}
    cc=np.zeros((128,768),np.float32)
    s=i[:,None]; t=i[None]
    cc[:,0:128]=np.eye(128)
    cc[:,128:256]=(t>=s)
    cc[:,256:384]=(t<s)
    cc[:,384:512]=(s//64==t//64)
    cc[:,512:768]=(s//32==np.arange(256)[None]//64)
    A["rst"]=bc((np.arange(1024)%128!=0).astype(np.float32)[None])
    A["cc"]=cc
    c2=np.zeros((128,128+128+64+1024),np.float32)
    bdm=(s//64==t//64)
    t6=np.arange(64)[None]
    c2[:,0:64]=s%64<t6; c2[:,64:128]=s%64<=t6
    c2[:,256:320]=(s%64==np.arange(64)[None])
    c2[:,320:]=(np.arange(1024)%64!=0)[None]
    A["c2c"]=c2
    
    NEG=-1e30
    mb=np.zeros((128,128+256*2+128),np.float32)
    mb[:,0:128]=np.eye(128)
    q=i[:,None]; k=i[None]
    prev=np.where(k>=q,0,NEG); cur=np.where(k<=q,0,NEG)
    mb[:,128:256]=prev; mb[:,256:384]=cur
    mb[:,384:512]=NEG; mb[:,512:640]=cur
    mb[:,640:768]=np.where((q//64==k//64)&(k<=q),0,NEG)
    A["mb"]=mb.astype(mybir.dt.np(BF16))
    lm=np.zeros((128,7,128),np.float32)
    for l in range(7):
        B=1<<l
        lm[:,l]=((s//(2*B)==t//(2*B))&(s//B%2==0)&(t//B%2==1))
    A["lm"]=np.concatenate([lm.reshape(128,-1)]+[lm[i%64,l,:64] for l in range(6)],1)
    return A


def host1(I):
    w=I["w_in"][0]; A={}
    c=lambda o,i=0,n=128:w[:,o+128*i:o+128*i+n]
    L=[]
    for p in range(2): L+=[c(0,p),c(256,p),c(512,p),c(768,p)]
    for p in range(2): L+=[c(1024,p),c(1536,p),c(1280,p),c(1792,p)]
    L+=[c(2048),c(2176),c(2304),c(2304,1),c(2560),c(2560,1),np.concatenate([c(2816,0,16),np.zeros((1024,112),np.float32)],1)]
    A["w1"]=units(L)
    G=units([w[:,2832+1024*b+128*d:2832+1024*b+128*d+128] for d in range(8) for b in range(3)])
    up=I["w_up"][0]
    U=np.stack([up[b].reshape(2,128,8,128)[:,:,d,:].transpose(1,0,2).reshape(128,256) for d in range(8) for b in range(3)])
    A["wg"]=np.ascontiguousarray(np.concatenate([G,U],2))
    A["c1"]=np.ascontiguousarray(np.concatenate([col(I["hgrn_norm_g"][0]),col(I["gla_norm_g"][0]),col(I["gla_gate_b"][0]),col(I["hgrn_lb_logits"][0]),np.zeros((128,9),np.float32)],1))
    A["w2"]=I["gla_gate_w2"][0]
    A["wo1"]=np.ascontiguousarray(I["w_out"][0].reshape(8,128,1024).transpose(1,0,2))
    A["rows1"]=np.ascontiguousarray(np.stack([bc(I["ln_g"][0][None]),bc(I["ln_b"][0][None])],1))
    return A


def host2(I):
    g=lambda n:I[n+"_2"]
    w=g("w_in"); c=lambda o,i=0:w[:,o+128*i:o+128*i+128]
    L=[c(3072)]
    rk=lambda p:[c(0,p),c(1024,p),c(2048,p)]
    G0=3200; A0=4224; AG=7296
    L+=rk(0)+rk(1)[:2]+rk(1)[2:]
    for p in range(1,7): L+=rk(p+1)+[c(G0,p-1)]
    L+=[c(G0,6),c(G0,7)]
    for p in range(8): L+=[c(A0,p),c(A0+1024,p),c(A0+2048,p),c(AG,p)]
    A={}
    A["w2u"]=units(L)
    mu=g("mu_shift")
    A["c2"]=np.ascontiguousarray(np.concatenate([np.zeros((128,8),np.float32)]+[col(g(n)) for n in ("w0","a0","k_k","k_a")]+[col(g("r_k").reshape(-1)),col(g("ln_x_w")),col(g("ln_x_b")),col(mu[:3072]),col(mu[3072:]),np.zeros((128,7),np.float32)],1))
    A["wup2"]=np.ascontiguousarray(np.concatenate([g("w_up"),g("a_up")],0))
    A["nw2"]=col(g("norm_w"))
    A["wo2"]=np.ascontiguousarray(g("w_out").reshape(16,128,2,512).transpose(2,1,0,3))
    A["fw2"]=bc(g("final_norm_w")[None])
    return A


def host3(I):
    w=I["w_in_3"][0]; o=[]
    v=w[:,512:1024]; u=w[:,:512]; g=w[:,1024:1536]; z=w[:,1536:2048]; gb=w[:,2048:]
    c=lambda a,i:a[:,128*i:128*i+128]
    cols=[c(v,i) for i in range(4)]
    for i in range(4): cols+=[c(u,i),c(g,i)]
    for i in range(4): cols+=[c(z,i),c(gb,i)]
    A={}
    A["w3"]=units(cols)
    A["c3"]=np.ascontiguousarray(np.concatenate([I["pre_g_3"][0].reshape(8,128).T, I["b_f_3"][0].T, np.zeros((128,4),np.float32)],1))
    p=np.arange(128)[:,None]; uu=np.arange(128)[None]
    d=np.zeros((128,8,2,128))
    for vv in range(8):
        th=2*np.pi*(((8*uu+vv)*p)%1024)/1024
        d[:,vv,0]=np.cos(th);d[:,vv,1]=np.sin(th)
    A["d3"]=d.reshape(128,2048).astype(np.float32)
    A["rows3"]=np.stack([bc(I["ln_g_3"][0][None]),bc(I["ln_b_3"][0][None]),bc(I["b_s_3"][0].reshape(1,512))])
    A["ws3"]=np.ascontiguousarray(I["w_s_3"][0].transpose(2,0,1).reshape(128,512))
    th=2*np.pi*((p*uu)%128)/128
    s=1/np.sqrt(1024*128)
    A["cd"]=np.concatenate([np.cos(th)*s,-np.sin(th)*s],1).astype(np.float32)
    A["wf3"]=np.ascontiguousarray(I["w_f_3"][0].transpose(1,0,2).reshape(128,512))
    A["wo3"]=np.ascontiguousarray(I["w_out_3"][0].reshape(8,128,1024).transpose(1,0,2))
    A["post3"]=bc(I["post_g_3"][0][None])
    return A



def kernel(**inputs):
    import concourse.bacc as bacc
    from concourse.bass_utils import run_bass_kernel_spmd

    I = {k: np.asarray(v) for k, v in inputs.items()}
    A = consts()
    A.update(host1(I))
    A.update(host2(I))
    A.update(host3(I))
    x = I["x"][0]
    A["x"] = np.ascontiguousarray(x.reshape(8, 128, 1024).transpose(1, 0, 2))
    A["xT"] = np.ascontiguousarray(x.T.reshape(8, 128, 1024).transpose(1, 0, 2))
    nc = bacc.Bacc("TRN2", target_bir_lowering=False, num_devices=1)
    aps, arrays = {}, {}
    for n, a in A.items():
        arrays["in_" + n] = a
        aps[n] = nc.dram_tensor("in_" + n, a.shape, mybir.dt.from_np(a.dtype), kind="ExternalInput").ap()
    aps["out"] = nc.dram_tensor("out_0", (8, 128, 1024), F32, kind="ExternalOutput").ap()
    aps["hs"] = nc.dram_tensor("hs", (128, 8, 1024), F32, kind="Internal").ap()
    aps["mix"] = nc.dram_tensor("mix", (16, 128, 1024), F32, kind="Internal").ap()
    build_program(nc, aps)
    r = run_bass_kernel_spmd(nc, [arrays], core_ids=[0])
    return r.results[0]["out_0"].reshape(1, 1024, 1024)
```

```python
import numpy as np
from contextlib import ExitStack
import concourse.bass as bass
from concourse import mybir

F32 = mybir.dt.float32
BF16 = mybir.dt.bfloat16
U8 = mybir.dt.uint8
F32R = mybir.dt.float32r
ALU = mybir.AluOpType
ACT = mybir.ActivationFunctionType
AX = mybir.AxisListType


class Queue:

    def __init__(self, eng, sem, name, linked):
        self.eng, self.sem, self.name, self.linked = eng, sem, name, linked
        self.n = 0
        self.seen = {}

    def wait(self, *tokens):
        for t in tokens:
            if t is None:
                continue
            if isinstance(t, list):
                self.wait(*t)
                continue
            sem, name, value = t
            if self.seen.get(name, 0) < value:
                self.seen[name] = value
                self.eng.wait_ge(sem, value)

    def last(self):
        return (self.sem, self.name, self.n) if self.n else None

    def __call__(self, make, *tokens, sig=True):
        self.wait(*tokens)
        if self.linked:
            self.wait(self.last())
        ins = make()
        if sig:
            self.n += 1
            ins.then_inc(self.sem, 1)
            return (self.sem, self.name, self.n)
        return None


class Slot:

    def __init__(self, ap):
        self.ap = ap
        self.free = []


class Ring:
    def __init__(self, aps):
        self.slots = [Slot(a) for a in aps]
        self.n = 0

    @staticmethod
    def of(slots):
        r = Ring([])
        r.slots = list(slots)
        return r

    def take(self):
        s = self.slots[self.n % len(self.slots)]
        self.n += 1
        f, s.free = s.free, []
        return s, f


class Kern:
    def __init__(self, nc, ctx):
        self.nc, self.ctx = nc, ctx
        self.nsem = 0
        self.names = 0
        self.dsem = []
        self.stores = {}
        self.phase()

    def sem(self, name):
        self.nsem += 1
        n = f"{name}_{self.nsem}"
        return self.ctx.enter_context(self.nc.semaphore(n)), n

    def phase(self):
        nc = self.nc
        self.P = Queue(nc.tensor, *self.sem("pe"), False)
        self.V = Queue(nc.vector, *self.sem("dve"), True)
        self.S = Queue(nc.scalar, *self.sem("act"), True)
        self.G = Queue(nc.gpsimd, *self.sem("pool"), True)
        self.D = Queue(nc.sync, *self.sem("sp"), False)

    def fence(self):
        qs = [self.P, self.V, self.S, self.G]
        self.P(lambda: self.nc.tensor.matmul(
            self.fence_ps[0:1, 0:1], self.fence_sb[0:1, 0:1], self.fence_sb[0:1, 0:1], start=True, stop=True),
            self.V.last(), self.S.last())
        toks = [q.last() for q in qs]
        for q in qs + [self.D]:
            q.wait(*toks)
        self.phase()

    def stored(self, token):
        self.stores[token[1]] = token

    def sb(self, stack, name, shape, dt=F32):
        self.names += 1
        return stack.enter_context(self.nc.sbuf_tensor(f"{name}_{self.names}", shape, dt))

    def dma(self, dst, src, *tokens, q=None, sem=None):
        q = q or self.D
        q.wait(*tokens)
        if sem is None:
            s, n = self.sem("dma")
            sem = [s, n, 0]
        sem[2] += 16
        q.eng.dma_start(dst, src).then_inc(sem[0], 16)
        return (sem[0], sem[1], sem[2])


class Weights:

    def __init__(self, K, stack, units, depth=3, width=1024):
        self.K, self.units, self.depth = K, units, depth
        self.buf = K.sb(stack, "wring", [128, depth, width])
        self.sems = [[*K.sem("w"), 0] for _ in range(depth)]
        self.rel = [None] * depth
        self.issued = 0
        self.n = 0
        self.tok = {}

    def pump(self):
        while self.issued < min(len(self.units), self.n + self.depth):
            i = self.issued
            s = i % self.depth
            self.tok[i] = self.K.dma(self.buf[:, s, 0:self.units[i].shape[-1]], self.units[i], self.rel[s], sem=self.sems[s])
            self.issued += 1

    def get(self):
        self.pump()
        i = self.n
        return self.buf[:, i % self.depth, :].rearrange("p (k c) -> p k c", c=128), self.tok[i]

    def done(self, token):
        self.rel[self.n % self.depth] = token
        self.n += 1
        self.pump()


def weave(*gens):
    live = list(gens)
    while live:
        for g in list(live):
            try:
                next(g)
            except StopIteration:
                live.remove(g)


def split(K, x, high, low, *tokens):
    t = K.S(lambda: K.nc.scalar.activation(high, x, ACT.Copy), *tokens)
    return K.V(lambda: K.nc.vector.tensor_tensor(low, x, high.bitcast(F32), ALU.subtract), t)


def products(K, out, lhs, rhs, start, stop, *tokens, sig=False):
    (a, b), (c, d) = lhs, rhs
    mm = K.nc.tensor.matmul
    K.P(lambda: mm(out, a, c, start=start, stop=False), *tokens, sig=False)
    K.P(lambda: mm(out, b, c, start=False, stop=False), sig=False)
    return K.P(lambda: mm(out, a, d, start=False, stop=stop), sig=sig)


class SplitWeights:

    def __init__(self, K, stack, units, depth=2, width=1024):
        self.K, self.n = K, 0
        self.W = Weights(K, stack, units, depth, width)
        self.parts = K.sb(stack, "wparts", [128, 2, 2, width], F32R)
        self.tok = {}
        self.rel = [None, None]
        self.split(0)

    def split(self, i):
        W = self.W
        if i in self.tok or i >= len(W.units):
            return
        tok = W.get()[1]
        b = i % 2
        self.tok[i] = split(self.K, W.buf[:, i % W.depth, :], self.parts[:, b, 0, :], self.parts[:, b, 1, :],
                            tok, self.rel[b])
        W.done(self.tok[i])

    def get(self):
        i = self.n
        self.split(i)
        self.split(i + 1)
        view = lambda ap: ap.rearrange("p (k c) -> p k c", c=128)
        return (view(self.parts[:, i % 2, 0, :]), view(self.parts[:, i % 2, 1, :])), self.tok[i]

    def done(self, token):
        self.rel[self.n % 2] = token
        self.n += 1


def load_masks(K, stack, A, C):
    lm = K.sb(stack, "lm", [128, 1280], U8)
    with ExitStack() as st:
        wide = K.sb(st, "wide", [128, 1280])
        K.D.wait(K.V(lambda: K.nc.vector.tensor_copy(lm[:, :], wide[:, :]), K.dma(wide[:, :], A["lm"])))
    C.lmask = lm[:, 0:896].rearrange("p (l t) -> p l t", l=7)
    C.lm64 = lm[:, 896:1280].rearrange("p (l t) -> p l t", l=6)




def rms_T(K, stack, h, htok, xT, gain, eps, ident, banks, xs=None):
    nc, V, S, P = K.nc, K.V, K.S, K.P
    sq = K.sb(stack, "sq", [128, 1024])
    ss = K.sb(stack, "ss", [128, 8])
    xn = K.sb(stack, "xn", [128, 4, 1024])
    r = []
    for half in range(2):
        part = ss[:, 4 * half:4 * half + 4]
        for t in range(4 * half, 4 * half + 4):
            a = S(lambda: nc.scalar.activation(sq[:, :], h[:, t, :], ACT.Square, accum_out=ss[:, t:t + 1]), htok)
        b = V(lambda: nc.vector.tensor_scalar(part, part, 1.0 / 1024, eps, ALU.mult, ALU.add), a)
        r.append(S(lambda: nc.scalar.activation(part, part, ACT.Sqrt), b))
    out = None
    tp = None
    for half in range(2):
        part = ss[:, 4 * half:4 * half + 4]
        V(lambda: nc.vector.reciprocal(part, part), r[half])
        for j in range(4):
            t = 4 * half + j
            nt = V(lambda: nc.vector.tensor_scalar(xn[:, j, :], h[:, t, :], ss[:, t:t + 1], None, ALU.mult), tp)
        for k in range(8):
            s, f = banks.take()
            for j in range(4):
                tp = P(lambda: nc.tensor.transpose(s.ap[:, 128 * j:128 * j + 128],
                                                   xn[:, j, 128 * k:128 * k + 128], ident), nt, f, sig=(j == 3))
            sl = slice(512 * half, 512 * half + 512)
            if xs is None:
                out = S(lambda: nc.scalar.activation(xT[:, k, sl], s.ap, ACT.Copy, scale=gain[:, k:k + 1]), tp)
            else:
                out = S(lambda: nc.scalar.activation(xs[:, 0, k, sl], s.ap, ACT.Copy, scale=gain[:, k:k + 1]), tp)
                out = V(lambda: nc.vector.scalar_tensor_tensor(xs[:, 1, k, sl], s.ap, gain[:, k:k + 1],
                                                               xs[:, 0, k, sl].bitcast(F32), ALU.mult,
                                                               ALU.subtract), out)
            s.free = [out]
    return out


def split_unit(K, W, xs, xtok, pair, free):
    (wh, wl), tok = W.get()
    for k in range(8):
        for h in range(2):
            sl = slice(512 * h, 512 * h + 512)
            t = products(K, pair[h], (wh[:, k, :], wl[:, k, :]), (xs[:, 0, k, sl], xs[:, 1, k, sl]),
                         k == 0, k == 7, tok, xtok, free, sig=(k == 7))
    W.done(t)
    return t


def rows_product(K, slots, left, W, last):
    n = left.n
    for k in range(n):
        parts, ltok = left(k)
        (wh, wl), tok = W.get()
        for t in range(8):
            sl = slice(128 * t, 128 * t + 128)
            a = products(K, slots[t].ap, (parts[0][:, sl], parts[1][:, sl]),
                         (wh.rearrange("p k c -> p (k c)"), wl.rearrange("p k c -> p (k c)")),
                         k == 0, k == n - 1, ltok, tok, slots[t].free, sig=(t == 7 or k == n - 1))
            if k == n - 1:
                slots[t].free = last(t, slots[t].ap, a)
        W.done(a)


def block3(K, C, h, A, banks):
    nc, P, V, S = K.nc, K.P, K.V, K.S
    with ExitStack() as st:
        ident = C.ident
        cols = K.sb(st, "cols", [128, 8 + 4 + 4])
        ct = K.dma(cols[:, :], A["c3"])
        g8 = cols[:, 0:8]
        bf = cols[:, 8:12]
        ring = Ring(banks)
        mixT = K.sb(st, "mixT", [128, 8, 1024])
        stat = K.sb(st, "stat", [128, 8, 8])
        ss = K.sb(st, "ss3", [128, 8, 2])
        inner = st.enter_context(ExitStack())
        xs = K.sb(inner, "xs", [128, 2, 8, 1024], F32R)
        with ExitStack() as s2:
            xtok = rms_T(K, s2, h, ct, None, g8, 1e-6, ident, ring, xs)
        K.D.wait(xtok)
        u = K.sb(inner, "ua", [128, 2, 1024])
        vn = K.sb(inner, "vn", [128, 8, 512])
        with ExitStack() as s2:
            WV = SplitWeights(K, s2, [A["w3v"][k] for k in range(8)], 3, 512)

            def left(k):
                return (xs[:, 0, k, :], xs[:, 1, k, :]), xtok

            left.n = 8
            rows_product(K, ring.slots, left, WV, lambda t, ap, a: [S(
                lambda: nc.scalar.activation(vn[:, t, :], ap, ACT.Gelu), a)])
            vt = S.last()
            K.D.wait(P.last())
            S.wait(P.last())
            V.wait(P.last())
        cmat = K.sb(inner, "cmat", [128, 4096])
        t_g = K.dma(cmat[:, 2048:2560], A["rows3"][0])
        t_g2 = K.dma(cmat[:, 2560:3072], A["rows3"][1])
        t_bs = K.dma(cmat[:, 3072:3584], A["rows3"][2])
        t_ws = K.dma(cmat[:, 3584:4096], A["ws3"])
        W = SplitWeights(K, inner, [A["w3"][i] for i in range(16)])
        t_c = K.dma(cmat[:, 0:2048], A["d3"][:, 0:2048])
        dft = cmat[:, 0:2048].rearrange("p (v m u) -> p v m u", v=8, m=2)
        lng, lnb, bs = cmat[:, 2048:2560], cmat[:, 2560:3072], cmat[:, 3072:3584]
        ws = cmat[:, 3584:4096].rearrange("p (h q) -> p h q", h=4)
        cd = K.sb(inner, "cd", [128, 256])
        t_cd = K.dma(cd[:, :], A["cd"])
        wf = K.sb(inner, "wf", [128, 512])
        t_wf = K.dma(wf[:, :], A["wf3"])
        for t in range(8):
            V(lambda: nc.vector.bn_stats(stat[:, t, 0:6], vn[:, t, :]), vt)
            x = V(lambda: nc.vector.bn_aggr(stat[:, t, 6:8], stat[:, t, 0:6]))
        x = V(lambda: nc.vector.tensor_scalar(stat[:, :, 7], stat[:, :, 7], 1e-6, None, ALU.add))
        x = S(lambda: nc.scalar.activation(stat[:, :, 7], stat[:, :, 7], ACT.Sqrt), x)
        V(lambda: nc.vector.reciprocal(stat[:, :, 7], stat[:, :, 7]), x)
        for t in range(8):
            V(lambda: nc.vector.tensor_scalar(vn[:, t, :], vn[:, t, :], stat[:, t, 6:7], stat[:, t, 7:8],
                                              ALU.subtract, ALU.mult))
            V(lambda: nc.vector.tensor_tensor(vn[:, t, :], vn[:, t, :], lng, ALU.mult), t_g)
            vtok = V(lambda: nc.vector.tensor_tensor(vn[:, t, :], vn[:, t, :], lnb, ALU.add), t_g2)
        ufree = None
        for c in range(4):
            for kind in range(2):
                pair, fr = [], []
                for _ in range(2):
                    s, f = ring.take()
                    pair.append(s)
                    fr += f
                a = split_unit(K, W, xs, xtok, [p.ap for p in pair], fr)
                for hh in range(2):
                    o = u[:, kind, 512 * hh:512 * hh + 512]
                    b = S(lambda: nc.scalar.activation(o, pair[hh].ap, ACT.Gelu if kind == 0 else ACT.Silu), a, ufree)
                    pair[hh].free = [b]
            ug = V(lambda: nc.vector.tensor_tensor(u[:, 0, :], u[:, 0, :], u[:, 1, :], ALU.mult), b)
            for half in range(2):
                s, f = ring.take()
                for j in range(4):
                    t = 4 * half + j
                    a = P(lambda: nc.tensor.matmul(s.ap[:, 128 * j:128 * j + 128], vn[:, t, 128 * c:128 * c + 128],
                                                   ws[:, c, :], start=True, stop=True), vtok, t_ws, f, sig=(j == 3))
                o = mixT[:, c, 512 * half:512 * half + 512]
                bb = bs[:, 128 * c:128 * c + 128].unsqueeze(1).to_broadcast([128, 4, 128])
                b = V(lambda: nc.vector.tensor_tensor(o.rearrange("p (j q) -> p j q", j=4),
                                                      s.ap.rearrange("p (j q) -> p j q", j=4), bb, ALU.add),
                      a, t_bs)
                s.free = [b]
                ufree = V(lambda: nc.vector.tensor_tensor(o, o, u[:, 0, 512 * half:512 * half + 512], ALU.mult))
        zT = cmat[:, 2048:3072]
        fT = u[:, 1, :]
        Z = vn[:, :, :].rearrange("p a (b m c) -> p (a b m c)", b=2, m=2).rearrange("p (z a m c) -> p z a m c",
                                                                                    z=2, a=8, m=2)
        Y = K.sb(inner, "Y", [128, 8, 2, 128])
        r2 = float(np.sqrt(0.5))
        at = {"z": [P.last(), V.last()], "y": P.last(), "f": S.last(), "u": ufree}

        def z_unit():
            pair, fr = [], []
            for _ in range(2):
                s, f = ring.take()
                pair.append(s)
                fr += f
            a = split_unit(K, W, xs, xtok, [p.ap for p in pair], fr)
            for hh in range(2):
                b = S(lambda: nc.scalar.activation(zT[:, 512 * hh:512 * hh + 512], pair[hh].ap, ACT.Copy), a, at["z"])
                pair[hh].free = [b]
            return b

        def transform(b):
            yfree = at["y"]
            for q in range(4):
                s, f = ring.take()
                for j in range(2):
                    t = 2 * q + j
                    a = P(lambda: nc.tensor.matmul(s.ap[:, 256 * j:256 * j + 256], zT[:, 128 * t:128 * t + 128],
                                                   cd[:, :], start=True, stop=True), b, t_cd, f, sig=(j == 1))
                zz = S(lambda: nc.scalar.activation(Z[:, 0, 2 * q:2 * q + 2, :, :],
                                                    s.ap.rearrange("p (a m c) -> p a m c", a=2, m=2), ACT.Copy),
                       a, yfree)
                s.free = [zz]
            at["z"] = a
            z0, z1 = Z[:, 0, :, :, :], Z[:, 1, :, :, :]
            V(lambda: nc.vector.tensor_tensor(z1[:, 0:4], z0[:, 0:4], z0[:, 4:8], ALU.add), zz)
            V(lambda: nc.vector.tensor_tensor(z1[:, 4:8], z0[:, 0:4], z0[:, 4:8], ALU.subtract))
            sc = z0[:, 0, :, :]
            V(lambda: nc.vector.tensor_tensor(sc[:, 0], z1[:, 5, 0], z1[:, 5, 1], ALU.add))
            V(lambda: nc.vector.tensor_tensor(sc[:, 1], z1[:, 5, 1], z1[:, 5, 0], ALU.subtract))
            V(lambda: nc.vector.tensor_scalar(z1[:, 5], sc, r2, None, ALU.mult))
            sc = z0[:, 1, :, :]
            V(lambda: nc.vector.tensor_copy(sc[:, 0], z1[:, 6, 1]))
            V(lambda: nc.vector.tensor_scalar(sc[:, 1], z1[:, 6, 0], -1.0, None, ALU.mult))
            V(lambda: nc.vector.tensor_copy(z1[:, 6], sc))
            V(lambda: nc.vector.tensor_tensor(sc[:, 0], z1[:, 7, 1], z1[:, 7, 0], ALU.subtract))
            V(lambda: nc.vector.tensor_tensor(sc[:, 1], z1[:, 7, 1], z1[:, 7, 0], ALU.add))
            V(lambda: nc.vector.tensor_scalar(z1[:, 7, 0], sc[:, 0], r2, None, ALU.mult))
            V(lambda: nc.vector.tensor_scalar(z1[:, 7, 1], sc[:, 1], -r2, None, ALU.mult))
            for hb in (0, 4):
                V(lambda: nc.vector.tensor_tensor(z0[:, hb:hb + 2], z1[:, hb:hb + 2], z1[:, hb + 2:hb + 4], ALU.add))
                V(lambda: nc.vector.tensor_tensor(z0[:, hb + 2:hb + 4], z1[:, hb:hb + 2], z1[:, hb + 2:hb + 4],
                                                  ALU.subtract))
                V(lambda: nc.vector.tensor_copy(z1[:, hb + 3, 0], z0[:, hb + 3, 1]))
                V(lambda: nc.vector.tensor_scalar(z1[:, hb + 3, 1], z0[:, hb + 3, 0], -1.0, None, ALU.mult))
            for hb in (0, 4):
                o = hb // 4
                V(lambda: nc.vector.tensor_tensor(Y[:, o], z0[:, hb], z0[:, hb + 1], ALU.add), yfree)
                V(lambda: nc.vector.tensor_tensor(Y[:, o + 4], z0[:, hb], z0[:, hb + 1], ALU.subtract))
                V(lambda: nc.vector.tensor_tensor(Y[:, o + 2], z0[:, hb + 2], z1[:, hb + 3], ALU.add))
                yt = V(lambda: nc.vector.tensor_tensor(Y[:, o + 6], z0[:, hb + 2], z1[:, hb + 3], ALU.subtract))
            return yt

        def gate_unit():
            pair, fr = [], []
            for _ in range(2):
                s, f = ring.take()
                pair.append(s)
                fr += f
            a = split_unit(K, W, xs, xtok, [p.ap for p in pair], fr)
            for hh in range(2):
                sg = S(lambda: nc.scalar.activation(u[:, 0, 512 * hh:512 * hh + 512], pair[hh].ap, ACT.Silu),
                       a, at["u"])
                pair[hh].free = [sg]
            return sg

        def finish(c, yt, sg):
            fv = fT.rearrange("p (u v) -> p v u", v=8)
            for half in range(2):
                s, f = ring.take()
                for j in range(4):
                    v = 4 * half + j
                    for m in range(2):
                        a = P(lambda: nc.tensor.matmul(s.ap[:, 128 * j:128 * j + 128], Y[:, v, m, :], dft[:, v, m, :],
                                                       start=(m == 0), stop=(m == 1)), yt, t_c, f,
                              sig=(j == 3 and m == 1))
                b = V(lambda: nc.vector.tensor_copy(fv[:, 4 * half:4 * half + 4, :],
                                                    s.ap.rearrange("p (v u) -> p v u", v=4)), a, at["f"])
                s.free = [b]
            at["y"] = [a, yt]
            for hh in range(2):
                s, f = ring.take()
                at["f"] = P(lambda: nc.tensor.matmul(s.ap, wf[:, 128 * c:128 * c + 128],
                                                     fT[:, 512 * hh:512 * hh + 512], start=True, stop=True),
                            b, t_wf, f)
                at["u"] = V(lambda: nc.vector.scalar_tensor_tensor(
                    mixT[:, 4 + c, 512 * hh:512 * hh + 512], s.ap, bf[:, c:c + 1],
                    u[:, 0, 512 * hh:512 * hh + 512], ALU.add, ALU.mult), at["f"], sg)
                s.free = [at["u"]]

        zt = z_unit()
        for c in range(4):
            yt = transform(zt)
            sg = gate_unit()
            if c < 3:
                zt = z_unit()
            finish(c, yt, sg)
        inner.close()
        for q in (S, V, K.D):
            q.wait(P.last(), V.last(), S.last())
        slots = ring.slots
        ms = K.sb(st, "ms", [128, 2, 8, 1024], F32R)
        y = K.sb(st, "y3", [128, 8, 1024])
        W = SplitWeights(K, st, [A["wo3"][hh][k] for hh in range(2) for k in range(8)], 3, 512)
        pg = K.sb(st, "pg", [128, 1024])
        pt = K.dma(pg[:, :], A["post3"])
        sq = K.sb(st, "sq3", [128, 512])
        mtoks = {}

        def left(k):
            for i in (k, k + 1):
                if i < 8 and i not in mtoks:
                    mtoks[i] = split(K, mixT[:, i, :], ms[:, 0, i, :], ms[:, 1, i, :])
            return (ms[:, 0, k, :], ms[:, 1, k, :]), mtoks[k]

        left.n = 8

        def first(t, ap, a):
            yy = y[:, t, 0:512]
            b = S(lambda: nc.scalar.activation(sq[:, :], ap, ACT.Square, accum_out=ss[:, t, 0:1]), a)
            return [V(lambda: nc.vector.tensor_tensor(yy, ap, pg[:, 0:512], ALU.mult), b, pt)]

        def second(t, ap, a):
            b = S(lambda: nc.scalar.activation(sq[:, :], ap, ACT.Square, accum_out=ss[:, t, 1:2]), a)
            r = ss[:, t, 0:1]
            c = V(lambda: nc.vector.tensor_tensor(y[:, t, 512:1024], ap, pg[:, 512:1024], ALU.mult), b)
            b = V(lambda: nc.vector.tensor_tensor(r, r, ss[:, t, 1:2], ALU.add), b)
            b = V(lambda: nc.vector.tensor_scalar(r, r, 1.0 / 1024, 1e-6, ALU.mult, ALU.add))
            b = S(lambda: nc.scalar.activation(r, r, ACT.Sqrt), b)
            V(lambda: nc.vector.reciprocal(r, r), b)
            yy = y[:, t, :]
            b = V(lambda: nc.vector.scalar_tensor_tensor(yy, yy, r, h[:, t, :], ALU.mult, ALU.add))
            K.stored(K.dma(A["out"][t], yy, b))
            return [c]

        rows_product(K, slots, left, W, first)
        rows_product(K, slots, left, W, second)




def take2(ring):
    pair, fr = [], []
    for _ in range(2):
        s, f = ring.take()
        pair.append(s)
        fr += f
    return pair, fr


def rows_steps(K, W, xs, xtok, ring, ident, tmp, dst, c, out):
    nc, P, S = K.nc, K.P, K.S
    S.wait(K.V.last())
    yield from unit_to(K, W, xs, xtok, ring, out, "tmp", tmp, ACT.Copy, 1.0, out.get("turned"))
    for half in range(2):
        s, f = ring.take()
        for j in range(4):
            t = 4 * half + j
            a = P(lambda: nc.tensor.transpose(s.ap[:, 128 * j:128 * j + 128], tmp[:, 128 * t:128 * t + 128], ident),
                  out["tmp"], f, sig=(j == 3))
        vt = S(lambda: nc.scalar.activation(dst[:, 4 * half:4 * half + 4, 128 * c:128 * c + 128],
                                            s.ap.rearrange("p (j c) -> p j c", j=4), ACT.Copy), a)
        s.free = [vt]
    out["turned"], out["v"] = a, vt
    yield


def unit_banks(K, W, xs, xtok, ring, got, rows=128):
    pair, fr = take2(ring)
    (wh, wl), tok = W.get()
    for k in range(8):
        for h in range(2):
            sl = slice(512 * h, 512 * h + 512)
            a = products(K, pair[h].ap[0:rows, :], (wh[:, k, 0:rows], wl[:, k, 0:rows]),
                         (xs[:, 0, k, sl], xs[:, 1, k, sl]), k == 0, k == 7, tok, xtok[k], fr, sig=(k == 7))
        if k < 7:
            yield
    W.done(a)
    got += [pair, a]


def unit_to(K, W, xs, xtok, ring, out, name, dst, func, scale=1.0, token=None, rows=128):
    nc = K.nc
    got = []
    yield from unit_banks(K, W, xs, xtok, ring, got, rows)
    pair, a = got
    for h in range(2):
        e = K.S(lambda: nc.scalar.activation(dst[:, 512 * h:512 * h + 512], pair[h].ap[0:rows, :], func, scale=scale),
                a, token)
        pair[h].free = [e]
    out[name] = e
    yield


def stick_breaking(K, C, ring, oring, p, q, k, vn, be, nb, wt, pr, yT, qk, vt, gt):
    nc, P, V, S = K.nc, K.P, K.V, K.S
    avr, tpr = [None, None], [None, None]
    work = [(h, i) for h in range(2) for i in range(8)]
    at = {}

    def scores(n):
        h, i = work[n]
        b = n % 2
        r = slice(64 * h, 64 * h + 64)
        L = 128 * (i + 1)
        for c0 in range(0, L, 512):
            w = min(512, L - c0)
            s, f = ring.take()
            a = P(lambda: nc.tensor.matmul(s.ap[:, 0:w], q[r, 128 * i:128 * i + 128], k[r, c0:c0 + w],
                                           start=True, stop=True), qk, f)
            S(lambda: nc.scalar.activation(be[:, b, c0:c0 + w], s.ap[:, 0:w], ACT.Sigmoid), a, tpr[b])
            a = S(lambda: nc.scalar.activation(nb[:, b, c0:c0 + w], s.ap[:, 0:w], ACT.Sigmoid, scale=-1.0),
                  tpr[b])
            s.free = [a]
        V(lambda: nc.vector.tensor_tensor(nb[:, b, L - 128:L], nb[:, b, L - 128:L], C.ge, ALU.max), a)
        V(lambda: nc.vector.tensor_tensor(be[:, b, L - 128:L], be[:, b, L - 128:L], C.lt, ALU.mult))
        V(lambda: nc.vector.memset(pr[:, b, L:L + 1], 1.0))
        V(lambda: nc.vector.tensor_tensor_scan(pr[:, b, 0:L][:, ::-1], nb[:, b, 0:L][:, ::-1],
                                               nb[:, b, 0:L][:, ::-1], 1.0, ALU.mult, ALU.bypass))
        at[n] = V(lambda: nc.vector.tensor_tensor(be[:, b, 0:L], be[:, b, 0:L], pr[:, b, 1:L + 1], ALU.mult))

    def turn(n):
        h, i = work[n]
        b = n % 2
        wtok = at[n]
        evs = []
        for c0 in range(0, i + 1, 4):
            m = min(4, i + 1 - c0)
            s, f = ring.take()
            for j in range(m):
                t = P(lambda: nc.tensor.transpose(s.ap[:, 128 * j:128 * j + 128],
                                                  be[:, b, 128 * (c0 + j):128 * (c0 + j) + 128], C.ident),
                      wtok, f, sig=(j == m - 1))
            d, x = wt[:, b, 128 * c0:128 * (c0 + m)], s.ap[:, 0:128 * m]
            if c0:
                ev = S(lambda: nc.scalar.activation(d, x, ACT.Copy), t, avr[b])
            else:
                ev = V(lambda: nc.vector.tensor_copy(d, x), t, avr[b])
            s.free = [ev]
            evs.append(ev)
        tpr[b] = [t, wtok]
        at[n] = evs

    def values(n):
        h, i = work[n]
        b = n % 2
        r = slice(64 * h, 64 * h + 64)
        if i % 4 == 0:
            at["ob"] = oring.take()
        ob, f = at["ob"]
        for j in range(i + 1):
            a = P(lambda: nc.tensor.matmul(ob.ap[r, 128 * (i % 4):128 * (i % 4) + 128], vn[:, j, r],
                                           wt[:, b, 128 * j:128 * j + 128], start=(j == 0), stop=(j == i)),
                  at[n], vt, f, sig=(j == i))
        avr[b] = a
        if i % 4 == 3:
            c0 = 512 * (i // 4)
            y = yT[r, p, c0:c0 + 512]
            e = V(lambda: nc.vector.tensor_tensor(y, ob.ap[r, :], y, ALU.mult), a, gt)
            ob.free = [e]

    for n in range(18):
        if n < 16:
            scores(n)
            yield
        if 0 <= n - 1 < 16:
            turn(n - 1)
            yield
        if 0 <= n - 2 < 16:
            values(n - 2)
            yield


def recurrence(K, B, C, ring, nh, dk, q, k, lf, toks, V_n, vcol, vtok, yT, yi, gtok, gain):
    nc, P, V, S = K.nc, K.P, K.V, K.S
    V.wait(P.last(), S.last())
    S.wait(P.last(), V.last())
    vw = 64 * nh
    E, Xs, acc, Kn, on, dec, rs = B.E, B.X, B.acc, B.Kn, B.on, B.dec, B.rs
    St = B.St[:, 0:8 * vw].rearrange("p (t v) -> p t v", t=8)
    cum = B.cum
    per = 4 // nh
    for n in range(8):
        sl = slice(128 * n, 128 * n + 128)
        ct = V(lambda: nc.vector.tensor_tensor_scan(cum[:, sl], C.one.to_broadcast([128, 128]), lf[:, sl], 0.0, ALU.mult,
                                                    ALU.add), toks)
    a4 = acc[:, 0:nh * 1024].rearrange("p (g j s) -> p g j s", j=4, s=128)
    xr = [None, None]
    ready = {}

    def blocks(x, lev):
        return x.rearrange("p (n b) -> p n b", b=2 << lev)

    def distances(lev):
        if lev > 6:
            return
        X = Xs[:, lev % 2, :]
        c3 = blocks(cum, lev)
        m = c3[:, :, (1 << lev) - 1:1 << lev].to_broadcast([128, 512 >> lev, 2 << lev])
        t = V(lambda: nc.vector.tensor_tensor(blocks(X, lev), c3, m, ALU.subtract), xr[lev % 2])
        t = S(lambda: nc.scalar.activation(X, X, ACT.Abs), t)
        ready[lev] = S(lambda: nc.scalar.activation(X, X, ACT.Exp, scale=-1.0), t)

    def weigh(lev):
        if lev > 6:
            return
        Bk = 1 << lev
        X3 = blocks(Xs[:, lev % 2, :], lev)
        V(lambda: nc.vector.tensor_tensor(X3[:, :, 0:Bk], X3[:, :, 0:Bk], blocks(k, lev)[:, :, 0:Bk], ALU.mult),
          ready[lev])
        ready[lev] = V(lambda: nc.vector.tensor_tensor(X3[:, :, Bk:], X3[:, :, Bk:], blocks(q, lev)[:, :, Bk:],
                                                       ALU.mult))

    for lev in range(-1, 7):
        if lev < 0:
            xt = toks
            left, right = k, q
        else:
            b = lev % 2
            left = right = Xs[:, b, :]
            xt = ready[lev]
        distances(lev + 1)
        for grp in range(2 * nh):
            if grp == 2 * nh - 2:
                weigh(lev + 1)
            s, f = ring.take()
            h = grp // 2
            for j in range(4):
                t = 4 * (grp % 2) + j
                r = slice(dk * h, dk * h + dk)
                a = P(lambda: nc.tensor.matmul(s.ap[:, 128 * j:128 * j + 128], left[r, 128 * t:128 * t + 128],
                                               right[r, 128 * t:128 * t + 128], start=True, stop=True,
                                               tile_position=(dk * h, 0)),
                      xt, f, sig=(j == 3))
            dst = a4[:, grp]
            src = s.ap.rearrange("p (j s) -> p j s", s=128)
            if lev < 0:
                im = C.ident.unsqueeze(1).to_broadcast([128, 4, 128])
                e = V(lambda: nc.vector.tensor_tensor(dst, src, im, ALU.mult), a)
            else:
                lm = C.lmask[:, lev, :].unsqueeze(1).to_broadcast([128, 4, 128])
                e = V(lambda: nc.vector.copy_predicated(dst, lm, src), a)
            s.free = [e]
            yield
        if lev >= 0:
            xr[b] = a
    acct = e
    c3 = cum.rearrange("p (n b) -> p n b", b=128)
    last = c3[:, :, 127:128]
    dt = S(lambda: nc.scalar.activation(dec, c3[:, :, 127], ACT.Exp), ct)
    t = V(lambda: nc.vector.tensor_tensor(E.rearrange("p (n b) -> p n b", b=128), last.to_broadcast([128, 8, 128]), c3,
                                          ALU.subtract))
    t = S(lambda: nc.scalar.activation(E, E, ACT.Exp), t)
    kd = V(lambda: nc.vector.tensor_tensor(E, E, k, ALU.mult), t)
    Qc = Xs[:, 0, :]
    t = S(lambda: nc.scalar.activation(Qc, cum, ACT.Exp), xr[0], xr[1])
    qc = V(lambda: nc.vector.tensor_tensor(Qc, Qc, q, ALU.mult), t)
    for half in range(2):
        s, f = ring.take()
        for j in range(4):
            t = 4 * half + j
            a = P(lambda: nc.tensor.transpose(s.ap[:, 128 * j:128 * j + 128], E[:, 128 * t:128 * t + 128], C.ident),
                  kd, f, sig=(j == 3))
        e = S(lambda: nc.scalar.activation(Kn[:, 512 * half:512 * half + 512], s.ap, ACT.Copy), a)
        s.free = [e]
    kn = e
    yield
    bm = C.bd64 if nh == 2 else C.bd32
    tokS = None
    tmp = B.tmp
    for t in range(7):
        s, f = ring.take()
        a = P(lambda: nc.tensor.matmul(s.ap[:, 0:vw], Kn[:, 128 * t:128 * t + 128], V_n[:, t, vcol:vcol + vw],
                                       start=True, stop=True), kn, vtok, f)
        if t == 0:
            tokS = V(lambda: nc.vector.tensor_tensor(St[:, 1, 0:vw], s.ap[:, 0:vw], bm, ALU.mult), a)
        else:
            V(lambda: nc.vector.tensor_tensor(tmp[:, 0:vw], s.ap[:, 0:vw], bm, ALU.mult), a)
            tokS = V(lambda: nc.vector.scalar_tensor_tensor(St[:, t + 1, 0:vw], St[:, t, 0:vw], dec[:, t:t + 1],
                                                            tmp[:, 0:vw], ALU.mult, ALU.add), dt)
        s.free = [tokS]
        yield
    tpb = 512 // vw
    o3 = on[:, 0:8 * vw]
    for grp in range(8 // tpb):
        s, f = ring.take()
        for j in range(tpb):
            t = grp * tpb + j
            if t > 0:
                P(lambda: nc.tensor.matmul(s.ap[:, vw * j:vw * j + vw], Qc[:, 128 * t:128 * t + 128],
                                           St[:, t, 0:vw], start=True, stop=False, skip_group_check=True),
                  qc, tokS, acct, f, sig=False)
            for h in range(nh):
                idx = 8 * h + t
                a = P(lambda: nc.tensor.matmul(s.ap[:, vw * j + 64 * h:vw * j + 64 * h + 64],
                                               acc[:, 128 * idx:128 * idx + 128],
                                               V_n[:, t, vcol + 64 * h:vcol + 64 * h + 64],
                                               start=(t == 0 and h == 0), stop=(h == nh - 1), skip_group_check=True),
                      acct, vtok, qc, f, sig=(j == tpb - 1 and h == nh - 1))
        e = S(lambda: nc.scalar.activation(on[:, 512 * grp:512 * grp + 512], s.ap, ACT.Copy), a)
        s.free = [e]
        yield
    n = 8 * nh
    e2 = S(lambda: nc.scalar.activation(B.sq[:, 0:8 * vw], on[:, 0:8 * vw], ACT.Square), a)
    V(lambda: nc.vector.tensor_reduce(rs[:, 0:n], B.sq[:, 0:8 * vw].rearrange("p (n v) -> p n v", v=64), AX.X,
                                      ALU.add), e2)
    b = V(lambda: nc.vector.tensor_scalar(rs[:, 0:n], rs[:, 0:n], 1.0 / 64, 1e-5, ALU.mult, ALU.add))
    b = S(lambda: nc.scalar.activation(rs[:, 0:n], rs[:, 0:n], ACT.Sqrt), b)
    V(lambda: nc.vector.reciprocal(rs[:, 0:n], rs[:, 0:n]), b)
    ov = o3.rearrange("p (n v) -> p n v", v=64)
    b = V(lambda: nc.vector.tensor_tensor(ov, ov, rs[:, 0:n].unsqueeze(2).to_broadcast([128, n, 64]), ALU.mult))
    for c in range(nh // 2):
        for half in range(2):
            s, f = ring.take()
            for j in range(4):
                t = 4 * half + j
                a = P(lambda: nc.tensor.transpose(s.ap[:, 128 * j:128 * j + 128],
                                                  on[:, vw * t + 128 * c:vw * t + 128 * c + 128], C.ident),
                      b, f, sig=(j == 3))
            e = V(lambda: nc.vector.scalar_tensor_tensor(yT[:, yi + c, 512 * half:512 * half + 512], s.ap,
                                                         gain[:, c:c + 1], yT[:, yi + c, 512 * half:512 * half + 512],
                                                         ALU.mult, ALU.mult), a, gtok)
            s.free = [e]
        yield


def log_sigmoid(K, E, src, stok, bias, dst):
    nc, V, S = K.nc, K.V, K.S
    for h in range(2):
        sl = slice(512 * h, 512 * h + 512)
        e = S(lambda: nc.scalar.activation(E[:, sl], src[h].ap, ACT.Identity, bias=bias), stok, V.last())
        src[h].free = src[h].free + [e]
    S(lambda: nc.scalar.activation(dst, E, ACT.Abs))
    S(lambda: nc.scalar.activation(dst, dst, ACT.Exp, scale=-1.0))
    e = S(lambda: nc.scalar.activation(dst, dst, ACT.Ln, bias=1.0))
    return V(lambda: nc.vector.scalar_tensor_tensor(dst, E, 0.0, dst, ALU.min, ALU.subtract), e)


class Bufs:
    pass


def run(gen):
    for _ in gen:
        pass


def block1(K, C, h, xT, xtok, A, banks):
    nc, P, V, S = K.nc, K.P, K.V, K.S
    ring = Ring(banks)
    with ExitStack() as st:
        cols = K.sb(st, "cols1", [128, 16])
        one = K.sb(st, "one", [128, 1])
        C.one = one[:, :]
        V(lambda: nc.vector.memset(one[:, :], 1.0))
        ct = K.dma(cols[:, :], A["c1"])
        hg, cg, cb, lbl = cols[:, 0:2], cols[:, 2:4], cols[:, 4:5], cols[:, 5:7]
        lb, oml, z1 = cols[:, 7:9], cols[:, 9:11], cols[:, 11:13]
        yT = K.sb(st, "yT", [128, 6, 1024])
        T = xT
        T2 = K.sb(st, "b1t", [128, 2, 1024])
        xs = K.sb(st, "xs", [128, 2, 8, 1024], F32R)
        xtok = [split(K, xT[:, i, :], xs[:, 0, i, :], xs[:, 1, i, :], xtok[i]) for i in range(8)]
        V(lambda: nc.vector.tensor_tensor(z1, lbl, lbl, ALU.subtract), ct)
        t = V.last()
        t = S(lambda: nc.scalar.activation(z1, z1, ACT.Exp), t)
        V(lambda: nc.vector.reciprocal(lb, z1), t)
        V(lambda: nc.vector.tensor_tensor(z1, z1, lb, ALU.mult))
        V(lambda: nc.vector.tensor_tensor(lb, z1, z1, ALU.subtract))
        lbt = V(lambda: nc.vector.tensor_scalar(oml, lb, -1.0, 1.0, ALU.mult, ALU.add))
        W = SplitWeights(K, st, [A["w1"][i] for i in range(23)] + [A["wg"][i][:, 0:1024] for i in range(24)]
                         + [A["wo1"][i] for i in range(8)])
        U = Weights(K, st, [A["wg"][i][:, 1024:1280] for i in range(24)], 2, 256)
        load_masks(K, st, A, C)
        tri = K.sb(st, "tri", [128, 640])
        V.wait(K.dma(tri[:, :], A["cc"][:, 128:768]))
        C.ge, C.lt, C.bd32 = tri[:, 0:128], tri[:, 128:256], tri[:, 384:640]
        slots = [h[:, i, :] for i in range(8)] + [T[:, i, :] for i in range(8)] + [T2[:, i, :] for i in range(2)]
        cells = lambda ap: ap.rearrange("p (t v) -> p t v", t=8)
        E = slots[17]
        RF, RM = Ring.of(ring.slots[0:3]), Ring.of(ring.slots[3:8])

        def sb_units(p, q, k, v, out):
            yield from unit_to(K, W, xs, xtok, RF, out, "q", q, ACT.Copy, 0.125)
            yield from unit_to(K, W, xs, xtok, RF, out, "k", k, ACT.Copy)
            yield from rows_steps(K, W, xs, xtok, RF, C.ident, E, cells(v), 0, out)
            yield from unit_to(K, W, xs, xtok, RF, out, "g", yT[:, p, :], ACT.Silu)

        def hgrn_units(p, q, kk, lf, v, out):
            got = []
            yield from unit_banks(K, W, xs, xtok, RF, got)
            pair, a = got
            for hh in range(2):
                e = S(lambda: nc.scalar.activation(kk[:, 512 * hh:512 * hh + 512], pair[hh].ap, ACT.Sigmoid,
                                                   scale=-1.0), a)
                pair[hh].free = [e]
            V(lambda: nc.vector.tensor_scalar(kk, kk, oml[:, p:p + 1], None, ALU.mult), e, lbt)
            log_sigmoid(K, E, pair, a, 0.0, lf)
            V(lambda: nc.vector.tensor_scalar(E, E, -1.0, 60.0, ALU.mult, ALU.min))
            t = S(lambda: nc.scalar.activation(E, E, ACT.Exp), V.last())
            t = V(lambda: nc.vector.tensor_scalar(E, E, lb[:, p:p + 1], None, ALU.mult), t)
            t = S(lambda: nc.scalar.activation(E, E, ACT.Ln, bias=1.0), t)
            out["lf"] = V(lambda: nc.vector.tensor_tensor(lf, lf, E, ALU.add), t)
            yield
            yield from unit_to(K, W, xs, xtok, RF, out, "q", q, ACT.Copy)
            yield from rows_steps(K, W, xs, xtok, RF, C.ident, E, cells(v), 0, out)
            yield from unit_to(K, W, xs, xtok, RF, out, "g", yT[:, 2 + p, :], ACT.Silu)

        def gla_units(q, kk, lf, v, out):
            yield from unit_to(K, W, xs, xtok, RF, out, "q", q, ACT.Copy, 32 ** -0.5)
            yield from unit_to(K, W, xs, xtok, RF, out, "k", kk, ACT.Copy)
            for c in range(2):
                yield from rows_steps(K, W, xs, xtok, RF, C.ident, E, v, c, out)
            for c in range(2):
                yield from unit_to(K, W, xs, xtok, RF, out, "g", yT[:, 4 + c, :], ACT.Silu)
            cr = E[0:16, :]
            S.wait(V.last())
            yield from unit_to(K, W, xs, xtok, RF, out, "cr", cr, ACT.Copy, 1.0, None, 16)
            pair, fr = take2(RF)
            for hh in range(2):
                a = P(lambda: nc.tensor.matmul(pair[hh].ap, w2[:, :], cr[:, 512 * hh:512 * hh + 512], start=True,
                                               stop=True), out["cr"], w2t, fr)
            log_sigmoid(K, E, pair, a, cb, lf)
            out["lf"] = V(lambda: nc.vector.tensor_scalar(lf, lf, 1.0 / 16, None, ALU.mult))
            yield

        w2 = K.sb(st, "w2", [16, 128])
        w2t = K.dma(w2[:, :], A["w2"])
        S.wait(ct)
        with ExitStack() as s3:
            pr = K.sb(s3, "pr", [128, 2, 1025])
            be, nb, wt = h[:, 0:2, :], h[:, 2:4, :], h[:, 4:6, :]
            sets = [(slots[6], slots[7], slots[8]), (slots[9], slots[10], slots[16])]
            o0, o1, hg0 = {}, {}, {}
            run(sb_units(0, *sets[0], o0))
            run_sb = lambda p, o: stick_breaking(K, C, Ring.of(RM.slots[0:3]), Ring.of(RM.slots[3:5]), p, sets[p][0],
                                                 sets[p][1], cells(sets[p][2]), be, nb, wt, pr, yT, o["k"], o["v"],
                                                 o["g"])
            weave(run_sb(0, o0), sb_units(1, *sets[1], o1))
            V.wait(P.last(), S.last())
            S.wait(P.last(), V.last())
            setA = (slots[11], slots[12], slots[13], slots[14])
            weave(run_sb(1, o1), hgrn_units(0, *setA, hg0))
        B = Bufs()
        B.cum, B.E, B.X = slots[0], slots[1], h[:, 2:4, :]
        B.acc = h[:, 4:8, :].rearrange("p a n -> p (a n)")
        B.sq = B.X.rearrange("p a n -> p (a n)")
        B.on = h[:, 0:2, :].rearrange("p a n -> p (a n)")
        B.St = T[:, 1:3, :].rearrange("p a n -> p (a n)")
        B.Kn = slots[8]
        tmp = K.sb(st, "rtmp", [128, 256])
        sm = K.sb(st, "rsm", [128, 64])
        B.tmp, B.dec, B.rs = tmp, sm[:, 0:8], sm[:, 8:40]
        setB = (slots[6], slots[7], slots[10], slots[16])
        hg1, gl = {}, {}
        V.wait(P.last(), S.last())
        S.wait(P.last(), V.last())
        weave(recurrence(K, B, C, RM, 2, 64, setA[0], setA[1], setA[2], [hg0["q"], hg0["lf"]], cells(setA[3]), 0,
                         hg0["v"], yT, 2, hg0["g"], hg[:, 0:1]), hgrn_units(1, *setB, hg1))
        vg = T[:, 6:8, :].rearrange("p a n -> p (a n)")
        V.wait(P.last(), S.last())
        S.wait(P.last(), V.last())
        weave(recurrence(K, B, C, RM, 2, 64, setB[0], setB[1], setB[2], [hg1["q"], hg1["lf"]], cells(setB[3]), 0,
                         hg1["v"], yT, 3, hg1["g"], hg[:, 1:2]),
              gla_units(setA[0], setA[1], setA[2], cells(vg), gl))
        with ExitStack() as s2:
            few = K.sb(s2, "merged", [128, 3, 1024])
            merged = [few[:, i, :] for i in range(3)] + [slots[16]] + slots[8:12]
            sg = E
            sgf = [None, None]

            def merge(br, ring, ds=range(8)):
                for d in ds:
                    got = []
                    yield from unit_banks(K, W, xs, xtok, ring, got)
                    pair, a = got
                    gt = [None, None]
                    for hh in range(2):
                        gt[hh] = S(lambda: nc.scalar.activation(sg[:, 512 * hh:512 * hh + 512], pair[hh].ap,
                                                                ACT.Sigmoid), a, sgf[hh])
                        pair[hh].free = [gt[hh]]
                    pair, fr = take2(ring)
                    w, tok = U.get()
                    for k in range(2):
                        for hh in range(2):
                            a = P(lambda: nc.tensor.matmul(pair[hh].ap, w[:, k, :],
                                                           yT[:, 2 * br + k, 512 * hh:512 * hh + 512],
                                                           start=(k == 0), stop=(k == 1)), fr, tok, sig=(k == 1))
                    U.done(a)
                    for hh in range(2):
                        m = merged[d][:, 512 * hh:512 * hh + 512]
                        g = sg[:, 512 * hh:512 * hh + 512]
                        t = V(lambda: nc.vector.tensor_tensor(m if br == 0 else g, pair[hh].ap, g, ALU.mult), a,
                              gt[hh])
                        pair[hh].free = [t]
                        if br:
                            t = V(lambda: nc.vector.tensor_tensor(m, m, g, ALU.add))
                        sgf[hh] = t
                    yield

            P.wait(V.last())
            weave(recurrence(K, B, C, RM, 4, 32, setA[0], setA[1], setA[2], [gl["q"], gl["k"], gl["lf"]], cells(vg), 0,
                             gl["v"], yT, 4, gl["g"], cg), merge(0, RF, range(4)))
            free = [P.last(), V.last(), S.last()]
            ht = K.dma(h[:, :, :], A["x"], *free)
            rows = T[:, 4:6, :]
            rt = K.dma(rows, A["rows1"])
            P.wait(V.last())
            V.wait(*free)
            run(merge(0, ring, range(4, 8)))
            run(merge(1, ring))
            run(merge(2, ring))
            stt = K.sb(s2, "st1", [128, 8, 14])
            outs = ring.slots
            mtok = {}
            S.wait(P.last())
            V.wait(P.last())
            for hh in range(2):
                for k in range(8):
                    for i in (k, k + 1):
                        if i < 8 and i not in mtok:
                            mtok[i] = split(K, merged[i], xs[:, 0, i, :], xs[:, 1, i, :], V.last())
                    if k % 2 == 0:
                        (wh, wl), wt = W.get()
                    ws = slice(4 * (k % 2), 4 * (k % 2) + 4)
                    flat = lambda x: x[:, ws, :].rearrange("p k c -> p (k c)")
                    for t in range(8):
                        sl = slice(128 * t, 128 * t + 128)
                        a = products(K, outs[t].ap, (xs[:, 0, k, sl], xs[:, 1, k, sl]), (flat(wh), flat(wl)),
                                     k == 0, k == 7, mtok[k], wt, outs[t].free, sig=(k == 7 or t == 7))
                        if k == 7:
                            hs = h[:, t, 512 * hh:512 * hh + 512]
                            e = V(lambda: nc.vector.scalar_tensor_tensor(hs, hs, float(2 ** 0.25), outs[t].ap,
                                                                         ALU.mult, ALU.add), a, ht)
                            outs[t].free = [e]
                            V(lambda: nc.vector.bn_stats(stt[:, t, 6 * hh:6 * hh + 6], hs))
                    if k % 2:
                        W.done(a)
            for t in range(8):
                V(lambda: nc.vector.bn_aggr(stt[:, t, 12:14], stt[:, t, 0:12]))
            e = V(lambda: nc.vector.tensor_scalar(stt[:, :, 13], stt[:, :, 13], 1e-5, None, ALU.add))
            e = S(lambda: nc.scalar.activation(stt[:, :, 13], stt[:, :, 13], ACT.Sqrt), e)
            V(lambda: nc.vector.reciprocal(stt[:, :, 13], stt[:, :, 13]), e)
            b = V(lambda: nc.vector.scalar_tensor_tensor(stt[:, :, 12], stt[:, :, 12], -1.0, stt[:, :, 13], ALU.mult,
                                                         ALU.mult))
            for t in range(8):
                c = S(lambda: nc.scalar.activation(h[:, t, :], h[:, t, :], ACT.Identity, scale=stt[:, t, 13:14],
                                                   bias=stt[:, t, 12:13]), b)
                V(lambda: nc.vector.tensor_tensor(h[:, t, :], h[:, t, :], rows[:, 0, :], ALU.mult), rt, c)
                e = V(lambda: nc.vector.tensor_tensor(h[:, t, :], h[:, t, :], rows[:, 1, :], ALU.add))
            K.fence()
    return e



EC = float(np.exp(-0.5))


def steps(gen, n):
    for _ in range(n):
        try:
            next(gen)
        except StopIteration:
            return
        yield


def unit_steps(K, W, xT, xtok, ring, out):
    pair, fr = take2(ring)
    w, tok = W.get()
    for k in range(8):
        for h in range(2):
            t = K.P(lambda: K.nc.tensor.matmul(pair[h].ap, w[:, k, :], xT[:, k, 512 * h:512 * h + 512],
                                               start=(k == 0), stop=(k == 7)),
                    tok, xtok, fr, sig=(k == 7 and h == 1))
        yield
    W.done(t)
    out.append((pair, t))


def rwkv(K, C, W, xT, xtok, A, banks, st, cols, ctok):
    nc, P, V, S, G = K.nc, K.P, K.V, K.S, K.G
    RU, RG, RC, RY = Ring(banks[0:3]), Ring(banks[3:6]), Ring(banks[6:7]), Ring(banks[7:8])
    sb = lambda n, s, d=F32: K.sb(st, n, s, d)
    AR = sb("AR", [128, 2, 16, 2, 64])
    vT = sb("vT", [128, 2, 1024])
    Bc = sb("Bc", [128, 2, 1024])
    Kc = sb("Kc", [128, 2, 1024])
    bon = sb("bon", [128, 3, 1024])
    gf_ = sb("gf", [128, 2, 1024])
    pc = sb("pc", [128, 2, 16])
    raw = sb("raw", [128, 1028])
    r = sb("r", [128, 1024])
    k = sb("k", [128, 1024])
    sg = sb("sg2", [128, 1024])
    cum = sb("cum2", [128, 1024])
    ex = sb("ex", [128, 1024])
    av = sb("av", [128, 1024])
    kk = sb("kk", [128, 1024])
    D = sb("D", [128, 1024])
    lo = sb("lo", [128, 1024])
    wup = sb("wup", [128, 1024])
    MB_ = sb("mb_", [128, 4, 4, 2, 64])
    MK_ = sb("mk_", [128, 4, 4, 2, 64])
    XM_ = sb("X", [128, 2, 2, 4, 64])
    XT = sb("XT", [128, 4, 4, 64])
    Bn, Kn, Vn = sb("Bn", [128, 4, 4, 64]), sb("Kn", [128, 4, 4, 64]), sb("Vn", [128, 4, 4, 64])
    ST = sb("ST", [128, 2, 64])
    zu = sb("zu", [128, 3, 64])
    Y2 = sb("Y", [128, 2, 16, 64])
    ys = sb("ys", [128, 48])
    mu, w0, a0, kkc, kac, rkc, lnw, lnb = [cols[:, 8 * i:8 * i + 8] for i in range(8)]
    mur, muk, muv = cols[:, 64:72], cols[:, 72:80], cols[:, 80:88]
    mulo = cols[:, 88:89]
    omka = cols[:, 96:104]
    z = V(lambda: nc.vector.memset(raw[:, :], 0.0))
    for q in (S, G, P):
        q.wait(z)
    V(lambda: nc.vector.tensor_scalar(omka, kac, -1.0, 1.0, ALU.mult, ALU.add), ctok)
    wt = K.dma(wup[:, :], A["wup2"])
    state = {"pairfree": [None, None], "gfree": [None] * 4, "s1": [None, None], "raw": None, "y": None, "st": None,
             "gn": 0, "tmpf": None, "fin": None, "yfree": [None, None]}

    def shift(pair, a, mucol, dst, dfree):
        for h in range(2):
            e = S(lambda: nc.scalar.activation(raw[:, 1 + 512 * h:513 + 512 * h], pair[h].ap, ACT.Copy), a,
                  state["raw"])
            pair[h].free = [e]
        V(lambda: nc.vector.tensor_tensor(D[:, :], raw[:, 0:1024], raw[:, 1:1025], ALU.subtract), e, dfree)
        state["raw"] = V(lambda: nc.vector.scalar_tensor_tensor(dst, D[:, :], mucol, raw[:, 1:1025], ALU.mult,
                                                                ALU.add), ctok)
        return state["raw"]

    def prep_lo():
        out = []
        yield from unit_steps(K, W, xT, xtok, RU, out)
        t = shift(*out[0], mulo, lo[:, :], None)
        state["lo"] = S(lambda: nc.scalar.activation(lo[0:64, :], lo[0:64, :], ACT.Tanh), t)

    def both(lhs, rhs, toks):
        pair, fr = take2(RU)
        for h in range(2):
            a = P(lambda: nc.tensor.matmul(pair[h].ap, lhs, rhs[:, 512 * h:512 * h + 512], start=True, stop=True),
                  toks, fr)
        return pair, a

    def evac(pair, a, dst, func, scale=1.0, bias=0.0, *toks):
        for h in range(2):
            if func == ACT.Copy:
                e = S(lambda: nc.scalar.activation(dst[:, 512 * h:512 * h + 512], pair[h].ap, func, scale=scale), a,
                      *toks)
            else:
                e = S(lambda: nc.scalar.activation(dst[:, 512 * h:512 * h + 512], pair[h].ap, func, scale=scale,
                                                   bias=bias), a, *toks)
            pair[h].free = [e]
        return e

    def prep(p):
        b = p % 2
        pf = state[("pf1", p - 2)] if p > 1 else None
        out = []
        yield from unit_steps(K, W, xT, xtok, RU, out)
        rt = shift(*out[-1], mur[:, p:p + 1], r[:, :], None)
        yield
        yield from unit_steps(K, W, xT, xtok, RU, out)
        kt = shift(*out[-1], muk[:, p:p + 1], k[:, :], None)
        yield
        V(lambda: nc.vector.tensor_scalar(kk[:, :], k[:, :], kkc[:, p:p + 1], None, ALU.mult))
        t = S(lambda: nc.scalar.activation(ex[:, :], kk[:, :], ACT.Square), V.last(), state["tmpf"])
        yield from unit_steps(K, W, xT, xtok, RU, out)
        vt = shift(*out[-1], muv[:, p:p + 1], vT[:, b, :], pf)
        yield
        s, f = RU.take()
        for j in range(8):
            a = P(lambda: nc.tensor.matmul(s.ap[:, 2 * j:2 * j + 2], ex[:, 128 * j:128 * j + 128], C.bd64[:, 0:65:64],
                                           start=True, stop=True), t, f, sig=(j == 7))
        n16 = ys[:, 32:48]
        t = S(lambda: nc.scalar.activation(n16, s.ap[:, 0:16], ACT.Sqrt), a)
        s.free = [t]
        V(lambda: nc.vector.tensor_scalar(n16, n16, 1e-12, None, ALU.max), t)
        V(lambda: nc.vector.reciprocal(n16, n16))
        ext = V(lambda: nc.vector.tensor_copy(ex[:, :].rearrange("p (n c) -> p n c", c=64),
                                              n16.unsqueeze(2).to_broadcast([128, 16, 64])), a)
        yield
        cs = slice(128 * p, 128 * p + 128)
        pair, a = both(wup[0:64, cs], lo[0:64, :], [wt, state["lo"]])
        e = evac(pair, a, sg, ACT.Sigmoid, 1.0, w0[:, p:p + 1], state["tmpf"], ctok)
        ctk = V(lambda: nc.vector.tensor_tensor_scan(cum[:, :], C.reset64, sg[:, :], 0.0, ALU.mult, ALU.add), e)
        yield
        pair, a = both(wup[64:128, cs], lo[64:128, :], [wt, state["lo"]])
        at = evac(pair, a, av, ACT.Sigmoid, 1.0, a0[:, p:p + 1], state["tmpf"], ctok)
        yield
        for h in range(2):
            s, f = RU.take()
            for j in range(4):
                a = P(lambda: nc.tensor.transpose(s.ap[:, 128 * j:128 * j + 128],
                                                  ex[:, 512 * h + 128 * j:512 * h + 128 * j + 128], C.ident), ext, f,
                      sig=(j == 3))
            e = V(lambda: nc.vector.tensor_tensor(kk[:, 512 * h:512 * h + 512], kk[:, 512 * h:512 * h + 512], s.ap,
                                                  ALU.mult), a)
            s.free = [e]
            yield
        ea = a
        V(lambda: nc.vector.tensor_scalar(D[:, :], av[:, :], kac[:, p:p + 1], omka[:, p:p + 1], ALU.mult, ALU.add),
          at)
        yield
        V(lambda: nc.vector.tensor_tensor(k[:, :], k[:, :], D[:, :], ALU.mult))
        yield "half"
        pf = state["pairfree"][b]
        td = V(lambda: nc.vector.scalar_tensor_tensor(D[:, :], r[:, :], rkc[:, p:p + 1], k[:, :], ALU.mult, ALU.mult))
        t = S(lambda: nc.scalar.activation(ex[:, :], cum[:, :], ACT.Exp, scale=-EC), ctk, ea)
        yield
        c16 = lambda x: x.rearrange("p (c t) -> p c t", t=64)
        V(lambda: nc.vector.tensor_tensor(AR[:, b, :, 1, :], c16(r[:, :]), c16(ex[:, :]), ALU.mult), t, pf)
        x = V(lambda: nc.vector.tensor_copy(pc[:, b, :], c16(ex[:, :])[:, :, 63]))
        t2 = S(lambda: nc.scalar.activation(ex[:, :], cum[:, :], ACT.Exp, scale=EC), x)
        yield
        pair, a = both(C.bd64, D, [td])
        for h in range(2):
            sl = slice(512 * h, 512 * h + 512)
            e = V(lambda: nc.vector.tensor_tensor(bon[:, p % 3, sl], pair[h].ap, vT[:, b, sl], ALU.mult), a)
            pair[h].free = [e]
        yield
        t = V(lambda: nc.vector.tensor_tensor(D[:, :], cum[:, :], sg[:, :], ALU.subtract), a)
        t = S(lambda: nc.scalar.activation(D[:, :], D[:, :], ACT.Exp, scale=-EC), t)
        V(lambda: nc.vector.tensor_tensor(Kc[:, b, :], k[:, :], ex[:, :], ALU.mult), t2)
        yield
        V(lambda: nc.vector.scalar_tensor_tensor(AR[:, b, :, 0, :], c16(kk[:, :]), -1.0, c16(D[:, :]), ALU.mult,
                                                 ALU.mult), t)
        yield
        V(lambda: nc.vector.tensor_tensor(kk[:, :], kk[:, :], av[:, :], ALU.mult))
        yield
        t = V(lambda: nc.vector.tensor_tensor(Bc[:, b, :], kk[:, :], ex[:, :], ALU.mult))
        state["tmpf"] = t
        state[("prep", p)] = t

    RR = [slice(0, 64), slice(64, 128)]

    def tiles(outs, lhs, rhs, start=True, stop=True, toks=None, sig=True):
        for h, rr in enumerate(RR):
            a = P(lambda: nc.tensor.matmul(outs[rr], lhs[rr], rhs[rr], start=start, stop=stop,
                                           skip_group_check=True), toks, sig=(sig and h == 1))
        return a

    def rows(s, f, src, toks):
        for c in range(4):
            a = P(lambda: nc.tensor.transpose(s.ap[0:64, 128 * c:128 * c + 128], src[:, c, :], C.ident),
                  toks, f, sig=(c == 3))
        return a

    def apart(s, dst, a, toks):
        v = s.ap[0:64, :].rearrange("p (c h x) -> p c h x", c=4, h=2)
        for h, rr in enumerate(RR):
            e = S(lambda: nc.scalar.activation(dst[rr], v[:, :, h, :], ACT.Copy), a, toks)
        s.free = [e]
        return e

    def stage(p, g, n):
        b, gb = p % 2, n % 4
        pt = state[("prep", p)]
        gf = state["gfree"][gb]
        s1 = state["s1"][n % 2]
        X, M1 = XM_[:, 0, n % 2], XM_[:, 1, n % 2]
        gs = slice(256 * g, 256 * g + 256)
        c4 = lambda x: x.rearrange("p (c t) -> p c t", t=64)
        B4, K4, V4 = c4(Bc[:, b, gs]), c4(Kc[:, b, gs]), c4(vT[:, b, gs])
        for src, dst in ((B4, MB_), (K4, MK_)):
            s, f = RG.take()
            for c in range(4):
                a = tiles(s.ap[:, 128 * c:128 * c + 128], src[:, c, :],
                          AR[:, b, 4 * g + c, :, :].rearrange("p x t -> p (x t)"), toks=[pt, f], sig=(c == 3))
            mm = C.mAR.unsqueeze(1).to_broadcast([128, 4, 128])
            e = V(lambda: nc.vector.tensor_tensor(dst[:, gb].rearrange("p c x t -> p c (x t)"),
                                                  s.ap.rearrange("p (c t) -> p c t", c=4), mm, ALU.mult), a, gf)
            s.free = [e]
            if dst is MB_:
                lt = e
                LT = MB_[:, gb, :, 0, :]
                xt3 = XT[:, gb]
                lm = lambda l: C.lm64[:, l, :].unsqueeze(1).to_broadcast([128, 4, 64])
                V(lambda: nc.vector.tensor_copy(xt3, C.stack.unsqueeze(1).to_broadcast([128, 4, 64])))
                xtt = V(lambda: nc.vector.copy_predicated(xt3, lm(0), LT))
            yield
        mt = e
        side = iter([(B4, Bn), (K4, Kn), (V4, Vn)])
        nt = None
        xpe = mpe = s1
        for l in range(1, 6):
            s, f = RG.take()
            a = rows(s, f, xt3, [xtt])
            e = apart(s, X, a, xpe)
            yield
            for src, dst in [next(side, (None, None))]:
                if src is not None:
                    s, f = RG.take()
                    a = rows(s, f, src, [pt])
                    nt = apart(s, dst[:, gb], a, gf)
            s, f = RG.take()
            for c in range(4):
                a = tiles(s.ap[:, 64 * c:64 * c + 64], LT[:, c, :], X[:, c, :], toks=[lt, e, f], sig=(c == 3))
            xpe = a
            e = V(lambda: nc.vector.tensor_copy(M1[:, :, :].rearrange("p c s -> p (c s)"), s.ap[:, 0:256]), a, mpe)
            s.free = [e]
            yield
            s, f = RG.take()
            for c in range(4):
                a = tiles(s.ap[:, 64 * c:64 * c + 64], M1[:, c, :], xt3[:, c, :], toks=[xtt, e, f], sig=(c == 3))
            mpe = a
            xtt = V(lambda: nc.vector.copy_predicated(xt3, lm(l),
                                                      s.ap[:, 0:256].rearrange("p (c s) -> p c s", c=4)), a)
            s.free = [xtt]
            yield
        state["s1"][n % 2] = a
        state[("st", n)] = [mt, nt, xtt]
        if g >= 2:
            state.setdefault(("pf1", p), []).append(a)

    def chain(p, g, n):
        gb, b = n % 4, p % 2
        tk = state[("st", n)]
        ys_, yf = RY.take()
        for c in range(4):
            i = state["gn"] % 2
            j = 1 - i
            cc = 4 * g + c
            if cc == 0:
                state["st"] = V(lambda: nc.vector.memset(ST[:, i, :], 0.0), state["y"])
            stt = state["st"]
            V(lambda: nc.vector.tensor_scalar(zu[:, 2, :], ST[:, i, :], pc[:, b, cc:cc + 1], None, ALU.mult))
            s, f = RC.take()
            z = s.ap[:, 0:64]
            tiles(z, MK_[:, gb, c, 0, :], Vn[:, gb, c, :], True, False, [tk, f], sig=False)
            a = tiles(z, AR[:, b, cc, 0, :], ST[:, i, :], False, True, [stt])
            e = V(lambda: nc.vector.tensor_copy(zu[:, 0, :], z), a)
            s.free = [e]
            yo = ys_.ap[:, 64 * c:64 * c + 64]
            tiles(yo, AR[:, b, cc, 1, :], ST[:, i, :], True, False, [yf], sig=False)
            tiles(yo, MK_[:, gb, c, 1, :], Vn[:, gb, c, :], False, False, sig=False)
            yield
            s, f = RC.take()
            u = s.ap[:, 0:64]
            a = tiles(u, XT[:, gb, c, :], zu[:, 0, :], toks=[e, f])
            e = V(lambda: nc.vector.tensor_copy(zu[:, 1, :], u), a)
            s.free = [e]
            yield
            s, f = RC.take()
            w = s.ap[:, 0:64]
            tiles(w, Kn[:, gb, c, :], Vn[:, gb, c, :], True, False, [f], sig=False)
            a = tiles(w, Bn[:, gb, c, :], zu[:, 1, :], False, True, [e])
            state["st"] = V(lambda: nc.vector.scalar_tensor_tensor(ST[:, j, :], w, pc[:, b, cc:cc + 1],
                                                                   zu[:, 2, :], ALU.mult, ALU.add), a, state["y"])
            s.free = [state["st"]]
            state["y"] = tiles(yo, MB_[:, gb, c, 1, :], zu[:, 1, :], False, True)
            state["gn"] += 1
            yield
        e = S(lambda: nc.scalar.activation(Y2[:, p % 2, 4 * g:4 * g + 4, :].rearrange("p c v -> p (c v)"),
                                           ys_.ap[:, 0:256], ACT.Copy), state["y"], state["yfree"][p % 2])
        ys_.free = [e]
        state["gfree"][gb] = [state["y"]]
        state["yev"] = e
        if g == 3:
            state["pairfree"][b] = state[("pf1", p)] + [state["y"]]

    def finish(p):
        b = p % 2
        gate, fin = gf_[:, 0, :], gf_[:, 1, :]
        Y = Y2[:, b]
        pf1 = state["fin"]
        s16, q16 = ys[:, 0:16], ys[:, 16:32]
        bc = lambda x: x.unsqueeze(2).to_broadcast([128, 16, 64])
        V(lambda: nc.vector.tensor_reduce(s16, Y[:, :, :], AX.X, ALU.add), state["yev"])
        V(lambda: nc.vector.tensor_scalar(s16, s16, 1.0 / 64, None, ALU.mult))
        t = V(lambda: nc.vector.tensor_tensor(Y[:, :, :], Y[:, :, :], bc(s16), ALU.subtract))
        y1 = Y[:, :, :].rearrange("p c v -> p (c v)")
        t = S(lambda: nc.scalar.activation(fin[:, :], y1, ACT.Square), t, pf1)
        V(lambda: nc.vector.tensor_reduce(q16, fin[:, :].rearrange("p (c v) -> p c v", v=64), AX.X, ALU.add), t)
        t = V(lambda: nc.vector.tensor_scalar(q16, q16, 1.0 / 64, 64e-5, ALU.mult, ALU.add))
        t = S(lambda: nc.scalar.activation(q16, q16, ACT.Sqrt), t)
        V(lambda: nc.vector.reciprocal(q16, q16), t)
        yt = V(lambda: nc.vector.tensor_tensor(Y[:, :, :], Y[:, :, :], bc(q16), ALU.mult))
        out = []
        yield from unit_steps(K, W, xT, xtok, RU, out)
        pair, a = out[0]
        gt = evac(pair, a, gate, ACT.Silu, 1.0, 0.0, pf1)
        yield
        for half in range(2):
            s, f = RU.take()
            for c in range(8):
                a = tiles(s.ap[:, 64 * c:64 * c + 64], Y[:, 8 * half + c, :], C.stack, toks=[yt, f], sig=(c == 7))
            state["yfree"][b] = a
            sl = slice(512 * half, 512 * half + 512)
            e = S(lambda: nc.scalar.activation(fin[:, sl], s.ap, ACT.Identity, scale=lnw[:, p:p + 1],
                                               bias=lnb[:, p:p + 1]), a, V.last())
            s.free = [e]
            yield
            V(lambda: nc.vector.tensor_tensor(fin[:, sl], fin[:, sl], bon[:, p % 3, sl], ALU.add), e)
            e = V(lambda: nc.vector.tensor_tensor(fin[:, sl], fin[:, sl], gate[:, sl], ALU.mult), gt)
        d = K.dma(A["mix"][p], fin[:, :], e, sem=fsem[b])
        K.stored(d)
        state["fin"] = [e, d]

    fsem = [[*K.sem("fin"), 0] for _ in range(2)]
    run(prep_lo())
    run(prep(0))
    NP = 8

    def both_chains(n):
        yield from chain(n // 4, n % 4, n)
        yield from chain((n + 1) // 4, (n + 1) % 4, n + 1)

    def until_half(gen):
        for x in gen:
            if x == "half":
                return
            yield

    def then(*gens):
        for g in gens:
            yield from g

    nxt = None
    for n in range(0, 4 * NP + 2, 2):
        p, g = divmod(n, 4)
        gens = []
        if n > 0:
            gens.append(both_chains(n - 2))
        if n < 4 * NP:
            gens += [stage(p, g, n), stage(p, g + 1, n + 1)]
            if g == 0 and p + 1 < NP:
                nxt = prep(p + 1)
                gens.append(until_half(nxt))
            elif g == 2:
                parts = ([nxt] if p + 1 < NP else []) + ([finish(p - 1)] if p > 0 else [])
                gens.append(then(*parts))
        weave(*gens)
    run(finish(NP - 1))


def attention(K, C, W, xs, spare, xtok, A, banks, st):
    nc, P, V, S, G = K.nc, K.P, K.V, K.S, K.G
    RU, RS, RT, RO = Ring(banks[0:2]), Ring(banks[2:4]), Ring(banks[4:6]), Ring(banks[6:8])
    sb = lambda n, s, d=F32: K.sb(st, n, s, d)
    qkvg = spare.rearrange("p (b i) n -> p b i n", b=2)
    Vc = sb("Vc", [128, 24, 128])
    Pm = sb("Pm", [128, 4, 512])
    PT = sb("PT", [128, 4, 512])
    O2 = sb("O", [128, 2, 3, 1024])
    MB = sb("MB", [128, 3, 1024])
    den_, tmp_ = sb("den", [128, 1024]), sb("tmp", [128, 512])
    QV = sb("QV", [128, 2, 1024])
    XM = sb("XM", [128, 2, 4, 2, 64])
    ml2 = sb("ml", [128, 2, 2, 3, 2, 8])
    state = {"pm": [None] * 4, "pt": [None] * 4, "ml": [None, None], "vc": None,
             "xm": [None, None], "O": [None, None]}
    fsem = [*K.sem("fa"), 0]

    def prep(p):
        b = p % 2
        for i in range(4):
            pair, fr = take2(RU)
            (wh, wl), tok = W.get()
            for k in range(8):
                for h in range(2):
                    sl = slice(512 * h, 512 * h + 512)
                    a = products(K, pair[h].ap, (wh[:, k, :], wl[:, k, :]), (xs[:, 0, k, sl], xs[:, 1, k, sl]),
                                 k == 0, k == 7, tok, xtok, fr, sig=(k == 7))
                if k < 6:
                    yield
            W.done(a)
            for h in range(2):
                e = S(lambda: nc.scalar.activation(qkvg[:, b, i, 512 * h:512 * h + 512], pair[h].ap,
                                                   ACT.Silu if i == 3 else ACT.Copy,
                                                   scale=0.125 if i == 0 else 1.0), a,
                      state[("g", p - 2) if i == 3 else ("t", p - 2)] if p > 1 else None)
                pair[h].free = [e]
            yield
        state[("p", p)] = e

    def view(x, pi):
        if pi == 0:
            return x.rearrange("p (c i) -> p c i", i=128)
        if pi == 1:
            return x.rearrange("p (j r) -> p r j", r=4)
        return x.rearrange("p (j r) -> p r j", r=16)

    def cell(x, pi, c, two=False):
        if pi == 0:
            return x[:, 128 * (c - 1) if two else 128 * c:128 * c + 128]
        if pi == 1:
            v = x.rearrange("p (j r) -> p r j", r=4)
            return v[:, c // 2, 0:256] if two else v[:, c // 2, 128 * (c % 2):128 * (c % 2) + 128]
        v = x.rearrange("p (j r) -> p r j", r=16)
        return v[:, 2 * c:2 * c + 2, :]

    def scell(x, x3, pi, c):
        return x3[:, 128 * c:128 * c + 128] if pi == 2 else cell(x, pi, c)

    def group(x, pi, g):
        if pi == 0:
            return x[:, 512 * g:512 * g + 512], None
        r = 4 if pi == 1 else 16
        n = 2 if pi == 1 else 8
        return x.rearrange("p (j r) -> p r j", r=r)[:, n * g:n * g + n, :], n

    def scat(dst, src, pi, g, eng, *toks):
        d, n = group(dst, pi, g)
        s = src if n is None else src.rearrange("p (r j) -> p r j", r=n)
        if eng is S:
            return S(lambda: nc.scalar.activation(d, s, ACT.Copy), *toks)
        return V(lambda: nc.vector.tensor_copy(d, s), *toks)

    def main(p):
        b = p % 2
        O, ml = O2[:, b], ml2[:, b]
        pt = state[("p", p)]
        q, k, v, g = [qkvg[:, b, i, :] for i in range(4)]
        q3, v3 = QV[:, 0, :], QV[:, 1, :]
        G(lambda: nc.gpsimd.tensor_copy(v3.rearrange("p (r j) -> p r j", r=16),
                                        v.rearrange("p (j r) -> p r j", r=16)), pt, state["vc"])
        g3 = G(lambda: nc.gpsimd.tensor_copy(q3.rearrange("p (r j) -> p r j", r=16),
                                             q.rearrange("p (j r) -> p r j", r=16)))

        def turn_values(pi):
            for gg in range(2):
                s, f = RT.take()
                for j in range(4):
                    a = P(lambda: nc.tensor.transpose(s.ap[:, 128 * j:128 * j + 128], scell(v, v3, pi, 4 * gg + j),
                                                      C.ident), pt, g3 if pi == 2 else None, f, sig=(j == 3))
                i0 = 8 * pi + 4 * gg
                vc = S(lambda: nc.scalar.activation(Vc[:, i0:i0 + 4, :].rearrange("p c d -> p (c d)"), s.ap,
                                                    ACT.Copy), a, state["vc"])
                s.free = [vc]
                at["vc"] = vc

        at = {}
        turn_values(0)
        yield
        turn_values(1)
        yield
        work = []
        for pi in range(3):
            per = 2 if pi < 2 else 4
            for gg in range(2):
                for h in range(2):
                    for c0 in range(4 * gg, 4 * gg + 4, per):
                        work.append((pi, gg, h, c0, per, h == 0 and c0 == 4 * gg, h == 1 and c0 + per == 4 * gg + 4))

        def scores(i):
            pi, gg, h, c0, per, first, last = work[i]
            rr = slice(64 * h, 64 * h + 64)
            bb = i % 4
            s, f = RS.take()
            w = 512 // per
            parts = []
            for j in range(per):
                c = c0 + j
                prev = (pi == 0 and c > 0) or (pi == 1 and c % 2 == 1)
                parts.append((c, prev))
                m = C.m3 if pi == 2 else (C.m2 if prev else C.m1)
                P(lambda: nc.tensor.matmul(s.ap[:, w * j:w * j + w], C.identb, m, start=True, stop=False,
                                           skip_group_check=True), f, pt, g3 if pi == 2 else None, sig=False)
                o = s.ap[:, w * j:w * j + w] if (prev or pi == 2) else s.ap[:, w * j + 128:w * j + 256]
                a = P(lambda: nc.tensor.matmul(o, scell(q[rr], q3[rr], pi, c), cell(k[rr], pi, c, prev),
                                               start=False, stop=True, skip_group_check=True),
                      sig=(j == per - 1))
            nm = ml[:, 0, pi, h, c0:c0 + per]
            t = V(lambda: nc.vector.tensor_reduce(nm, s.ap.rearrange("p (j w) -> p j w", j=per), AX.X,
                                                  ALU.max, negate=True), a, state["ml"][b])
            for j, (c, prev) in enumerate(parts):
                lo = w * j if (prev or pi == 2) else w * j + 128
                e = S(lambda: nc.scalar.activation(Pm[:, bb, lo:w * j + w], s.ap[:, lo:w * j + w],
                                                   ACT.Exp, bias=ml[:, 0, pi, h, c:c + 1],
                                                   accum_out=ml[:, 1, pi, h, c:c + 1]), t, state["pm"][bb],
                      state["ml"][b])
            s.free = [e]
            at[i] = [parts, e]

        def turn(i):
            pi, gg, h, c0, per, first, last = work[i]
            parts, e = at[i]
            w = 512 // per
            bb = i % 4
            s, f = RT.take()
            blocks = []
            for j, (c, prev) in enumerate(parts):
                for lo in ((w * j, w * j + 128) if prev else (w * j + w - 128,)):
                    blocks.append((lo, c, prev and lo == w * j))
            for x, (lo, c, isp) in enumerate(blocks):
                a = P(lambda: nc.tensor.transpose(s.ap[:, 128 * x:128 * x + 128], Pm[:, bb, lo:lo + 128],
                                                  C.ident), e, f, sig=(x == len(blocks) - 1))
            state["pm"][bb] = a
            nb = len(blocks)
            e = V(lambda: nc.vector.tensor_copy(PT[:, bb, 0:128 * nb], s.ap[:, 0:128 * nb]), a, state["pt"][bb])
            s.free = [e]
            at[i] = [blocks, e]

        def values(i):
            pi, gg, h, c0, per, first, last = work[i]
            rr = slice(64 * h, 64 * h + 64)
            blocks, e = at[i]
            bb = i % 4
            nb = len(blocks)
            if first:
                at["ob"] = RO.take()
            ob, of = at["ob"]
            for x, (lo, c, isp) in enumerate(blocks):
                ci = 8 * pi + (c - 1 if isp else c)
                new = x == 0 or blocks[x - 1][1] != c
                end = x == nb - 1 or blocks[x + 1][1] != c
                a = P(lambda: nc.tensor.matmul(ob.ap[rr, 128 * (c % 4):128 * (c % 4) + 128],
                                               Vc[:, ci, rr], PT[:, bb, 128 * x:128 * x + 128],
                                               start=new, stop=end), e, at["vc"], of, sig=(x == nb - 1))
            state["pt"][bb] = a
            at["pv"] = a
            if last:
                at["o"] = scat(O[:, pi, :], ob.ap, pi, gg, S, a, state["O"][b])
                ob.free = [at["o"]]

        n = len(work)
        for i in range(n + 5):
            if i < n:
                scores(i)
            if i == 14:
                turn_values(2)
            if 0 <= i - 3 < n:
                turn(i - 3)
            if 0 <= i - 5 < n:
                values(i - 5)
            yield
        state["vc"] = at["pv"]
        state[("t", p)] = [at["o"], S.last(), V.last(), at["pv"]]

    def tail(p):
        b = p % 2
        O, ml = O2[:, b], ml2[:, b]
        g = qkvg[:, b, 3, :]
        done = state[("t", p)]
        tt = lambda o, x, y, op, *tk: V(lambda: nc.vector.tensor_tensor(o, x, y, op), *tk)
        mn = den = den_[:, :]

        def spread(x, take):
            et = [None, None]
            for n in range(7):
                if n < 6:
                    pi, gg = divmod(n, 2)
                    for h in range(2):
                        et[gg] = V(lambda: nc.vector.tensor_copy(
                            XM[:, gg, :, h, :],
                            ml[:, x, pi, h, 4 * gg:4 * gg + 4].unsqueeze(2).to_broadcast([128, 4, 64])),
                            done, state["xm"][gg])
                if n:
                    pi, gg = divmod(n - 1, 2)
                    s, f = RT.take()
                    for j in range(4):
                        a = P(lambda: nc.tensor.transpose(s.ap[:, 128 * j:128 * j + 128],
                                                          XM[:, gg, j].rearrange("p h v -> p (h v)"), C.ident),
                              et[gg], f, sig=(j == 3))
                    state["xm"][gg] = a
                    s.free = [take(pi, gg, s.ap, a)]
                yield
            state["ml"][b] = et[1]

        yield from spread(0, lambda pi, gg, ap, a: scat(MB[:, pi, :], ap, pi, gg, S, a, V.last()))
        tt(mn, MB[:, 0, :], MB[:, 1, :], ALU.min, S.last())
        tt(mn, mn, MB[:, 2, :], ALU.min)
        for pi in range(3):
            t = tt(MB[:, pi, :], mn, MB[:, pi, :], ALU.subtract)
            et = S(lambda: nc.scalar.activation(MB[:, pi, :], MB[:, pi, :], ACT.Exp), t)
            yield

        def weigh(pi, gg, ap, a):
            d, n = group(den, pi, gg)
            m, n = group(MB[:, pi, :], pi, gg)
            rj = lambda x: x if n is None else x.rearrange("p (r j) -> p r j", r=n)
            if pi == 0:
                return tt(d, ap, m, ALU.mult, a, et)
            t = tt(rj(tmp_[:, :]), rj(ap), m, ALU.mult, a)
            tt(d, d, rj(tmp_[:, :]), ALU.add)
            return t

        for pi in range(3):
            tt(O[:, pi, :], O[:, pi, :], MB[:, pi, :], ALU.mult, et)
            if pi:
                tt(O[:, 0, :], O[:, 0, :], O[:, pi, :], ALU.add)
            yield
        state[("g", p)] = tt(O[:, 0, :], O[:, 0, :], g, ALU.mult)
        yield from spread(1, weigh)
        for x in range(4):
            sl = slice(256 * x, 256 * x + 256)
            V(lambda: nc.vector.reciprocal(den[:, sl], den[:, sl]))
            yield
        e = tt(O[:, 0, :], O[:, 0, :], den, ALU.mult)
        state["O"][b] = K.dma(A["mix"][8 + p], O[:, 0, :], e, sem=fsem)
        K.stored(state["O"][b])
        yield

    run(prep(0))
    for p in range(8):
        side = [tail(p - 1)] if p > 0 else []
        if p < 7:
            side.append(prep(p + 1))
        weave(main(p), *side)
    run(tail(7))


def block2(K, C, h, htok, xT, A, banks):
    nc = K.nc
    with ExitStack() as st:
        ring = Ring(banks)
        with ExitStack() as s2:
            nw = K.sb(s2, "nw", [128, 8])
            nt = K.dma(nw[:, :], A["nw2"])
            xtok = rms_T(K, s2, h, [htok, nt], xT, nw, 1e-5, C.ident, ring)
            hs = K.dma(A["hs"], h[:, :, :], htok)
            K.stored(hs)
            K.fence()
        K.D.wait(hs)
        for q in (K.P, K.V, K.S, K.G):
            q.wait(hs)
        return xtok


def block2_rest(K, C, hbuf, xT, A, banks):
    nc = K.nc
    with ExitStack() as st:
        with ExitStack() as s2:
            cols = K.sb(s2, "cols2", [128, 112])
            ct = K.dma(cols[:, 0:96], A["c2"])
            load_masks(K, s2, A, C)
            c2 = K.sb(s2, "c2c", [128, 1344])
            t = K.dma(c2[:, :], A["c2c"])
            for q in (K.P, K.V):
                q.wait(t)
            C.mAR, C.stack, C.reset64 = c2[:, 0:128], c2[:, 256:320], c2[:, 320:1344]
            W = Weights(K, s2, [A["w2u"][i] for i in range(33)])
            rwkv(K, C, W, xT, None, A, banks, s2, cols, ct)
            K.fence()
        K.V.wait(*K.stores.values())
        K.D.wait(*K.stores.values())
        with ExitStack() as s2:
            mb = K.sb(s2, "mb", [128, 768], BF16)
            K.P.wait(K.dma(mb[:, :], A["mb"]))
            C.identb, C.m2, C.m1, C.m3 = mb[:, 0:128], mb[:, 128:384], mb[:, 384:640], mb[:, 640:768]
            xs = K.sb(s2, "xs", [128, 2, 8, 1024], F32R)
            for k in range(8):
                xtok = split(K, xT[:, k, :], xs[:, 0, k, :], xs[:, 1, k, :])
            W = SplitWeights(K, s2, [A["w2u"][33 + i] for i in range(32)])
            attention(K, C, W, xs, xT, xtok, A, banks, s2)
            K.fence()
        for q in (K.P, K.V, K.S, K.D):
            q.wait(*K.stores.values())


def block2_out(K, C, h, xT, A, banks):
    nc, P, V, S = K.nc, K.P, K.V, K.S
    with ExitStack() as st:
        mix = K.sb(st, "mixs", [128, 2, 16, 1024], F32R)
        M = Weights(K, st, [A["mix"][i] for i in range(16)])
        W = SplitWeights(K, st, [A["wo2"][hh][:, k, :] for hh in range(2) for k in range(16)], 3, 512)
        t1 = K.dma(h[:, :, :], A["hs"])
        slots = Ring(banks).slots
        toks = {}
        for hh in range(2):
            for k in range(16):
                for i in (k, k + 1):
                    if i < 16 and i not in toks:
                        tok = M.get()[1]
                        toks[i] = split(K, M.buf[:, i % 3, :], mix[:, 0, i, :], mix[:, 1, i, :], tok)
                        M.done(toks[i])
                (wh, wl), tok = W.get()
                for t in range(8):
                    sl = slice(128 * t, 128 * t + 128)
                    a = products(K, slots[t].ap, (mix[:, 0, k, sl], mix[:, 1, k, sl]),
                                 (wh.rearrange("p k c -> p (k c)"), wl.rearrange("p k c -> p (k c)")),
                                 k == 0, k == 15, toks[k], tok, slots[t].free, sig=(t == 7 or k == 15))
                    if k == 15:
                        hs = h[:, t, 512 * hh:512 * hh + 512]
                        e = V(lambda: nc.vector.tensor_tensor(hs, hs, slots[t].ap, ALU.add), a, t1)
                        slots[t].free = [e]
                W.done(a)
        K.fence()
    P, V, S = K.P, K.V, K.S
    with ExitStack() as st:
        fw = K.sb(st, "fw", [128, 1024])
        ft = K.dma(fw[:, :], A["fw2"])
        ss = K.sb(st, "ssf", [128, 8])
        sq = K.sb(st, "sqf", [128, 1024])
        for t in range(8):
            a = S(lambda: nc.scalar.activation(sq[:, :], h[:, t, :], ACT.Square, accum_out=ss[:, t:t + 1]), e)
        b = V(lambda: nc.vector.tensor_scalar(ss[:, :], ss[:, :], 1.0 / 1024, 1e-5, ALU.mult, ALU.add), a)
        b = S(lambda: nc.scalar.activation(ss[:, :], ss[:, :], ACT.Sqrt), b)
        V(lambda: nc.vector.reciprocal(ss[:, :], ss[:, :]), b)
        for t in range(8):
            e = V(lambda: nc.vector.scalar_tensor_tensor(h[:, t, :], h[:, t, :], ss[:, t:t + 1], fw[:, :], ALU.mult,
                                                         ALU.mult), ft)
        K.fence()
    return e


class Consts:
    pass


def load_consts(K, ctx, A):
    C = Consts()
    cc = K.sb(ctx, "cc", [128, 256])
    toks = [K.dma(cc[:, 0:128], A["cc"][:, 0:128]), K.dma(cc[:, 128:256], A["cc"][:, 384:512])]
    C.tok = toks
    C.ident, C.bd64 = cc[:, 0:128], cc[:, 128:256]
    K.fence_sb = cc
    for q in (K.P, K.V, K.S, K.G):
        q.wait(*toks)
    return C


def build_program(nc, A):
    with ExitStack() as ctx:
        K = Kern(nc, ctx)
        ps = ctx.enter_context(nc.psum_tensor("ps", [128, 8, 512], F32))
        K.fence_ps = ps[:, 7, :]
        banks = [ps[:, i, :] for i in range(8)]
        C = load_consts(K, ctx, A)
        with ExitStack() as s0:
            xT = K.sb(s0, "xT", [128, 8, 1024])
            t = [K.dma(xT[:, i, :], A["xT"][:, i, :]) for i in range(8)]
            with ExitStack() as s1:
                h = K.sb(s1, "h", [128, 8, 1024])
                e = block1(K, C, h, xT, t, A, banks)
                block2(K, C, h, None, xT, A, banks)
            block2_rest(K, C, None, xT, A, banks)
        h = K.sb(ctx, "h", [128, 8, 1024])
        block2_out(K, C, h, None, A, banks)
        block3(K, C, h, A, banks)
        K.D.wait(*K.stores.values())



def bc(v):
    return np.ascontiguousarray(np.broadcast_to(v.reshape(1, -1), (128, v.size)))


def units(blocks):
    w = np.concatenate(blocks, axis=1)
    n = w.shape[1] // 128
    return np.ascontiguousarray(w.reshape(8, 128, n, 128).transpose(2, 1, 0, 3).reshape(n, 128, 1024))


def col(v):
    return np.ascontiguousarray(v.reshape(-1, 128).T)


def zeros(*shape):
    return np.zeros(shape, np.float32)


def consts():
    i=np.arange(128)
    A={}
    cc=np.zeros((128,768),np.float32)
    s=i[:,None]; t=i[None]
    cc[:,0:128]=np.eye(128)
    cc[:,128:256]=(t>=s)
    cc[:,256:384]=(t<s)
    cc[:,384:512]=(s//64==t//64)
    cc[:,512:768]=(s//32==np.arange(256)[None]//64)
    A["cc"]=cc
    c2=np.zeros((128,128+128+64+1024),np.float32)
    bdm=(s//64==t//64)
    t6=np.arange(64)[None]
    c2[:,0:64]=s%64<t6; c2[:,64:128]=s%64<=t6
    c2[:,256:320]=(s%64==np.arange(64)[None])
    c2[:,320:]=(np.arange(1024)%64!=0)[None]
    A["c2c"]=c2
    
    NEG=-1e30
    mb=np.zeros((128,128+256*2+128),np.float32)
    mb[:,0:128]=np.eye(128)
    q=i[:,None]; k=i[None]
    prev=np.where(k>=q,0,NEG); cur=np.where(k<=q,0,NEG)
    mb[:,128:256]=prev; mb[:,256:384]=cur
    mb[:,384:512]=NEG; mb[:,512:640]=cur
    mb[:,640:768]=np.where((q//64==k//64)&(k<=q),0,NEG)
    A["mb"]=mb.astype(mybir.dt.np(BF16))
    lm=np.zeros((128,7,128),np.float32)
    for l in range(7):
        B=1<<l
        lm[:,l]=((s//(2*B)==t//(2*B))&(s//B%2==0)&(t//B%2==1))
    A["lm"]=np.concatenate([lm.reshape(128,-1)]+[lm[i%64,l,:64] for l in range(6)],1)
    return A


def host1(I):
    w=I["w_in"][0]; A={}
    c=lambda o,i=0,n=128:w[:,o+128*i:o+128*i+n]
    L=[]
    for p in range(2): L+=[c(0,p),c(256,p),c(512,p),c(768,p)]
    for p in range(2): L+=[c(1024,p),c(1536,p),c(1280,p),c(1792,p)]
    L+=[c(2048),c(2176),c(2304),c(2304,1),c(2560),c(2560,1),np.concatenate([c(2816,0,16),np.zeros((1024,112),np.float32)],1)]
    A["w1"]=units(L)
    G=units([w[:,2832+1024*b+128*d:2832+1024*b+128*d+128] for b in range(3) for d in range(8)])
    up=I["w_up"][0]
    U=np.stack([up[b].reshape(2,128,8,128)[:,:,d,:].transpose(1,0,2).reshape(128,256) for b in range(3) for d in range(8)])
    A["wg"]=np.ascontiguousarray(np.concatenate([G,U],2))
    A["c1"]=np.ascontiguousarray(np.concatenate([col(I["hgrn_norm_g"][0]),col(I["gla_norm_g"][0]),col(I["gla_gate_b"][0]),col(I["hgrn_lb_logits"][0]),np.zeros((128,9),np.float32)],1))
    A["w2"]=I["gla_gate_w2"][0]
    A["wo1"]=np.ascontiguousarray(I["w_out"][0].reshape(4,2,128,2,512).transpose(3,0,2,1,4).reshape(8,128,1024))
    A["rows1"]=np.ascontiguousarray(np.stack([bc(I["ln_g"][0][None]),bc(I["ln_b"][0][None])],1))
    return A


def host2(I):
    g=lambda n:I[n+"_2"]
    w=g("w_in"); c=lambda o,i=0:w[:,o+128*i:o+128*i+128]
    L=[c(3072)]
    rk=lambda p:[c(0,p),c(1024,p),c(2048,p)]
    G0=3200; A0=4224; AG=7296
    L+=rk(0)+rk(1)[:2]+rk(1)[2:]
    for p in range(1,7): L+=rk(p+1)+[c(G0,p-1)]
    L+=[c(G0,6),c(G0,7)]
    for p in range(8): L+=[c(A0,p),c(A0+1024,p),c(A0+2048,p),c(AG,p)]
    A={}
    A["w2u"]=units(L)
    mu=g("mu_shift")
    A["c2"]=np.ascontiguousarray(np.concatenate([np.zeros((128,8),np.float32)]+[col(g(n)) for n in ("w0","a0","k_k","k_a")]+[col(g("r_k").reshape(-1)),col(g("ln_x_w")),col(g("ln_x_b")),col(mu[:3072]),col(mu[3072:]),np.zeros((128,7),np.float32)],1))
    A["wup2"]=np.ascontiguousarray(np.concatenate([g("w_up"),g("a_up")],0))
    A["nw2"]=col(g("norm_w"))
    A["wo2"]=np.ascontiguousarray(g("w_out").reshape(16,128,2,512).transpose(2,1,0,3))
    A["fw2"]=bc(g("final_norm_w")[None])
    return A


def host3(I):
    w=I["w_in_3"][0]; o=[]
    v=w[:,512:1024]; u=w[:,:512]; g=w[:,1024:1536]; z=w[:,1536:2048]; gb=w[:,2048:]
    c=lambda a,i:a[:,128*i:128*i+128]
    cols=[]
    for i in range(4): cols+=[c(u,i),c(g,i)]
    for i in range(4): cols+=[c(z,i),c(gb,i)]
    A={}
    A["w3"]=units(cols)
    A["c3"]=np.ascontiguousarray(np.concatenate([I["pre_g_3"][0].reshape(8,128).T, I["b_f_3"][0].T, np.zeros((128,4),np.float32)],1))
    p=np.arange(128)[:,None]; uu=np.arange(128)[None]
    d=np.zeros((128,8,2,128))
    for vv in range(8):
        th=2*np.pi*(((8*uu+vv)*p)%1024)/1024
        d[:,vv,0]=np.cos(th);d[:,vv,1]=np.sin(th)
    A["d3"]=d.reshape(128,2048).astype(np.float32)
    A["rows3"]=np.stack([bc(I["ln_g_3"][0][None]),bc(I["ln_b_3"][0][None]),bc(I["b_s_3"][0].reshape(1,512))])
    A["ws3"]=np.ascontiguousarray(I["w_s_3"][0].transpose(2,0,1).reshape(128,512))
    th=2*np.pi*((p*uu)%128)/128
    s=1/np.sqrt(1024*128)
    A["cd"]=np.concatenate([np.cos(th)*s,-np.sin(th)*s],1).astype(np.float32)
    A["wf3"]=np.ascontiguousarray(I["w_f_3"][0].transpose(1,0,2).reshape(128,512))
    A["wo3"]=np.ascontiguousarray(I["w_out_3"][0].reshape(8,128,2,512).transpose(2,0,1,3))
    A["w3v"]=np.ascontiguousarray(v.reshape(8,128,512))
    A["post3"]=bc(I["post_g_3"][0][None])
    return A



def kernel(**inputs):
    import concourse.bacc as bacc
    from concourse.bass_utils import run_bass_kernel_spmd

    I = {k: np.asarray(v) for k, v in inputs.items()}
    A = consts()
    A.update(host1(I))
    A.update(host2(I))
    A.update(host3(I))
    x = I["x"][0]
    A["x"] = np.ascontiguousarray(x.reshape(8, 128, 1024).transpose(1, 0, 2))
    A["xT"] = np.ascontiguousarray(x.T.reshape(8, 128, 1024).transpose(1, 0, 2))
    nc = bacc.Bacc("TRN2", target_bir_lowering=False, num_devices=1)
    aps, arrays = {}, {}
    for n, a in A.items():
        arrays["in_" + n] = a
        aps[n] = nc.dram_tensor("in_" + n, a.shape, mybir.dt.from_np(a.dtype), kind="ExternalInput").ap()
    aps["out"] = nc.dram_tensor("out_0", (8, 128, 1024), F32, kind="ExternalOutput").ap()
    aps["hs"] = nc.dram_tensor("hs", (128, 8, 1024), F32, kind="Internal").ap()
    aps["mix"] = nc.dram_tensor("mix", (16, 128, 1024), F32, kind="Internal").ap()
    build_program(nc, aps)
    r = run_bass_kernel_spmd(nc, [arrays], core_ids=[0])
    return r.results[0]["out_0"].reshape(1, 1024, 1024)
```
